# Optimizing a Trainium2 kernel written in Bass

```python
import jax, jax.numpy as jnp
from jax import lax
import numpy as np

D_MODEL = 1024
BATCH = 1
SEQ = 256
DEPTH = 2

GLA_HEADS = 4
GLA_DK = 128
GLA_DV = 128
GLA_LOWRANK = 16
GLA_GATE_NORM = 16.0
GLA_CHUNK = 64
MOBA_HEADS = 8
MOBA_HD = 64
MOBA_BLOCK = 256
MOBA_TOPK = 3
MOBA_QCHUNK = 64
ROPE_THETA = 10000.0
MLSTM_HEADS = 4
MLSTM_DQK = 64
MLSTM_DV = 128
MLSTM_CHUNK = 64
MLSTM_CONV = 4
D_FF = 4 * D_MODEL
N_BRANCH = 3
EPS = 1e-6

GLA_K = GLA_HEADS * GLA_DK
GLA_V = GLA_HEADS * GLA_DV
MOBA_W = MOBA_HEADS * MOBA_HD
MLSTM_QK = MLSTM_HEADS * MLSTM_DQK
MLSTM_V = MLSTM_HEADS * MLSTM_DV
IN_SPLITS = (GLA_K, GLA_K, GLA_V, GLA_V, GLA_LOWRANK,
             MOBA_W, MOBA_W, MOBA_W,
             MLSTM_QK, MLSTM_QK, MLSTM_V, MLSTM_V, MLSTM_HEADS, MLSTM_HEADS,
             N_BRANCH * D_MODEL)
D_IN = sum(IN_SPLITS)


def rms_norm(x, g):
    xf = x.astype(jnp.float32)
    y = xf * lax.rsqrt(jnp.mean(xf * xf, axis=-1, keepdims=True) + EPS)
    return (y * g.astype(jnp.float32)).astype(x.dtype)

def split_heads(x, h):
    b, t, _ = x.shape
    return x.reshape(b, t, h, -1).transpose(0, 2, 1, 3)

def merge_heads(x):
    b, h, t, d = x.shape
    return x.transpose(0, 2, 1, 3).reshape(b, t, h * d)

def rope_tables(seq, dim):
    inv = 1.0 / (ROPE_THETA ** (jnp.arange(0, dim, 2, dtype=jnp.float32) / dim))
    ang = jnp.arange(seq, dtype=jnp.float32)[:, None] * inv[None, :]
    return jnp.cos(ang), jnp.sin(ang)

def apply_rope(x, cos, sin):
    x1, x2 = jnp.split(x, 2, axis=-1)
    return jnp.concatenate([x1 * cos - x2 * sin, x2 * cos + x1 * sin], axis=-1)

def causal_dwconv(x, w):
    wd, c = w.shape
    return lax.conv_general_dilated(x, w[:, None, :], window_strides=(1,), padding=((wd - 1, 0),),
                                    dimension_numbers=('NWC', 'WIO', 'NWC'), feature_group_count=c)

def gla_mixer(q, k, v, log_a):
    b, h, t, dk = q.shape
    dv = v.shape[-1]
    L = GLA_CHUNK
    n = t // L
    qc = (q * dk ** -0.5).reshape(b, h, n, L, dk)
    kc = k.reshape(b, h, n, L, dk)
    vc = v.reshape(b, h, n, L, dv)
    bcum = jnp.cumsum(log_a.reshape(b, h, n, L, dk), axis=3)
    b_last = bcum[:, :, :, -1:, :]
    q_dec = qc * jnp.exp(bcum)
    k_inv = kc * jnp.exp(-bcum)
    k_end = kc * jnp.exp(b_last - bcum)
    causal = jnp.tril(jnp.ones((L, L), dtype=bool))
    attn = jnp.where(causal, jnp.einsum('bhnid,bhnjd->bhnij', q_dec, k_inv), 0.0)
    o_intra = jnp.einsum('bhnij,bhnjv->bhniv', attn, vc)
    chunk_kv = jnp.einsum('bhnld,bhnlv->bhndv', k_end, vc)
    decay = jnp.exp(b_last[:, :, :, 0, :])

    def step(S, inp):
        dec, kv = inp
        return dec[..., None] * S + kv, S

    S0 = jnp.zeros((b, h, dk, dv), q.dtype)
    _, S_prev = lax.scan(step, S0, (jnp.moveaxis(decay, 2, 0), jnp.moveaxis(chunk_kv, 2, 0)))
    S_prev = jnp.moveaxis(S_prev, 0, 2)
    o_inter = jnp.einsum('bhnld,bhndv->bhnlv', q_dec, S_prev)
    return (o_intra + o_inter).reshape(b, h, t, dv)

def moba_mixer(q, k, v):
    b, h, t, d = q.shape
    t_pad = -(-t // MOBA_BLOCK) * MOBA_BLOCK
    pad = ((0, 0), (0, 0), (0, t_pad - t), (0, 0))
    q, k, v = jnp.pad(q, pad), jnp.pad(k, pad), jnp.pad(v, pad)
    nb = t_pad // MOBA_BLOCK
    k_sel = min(MOBA_TOPK, nb)
    scale = d ** -0.5
    k_blocks = k.reshape(b, h, nb, MOBA_BLOCK, d)
    v_blocks = v.reshape(b, h, nb, MOBA_BLOCK, d)
    k_mean = jnp.mean(k_blocks, axis=3)
    pos = jnp.arange(t_pad)
    past = jnp.arange(nb)[None, :] < (pos // MOBA_BLOCK)[:, None]
    gate = jnp.einsum('bhtd,bhnd->bhtn', q, k_mean)
    gate = jnp.where(past, gate, -jnp.inf)
    top_val, top_idx = lax.top_k(gate, k_sel)
    valid = jnp.isfinite(top_val)
    bi = jnp.arange(b)[:, None, None, None]
    hi = jnp.arange(h)[None, :, None, None]
    qn = MOBA_QCHUNK

    def chunk_fn(c):
        start = c * qn
        qc = lax.dynamic_slice_in_dim(q, start, qn, axis=2)
        idx = lax.dynamic_slice_in_dim(top_idx, start, qn, axis=2)
        ok = lax.dynamic_slice_in_dim(valid, start, qn, axis=2)
        kg = k_blocks[bi, hi, idx]
        vg = v_blocks[bi, hi, idx]
        s_sel = jnp.einsum('bhqd,bhqskd->bhqsk', qc, kg) * scale
        s_sel = jnp.where(ok[..., None], s_sel, -jnp.inf).reshape(b, h, qn, k_sel * MOBA_BLOCK)
        own_start = (start // MOBA_BLOCK) * MOBA_BLOCK
        ko = lax.dynamic_slice_in_dim(k, own_start, MOBA_BLOCK, axis=2)
        vo = lax.dynamic_slice_in_dim(v, own_start, MOBA_BLOCK, axis=2)
        s_own = jnp.einsum('bhqd,bhkd->bhqk', qc, ko) * scale
        qpos = start + jnp.arange(qn)
        kpos = own_start + jnp.arange(MOBA_BLOCK)
        s_own = jnp.where(kpos[None, :] <= qpos[:, None], s_own, -jnp.inf)
        p = jax.nn.softmax(jnp.concatenate([s_sel, s_own], axis=-1).astype(jnp.float32), axis=-1)
        p_sel = p[..., :k_sel * MOBA_BLOCK].reshape(b, h, qn, k_sel, MOBA_BLOCK)
        p_own = p[..., k_sel * MOBA_BLOCK:]
        return (jnp.einsum('bhqsk,bhqskd->bhqd', p_sel, vg)
                + jnp.einsum('bhqk,bhkd->bhqd', p_own, vo))

    outs = lax.map(chunk_fn, jnp.arange(t_pad // qn))
    out = outs.transpose(1, 2, 0, 3, 4).reshape(b, h, t_pad, d)
    return out[:, :, :t]

def mlstm_mixer(q, k, v, log_i, log_f):
    b, h, t, dk = q.shape
    dv = v.shape[-1]
    L = MLSTM_CHUNK
    n = t // L
    qc = q.reshape(b, h, n, L, dk)
    kc = (k * dk ** -0.5).reshape(b, h, n, L, dk)
    vc = v.reshape(b, h, n, L, dv)
    li = log_i.reshape(b, h, n, L)
    bcum = jnp.cumsum(log_f.reshape(b, h, n, L), axis=-1)
    b_last = bcum[..., -1]
    causal = jnp.tril(jnp.ones((L, L), dtype=bool))
    logD = jnp.where(causal, bcum[..., :, None] - bcum[..., None, :] + li[..., None, :], -jnp.inf)
    log_end = b_last[..., None] - bcum + li
    m_local = jnp.max(log_end, axis=-1)
    w_loc = jnp.exp(log_end - m_local[..., None])
    chunk_kv = jnp.einsum('bhnl,bhnld,bhnlv->bhndv', w_loc, kc, vc)
    chunk_k = jnp.einsum('bhnl,bhnld->bhnd', w_loc, kc)

    def step(carry, inp):
        S, nv, m = carry
        bl, ml, ckv, ck = inp
        m_new = jnp.maximum(bl + m, ml)
        a = jnp.exp(bl + m - m_new)
        c = jnp.exp(ml - m_new)
        S_new = a[..., None, None] * S + c[..., None, None] * ckv
        n_new = a[..., None] * nv + c[..., None] * ck
        return (S_new, n_new, m_new), (S, nv, m)

    init = (jnp.zeros((b, h, dk, dv), q.dtype), jnp.zeros((b, h, dk), q.dtype), jnp.zeros((b, h), q.dtype))
    xs = (jnp.moveaxis(b_last, 2, 0), jnp.moveaxis(m_local, 2, 0),
          jnp.moveaxis(chunk_kv, 2, 0), jnp.moveaxis(chunk_k, 2, 0))
    _, (S_prev, n_prev, m_prev) = lax.scan(step, init, xs)
    S_prev = jnp.moveaxis(S_prev, 0, 2)
    n_prev = jnp.moveaxis(n_prev, 0, 2)
    m_prev = jnp.moveaxis(m_prev, 0, 2)
    m_inter = bcum + m_prev[..., None]
    m_row = jnp.maximum(m_inter, jnp.max(logD, axis=-1))
    s = jnp.einsum('bhnid,bhnjd->bhnij', qc, kc) * jnp.exp(logD - m_row[..., None])
    inter_w = jnp.exp(m_inter - m_row)
    num = (jnp.einsum('bhnij,bhnjv->bhniv', s, vc)
           + inter_w[..., None] * jnp.einsum('bhnid,bhndv->bhniv', qc, S_prev))
    den = jnp.sum(s, axis=-1) + inter_w * jnp.einsum('bhnid,bhnd->bhni', qc, n_prev)
    hid = num / jnp.maximum(jnp.abs(den), jnp.exp(-m_row))[..., None]
    return hid.reshape(b, h, t, dv)

def hybrid_layer(x, cos, sin, norm1_g, w_in, gla_a_up, gla_a_b, gla_norm_g, moba_qn_g, moba_kn_g,
                 mlstm_conv_w, mlstm_i_b, mlstm_f_b, mlstm_norm_g, gate_b, w_br_gla, w_br_moba,
                 w_br_mlstm, w_out, norm2_g, w_ff1, w_ff2):
    dt = x.dtype
    f32 = jnp.float32
    bsz, t, _ = x.shape
    hn = rms_norm(x, norm1_g)
    proj = hn @ w_in
    offsets = np.cumsum(IN_SPLITS)[:-1].tolist()
    (g_q, g_k, g_v, g_g, g_a, m_q, m_k, m_v,
     l_q, l_k, l_v, l_o, l_i, l_f, br_gate) = jnp.split(proj, offsets, axis=-1)

    log_a = jax.nn.log_sigmoid((g_a @ gla_a_up + gla_a_b).astype(f32)) / GLA_GATE_NORM
    o_gla = gla_mixer(split_heads(g_q.astype(f32), GLA_HEADS), split_heads(g_k.astype(f32), GLA_HEADS),
                      split_heads(g_v.astype(f32), GLA_HEADS), split_heads(log_a, GLA_HEADS))
    o_gla = rms_norm(o_gla, gla_norm_g)
    y_gla = (merge_heads(o_gla) * jax.nn.silu(g_g.astype(f32))).astype(dt)

    mq = apply_rope(rms_norm(split_heads(m_q.astype(f32), MOBA_HEADS), moba_qn_g), cos, sin)
    mk = apply_rope(rms_norm(split_heads(m_k.astype(f32), MOBA_HEADS), moba_kn_g), cos, sin)
    mv = split_heads(m_v.astype(f32), MOBA_HEADS)
    y_moba = merge_heads(moba_mixer(mq, mk, mv)).astype(dt)

    qk = causal_dwconv(jnp.concatenate([l_q, l_k], axis=-1).astype(f32), mlstm_conv_w.astype(f32))
    lq, lk = jnp.split(qk, 2, axis=-1)
    log_i = (l_i + mlstm_i_b).astype(f32).transpose(0, 2, 1)
    log_f = jax.nn.log_sigmoid((l_f + mlstm_f_b).astype(f32)).transpose(0, 2, 1)
    h_ml = mlstm_mixer(split_heads(lq, MLSTM_HEADS), split_heads(lk, MLSTM_HEADS),
                       split_heads(l_v.astype(f32), MLSTM_HEADS), log_i, log_f)
    h_ml = rms_norm(h_ml, mlstm_norm_g)
    y_mlstm = (merge_heads(h_ml) * jax.nn.sigmoid(l_o.astype(f32))).astype(dt)

    gates = jax.nn.sigmoid(br_gate + gate_b).reshape(bsz, t, N_BRANCH, D_MODEL)
    mixed = (gates[:, :, 0] * (y_gla @ w_br_gla)
             + gates[:, :, 1] * (y_moba @ w_br_moba)
             + gates[:, :, 2] * (y_mlstm @ w_br_mlstm))
    x = x + mixed @ w_out

    h2 = rms_norm(x, norm2_g)
    x = x + jnp.square(jax.nn.relu(h2 @ w_ff1)) @ w_ff2
    return x

def first_inputs(seed: int = 0) -> dict:
    key = jax.random.key(seed)
    ks = jax.random.split(key, 24)

    def nrm(k, shape, fan_in):
        return jax.random.normal(k, shape, jnp.float32) * (fan_in ** -0.5)

    def gain(k, shape):
        return 1.0 + 0.02 * jax.random.normal(k, shape, jnp.float32)

    f_bias = (jnp.linspace(3.0, 6.0, MLSTM_HEADS, dtype=jnp.float32)[None, :]
              + 0.1 * jax.random.normal(ks[10], (DEPTH, MLSTM_HEADS), jnp.float32))
    return {
        "x": jax.random.normal(ks[0], (BATCH, SEQ, D_MODEL), jnp.float32),
        "norm1_g": gain(ks[1], (DEPTH, D_MODEL)),
        "w_in": nrm(ks[2], (DEPTH, D_MODEL, D_IN), D_MODEL),
        "gla_a_up": nrm(ks[3], (DEPTH, GLA_LOWRANK, GLA_K), GLA_LOWRANK),
        "gla_a_b": 0.02 * jax.random.normal(ks[4], (DEPTH, GLA_K), jnp.float32),
        "gla_norm_g": gain(ks[5], (DEPTH, GLA_DV)),
        "moba_qn_g": gain(ks[6], (DEPTH, MOBA_HD)),
        "moba_kn_g": gain(ks[7], (DEPTH, MOBA_HD)),
        "mlstm_conv_w": nrm(ks[8], (DEPTH, MLSTM_CONV, 2 * MLSTM_QK), MLSTM_CONV),
        "mlstm_i_b": 0.1 * jax.random.normal(ks[9], (DEPTH, MLSTM_HEADS), jnp.float32),
        "mlstm_f_b": f_bias,
        "mlstm_norm_g": gain(ks[11], (DEPTH, MLSTM_DV)),
        "gate_b": 0.02 * jax.random.normal(ks[12], (DEPTH, N_BRANCH * D_MODEL), jnp.float32),
        "w_br_gla": nrm(ks[13], (DEPTH, GLA_V, D_MODEL), GLA_V),
        "w_br_moba": nrm(ks[14], (DEPTH, MOBA_W, D_MODEL), MOBA_W),
        "w_br_mlstm": nrm(ks[15], (DEPTH, MLSTM_V, D_MODEL), MLSTM_V),
        "w_out": nrm(ks[16], (DEPTH, D_MODEL, D_MODEL), D_MODEL),
        "norm2_g": gain(ks[17], (DEPTH, D_MODEL)),
        "w_ff1": nrm(ks[18], (DEPTH, D_MODEL, D_FF), D_MODEL),
        "w_ff2": nrm(ks[19], (DEPTH, D_FF, D_MODEL), D_FF),
    }

def first_block(x, norm1_g, w_in, gla_a_up, gla_a_b, gla_norm_g, moba_qn_g, moba_kn_g, mlstm_conv_w,
              mlstm_i_b, mlstm_f_b, mlstm_norm_g, gate_b, w_br_gla, w_br_moba, w_br_mlstm, w_out,
              norm2_g, w_ff1, w_ff2):
    cos, sin = rope_tables(x.shape[1], MOBA_HD)
    for l in range(DEPTH):
        x = hybrid_layer(x, cos, sin, norm1_g[l], w_in[l], gla_a_up[l], gla_a_b[l], gla_norm_g[l],
                         moba_qn_g[l], moba_kn_g[l], mlstm_conv_w[l], mlstm_i_b[l], mlstm_f_b[l],
                         mlstm_norm_g[l], gate_b[l], w_br_gla[l], w_br_moba[l], w_br_mlstm[l], w_out[l],
                         norm2_g[l], w_ff1[l], w_ff2[l])
    return x


DEPTH_2 = 1

N_HEADS = 8
QK_NOPE_DIM = 64
QK_ROPE_DIM = 32
V_HEAD_DIM = 64
Q_LORA_RANK = 256
KV_LORA_RANK = 256
ATTN_WIDTH = N_HEADS * V_HEAD_DIM
Q_BLOCK = 128
FOURIER_GROUPS = 8
FOURIER_GROUP_DIM = 64
FOURIER_WIDTH = FOURIER_GROUPS * FOURIER_GROUP_DIM
N_BRANCHES = 2
N_EXPERT_GROUPS = 4
EXPERTS_PER_GROUP = 8
N_EXPERTS = N_EXPERT_GROUPS * EXPERTS_PER_GROUP
TOP_K_INNER = 2
D_EXPERT = 256
N_ADA = 6

IN_SIZES = (Q_LORA_RANK, KV_LORA_RANK, QK_ROPE_DIM, FOURIER_WIDTH, N_BRANCHES * D_MODEL)
IN_SPLITS_2 = tuple(int(v) for v in np.cumsum(IN_SIZES)[:-1])
IN_COLS = int(sum(IN_SIZES))


def rmsnorm(x, g):
    xf = x.astype(jnp.float32)
    r = lax.rsqrt(jnp.mean(xf * xf, axis=-1, keepdims=True) + EPS)
    return (xf * r * g.astype(jnp.float32)).astype(x.dtype)

def modulate(h, shift, scale):
    return h * (1.0 + scale[:, None, :]) + shift[:, None, :]

def rope_angles(positions):
    inv_freq = ROPE_THETA ** (-jnp.arange(0, QK_ROPE_DIM, 2, dtype=jnp.float32) / QK_ROPE_DIM)
    ang = positions.astype(jnp.float32)[..., None] * inv_freq
    return jnp.cos(ang), jnp.sin(ang)

def apply_rope_2(x, cos, sin):
    half = QK_ROPE_DIM // 2
    x1, x2 = x[..., :half], x[..., half:]
    cos = cos.astype(x.dtype)
    sin = sin.astype(x.dtype)
    return jnp.concatenate([x1 * cos - x2 * sin, x2 * cos + x1 * sin], axis=-1)

def mla_attention(q_lat, kv_lat, k_rope, positions, g_q, g_kv, w_uq, w_uk, w_uv):
    B, S, _ = q_lat.shape
    q_lat = rmsnorm(q_lat, g_q)
    kv_lat = rmsnorm(kv_lat, g_kv)
    q = jnp.einsum('bsr,rhd->bshd', q_lat, w_uq)
    q_nope, q_rope = q[..., :QK_NOPE_DIM], q[..., QK_NOPE_DIM:]
    k_nope = jnp.einsum('bsr,rhd->bshd', kv_lat, w_uk)
    v = jnp.einsum('bsr,rhd->bshd', kv_lat, w_uv)
    cos, sin = rope_angles(positions)
    q_rope = apply_rope_2(q_rope, cos[:, :, None, :], sin[:, :, None, :])
    k_rope = apply_rope_2(k_rope, cos, sin)
    scale = (QK_NOPE_DIM + QK_ROPE_DIM) ** -0.5
    nb = S // Q_BLOCK
    qn_blk = (q_nope * scale).reshape(B, nb, Q_BLOCK, N_HEADS, QK_NOPE_DIM).transpose(1, 0, 2, 3, 4)
    qr_blk = (q_rope * scale).reshape(B, nb, Q_BLOCK, N_HEADS, QK_ROPE_DIM).transpose(1, 0, 2, 3, 4)

    def attend(blk):
        qn, qr = blk
        s = (jnp.einsum('bqhd,bkhd->bhqk', qn, k_nope)
             + jnp.einsum('bqhd,bkd->bhqk', qr, k_rope))
        p = jax.nn.softmax(s.astype(jnp.float32), axis=-1).astype(v.dtype)
        return jnp.einsum('bhqk,bkhd->bqhd', p, v)

    o = lax.map(attend, (qn_blk, qr_blk))
    return o.transpose(1, 0, 2, 3, 4).reshape(B, S, ATTN_WIDTH)

def fourier_mix(u):
    B, S, _ = u.shape
    ug = u.astype(jnp.float32).reshape(B, S, FOURIER_GROUPS, FOURIER_GROUP_DIM)
    f = jnp.fft.fft2(ug, axes=(1, 3), norm='ortho').real
    return f.reshape(B, S, FOURIER_WIDTH).astype(u.dtype)

def hierarchical_moe(h, w_rg, b_rg, w_re, b_re, w_gate, w_up, w_down):
    B, S, D = h.shape
    t = h.reshape(B * S, D)
    g_logits = (t @ w_rg).astype(jnp.float32) + b_rg.astype(jnp.float32)
    g_prob = jax.nn.softmax(g_logits, axis=-1)
    g_sel = jnp.argmax(g_prob, axis=-1)
    g_p = jnp.take_along_axis(g_prob, g_sel[:, None], axis=-1)[:, 0]
    e_logits = jnp.einsum('td,dge->tge', t, w_re).astype(jnp.float32) + b_re.astype(jnp.float32)
    e_logits = jnp.take_along_axis(e_logits, g_sel[:, None, None], axis=1)[:, 0]
    e_prob = jax.nn.softmax(e_logits, axis=-1)
    top_p, top_i = lax.top_k(e_prob, TOP_K_INNER)
    top_p = top_p / jnp.sum(top_p, axis=-1, keepdims=True)
    weights = g_p[:, None] * top_p
    global_idx = g_sel[:, None] * EXPERTS_PER_GROUP + top_i
    combine = jnp.sum(jax.nn.one_hot(global_idx, N_EXPERTS, dtype=jnp.float32)
                      * weights[..., None], axis=1).astype(t.dtype)
    out = jnp.zeros_like(t)
    for e in range(N_EXPERTS):
        hid = jax.nn.silu(t @ w_gate[e]) * (t @ w_up[e])
        out = out + combine[:, e:e + 1] * (hid @ w_down[e])
    return out.reshape(B, S, D)

def second_inputs(seed: int = 0) -> dict:
    key = jax.random.key(seed)
    ks = jax.random.split(key, 32)
    f32 = jnp.float32
    L, D = DEPTH_2, D_MODEL

    def nrm(k, shape, fan_in, mult=1.0):
        return jax.random.normal(k, shape, f32) * (mult * fan_in ** -0.5)

    def gain(k, shape):
        return 1.0 + 0.02 * jax.random.normal(k, shape, f32)

    x = jax.random.normal(ks[0], (BATCH, SEQ, D), f32)
    c = jax.random.normal(ks[1], (BATCH, D), f32)
    positions = jnp.sort(jax.random.randint(ks[2], (BATCH, SEQ), 0, 4 * SEQ), axis=-1).astype(jnp.int32)
    return {
        "x": x,
        "c": c,
        "positions": positions,
        "w_ada": nrm(ks[3], (L, D, N_ADA * D), D, 0.5),
        "b_ada": 0.02 * jax.random.normal(ks[4], (L, N_ADA * D), f32),
        "g_norm_mix": gain(ks[5], (L, D)),
        "w_in": nrm(ks[6], (L, D, IN_COLS), D),
        "g_q_lat": gain(ks[7], (L, Q_LORA_RANK)),
        "g_kv_lat": gain(ks[8], (L, KV_LORA_RANK)),
        "w_uq": nrm(ks[9], (L, Q_LORA_RANK, N_HEADS, QK_NOPE_DIM + QK_ROPE_DIM), Q_LORA_RANK),
        "w_uk": nrm(ks[10], (L, KV_LORA_RANK, N_HEADS, QK_NOPE_DIM), KV_LORA_RANK),
        "w_uv": nrm(ks[11], (L, KV_LORA_RANK, N_HEADS, V_HEAD_DIM), KV_LORA_RANK),
        "w_branch_attn": nrm(ks[12], (L, ATTN_WIDTH, D), ATTN_WIDTH),
        "w_branch_fourier": nrm(ks[13], (L, FOURIER_WIDTH, D), FOURIER_WIDTH),
        "b_gates": 0.02 * jax.random.normal(ks[14], (L, N_BRANCHES * D), f32),
        "w_out": nrm(ks[15], (L, D, D), D),
        "g_norm_ffn": gain(ks[16], (L, D)),
        "w_router_group": nrm(ks[17], (L, D, N_EXPERT_GROUPS), D),
        "b_router_group": 0.01 * jax.random.normal(ks[18], (L, N_EXPERT_GROUPS), f32),
        "w_router_expert": nrm(ks[19], (L, D, N_EXPERT_GROUPS, EXPERTS_PER_GROUP), D),
        "b_router_expert": 0.01 * jax.random.normal(ks[20], (L, N_EXPERT_GROUPS, EXPERTS_PER_GROUP), f32),
        "w_expert_gate": nrm(ks[21], (L, N_EXPERTS, D, D_EXPERT), D),
        "w_expert_up": nrm(ks[22], (L, N_EXPERTS, D, D_EXPERT), D),
        "w_expert_down": nrm(ks[23], (L, N_EXPERTS, D_EXPERT, D), D_EXPERT),
        "w_ada_final": nrm(ks[24], (D, 2 * D), D, 0.5),
        "b_ada_final": 0.02 * jax.random.normal(ks[25], (2 * D,), f32),
        "g_norm_final": gain(ks[26], (D,)),
    }

def second_block(x, c, positions, w_ada, b_ada, g_norm_mix, w_in, g_q_lat, g_kv_lat,
              w_uq, w_uk, w_uv, w_branch_attn, w_branch_fourier, b_gates, w_out,
              g_norm_ffn, w_router_group, b_router_group, w_router_expert, b_router_expert,
              w_expert_gate, w_expert_up, w_expert_down, w_ada_final, b_ada_final, g_norm_final):
    h = x
    c_act = jax.nn.silu(c)
    for l in range(DEPTH_2):
        mod = c_act @ w_ada[l] + b_ada[l]
        sh1, sc1, gt1, sh2, sc2, gt2 = jnp.split(mod, N_ADA, axis=-1)

        u = modulate(rmsnorm(h, g_norm_mix[l]), sh1, sc1)
        z = u @ w_in[l]
        q_lat, kv_lat, k_rope, f_in, gate_logits = jnp.split(z, IN_SPLITS_2, axis=-1)
        a = mla_attention(q_lat, kv_lat, k_rope, positions, g_q_lat[l], g_kv_lat[l],
                          w_uq[l], w_uk[l], w_uv[l]) @ w_branch_attn[l]
        fo = fourier_mix(f_in) @ w_branch_fourier[l]
        ga, gf = jnp.split(gate_logits + b_gates[l], N_BRANCHES, axis=-1)
        merged = jax.nn.sigmoid(ga) * a + jax.nn.sigmoid(gf) * fo
        h = h + gt1[:, None, :] * (merged @ w_out[l])

        v = modulate(rmsnorm(h, g_norm_ffn[l]), sh2, sc2)
        h = h + gt2[:, None, :] * hierarchical_moe(
            v, w_router_group[l], b_router_group[l], w_router_expert[l], b_router_expert[l],
            w_expert_gate[l], w_expert_up[l], w_expert_down[l])

    fmod = c_act @ w_ada_final + b_ada_final
    shf, scf = jnp.split(fmod, 2, axis=-1)
    return modulate(rmsnorm(h, g_norm_final), shf, scf)


def setup_inputs(seed=0):
    out = dict(first_inputs(seed))
    for name, value in second_inputs(seed + 1).items():
        if name != "x":
            out[name + "_2"] = value
    return out


def reference(
    x, norm1_g, w_in, gla_a_up, gla_a_b, gla_norm_g, moba_qn_g, moba_kn_g, mlstm_conv_w,
    mlstm_i_b, mlstm_f_b, mlstm_norm_g, gate_b, w_br_gla, w_br_moba, w_br_mlstm, w_out, norm2_g,
    w_ff1, w_ff2, c_2, positions_2, w_ada_2, b_ada_2, g_norm_mix_2, w_in_2, g_q_lat_2,
    g_kv_lat_2, w_uq_2, w_uk_2, w_uv_2, w_branch_attn_2, w_branch_fourier_2, b_gates_2, w_out_2,
    g_norm_ffn_2, w_router_group_2, b_router_group_2, w_router_expert_2, b_router_expert_2,
    w_expert_gate_2, w_expert_up_2, w_expert_down_2, w_ada_final_2, b_ada_final_2,
    g_norm_final_2,
):
    x = first_block(
        x, norm1_g, w_in, gla_a_up, gla_a_b, gla_norm_g, moba_qn_g, moba_kn_g, mlstm_conv_w,
        mlstm_i_b, mlstm_f_b, mlstm_norm_g, gate_b, w_br_gla, w_br_moba, w_br_mlstm, w_out,
        norm2_g, w_ff1, w_ff2,
    )
    return second_block(
        x, c_2, positions_2, w_ada_2, b_ada_2, g_norm_mix_2, w_in_2, g_q_lat_2, g_kv_lat_2,
        w_uq_2, w_uk_2, w_uv_2, w_branch_attn_2, w_branch_fourier_2, b_gates_2, w_out_2,
        g_norm_ffn_2, w_router_group_2, b_router_group_2, w_router_expert_2, b_router_expert_2,
        w_expert_gate_2, w_expert_up_2, w_expert_down_2, w_ada_final_2, b_ada_final_2,
        g_norm_final_2,
    )


_drawn_inputs = setup_inputs


def setup_inputs(seed=0):
    import zlib

    import numpy as np

    out = dict(_drawn_inputs(seed))
    spreads = {}
    factors = {'gla_a_b': 8.0,
     'gla_norm_g': 5.998,
     'moba_qn_g': 8.0,
     'moba_kn_g': 8.0,
     'mlstm_i_b': 8.0,
     'mlstm_norm_g': 6.968,
     'gate_b': 8.0,
     'b_ada_2': 6.652,
     'g_norm_mix_2': 8.0,
     'g_q_lat_2': 8.0,
     'g_kv_lat_2': 8.0,
     'w_uq_2': 8.0,
     'w_uk_2': 8.0,
     'b_gates_2': 8.0,
     'g_norm_ffn_2': 8.0,
     'b_router_group_2': 8.0,
     'b_router_expert_2': 8.0,
     'g_norm_final_2': 7.956,
     'b_ada_final_2': 2.842}
    for name, (base, spread) in spreads.items():
        noise = np.random.default_rng([zlib.crc32(name.encode()), seed]).standard_normal(out[name].shape)
        drawn = base * np.exp(spread * noise) if base else spread * noise
        out[name] = __import__('jax').numpy.asarray(drawn.astype(out[name].dtype))
    for name, factor in factors.items():
        out[name] = (out[name] * factor).astype(out[name].dtype)
    return out
```

```python
from contextlib import ExitStack

import numpy as np

import concourse.bass as bass
from concourse import mybir

F32 = mybir.dt.float32
F32R = mybir.dt.float32r
U8 = mybir.dt.uint8
I32 = mybir.dt.int32
ALU = mybir.AluOpType
ACT = mybir.ActivationFunctionType
AX_X = mybir.AxisListType.X

P = 128
T = 256
NT = T // P
D = 1024
KD = D // P
DEPTH = 2
L = 64
NC = T // L
W = 512
EPS = 1e-6
NEG = -1e30
FF_CHUNKS = 4 * D // W
EXPERTS = 32
N_GROUPS, PER_GROUP = 4, 8
H8, HD = 8, 64
GH, GD = 4, 128
MH, MK, MV = 4, 64, 128
ROPE2 = 32
QK2 = 96
ADA = 2 * FF_CHUNKS

UNIT = 2048
HALF = UNIT // 2
STAGES = 4
SPLITS = 4
PAD_UNITS = 2
LAYER_UNITS = 16 * 2 + 6 + 4 + 4 * FF_CHUNKS + PAD_UNITS
BLOCK2_UNITS = 12 + 2 + 4 + 4
UNITS = DEPTH * LAYER_UNITS + BLOCK2_UNITS + 3 * EXPERTS
assert T == 2 * P and LAYER_UNITS % STAGES == 0

LAYER_COLS = dict(g1=8, g2=8, ab=4, conv=16, gn=128, qn=64, kn=64, mn=128, ifb=2, aup=512, wsm=8 * 24)
B2_COLS = dict(gmix=8, gffn=8, gq=2, gkv=2, bcols=32, wkr=8 * 32, wr=8 * 36, br=36)
CONST_COLS = dict(ident=128, cmask=256, lmask=128, reset=256, resetneg=256, cos=64, sin=64,
                  desc=8, invf=16)


def offsets(cols):
    at, out = 0, {}
    for name, n in cols.items():
        out[name] = (at, at + n)
        at += n
    return out, at


LAYER_AT, LAYER_N = offsets(LAYER_COLS)
B2_AT, B2_N = offsets(B2_COLS)
CONST_AT, CONST_N = offsets(CONST_COLS)


class Loop:

    def __init__(self, count):
        self.count, self.var, self.moved, self.items = count, {}, {}, {}


class Mark:

    def __init__(self, sem, const, loops):
        self.sem, self.const, self.loops = sem, const, loops


class Recorder:

    ENGINES = ("pe", "act", "dve", "pool", "sp")

    def __init__(self):
        self.at = {}
        self.loops = []
        self.queue = {e: [] for e in self.ENGINES}
        self.waited = {e: {} for e in self.ENGINES}
        self.last = {}

    def mark(self, sem, ahead=0):
        return Mark(sem, self.at.get(sem, 0) + ahead, tuple(self.loops))

    def step(self, engine, fn, after=(), sem=None, by=1, alone=False):
        sem = sem or engine
        waits = [m for m in after if m is not None]
        if engine in ("act", "dve", "pool") and not alone and engine in self.at:
            waits.append(self.mark(engine))
        known = self.waited[engine]
        best = {}
        for m in waits:
            key = (m.sem, m.loops)
            if m.const <= known.get(key, 0):
                continue
            if key not in best or best[key].const < m.const:
                best[key] = m
        for key, m in best.items():
            known[key] = m.const
        self.queue[engine].append((list(best.values()), fn, sem if by else None, by,
                                   tuple(self.loops)))
        if not by:
            return None
        self.at[sem] = self.at.get(sem, 0) + by
        return self.mark(sem)

    def loop(self, count, body):
        loop = Loop(count)
        outer, before = self.queue, dict(self.at)
        self.queue = {e: [] for e in self.ENGINES}
        self.loops.append(loop)
        self.waited = {e: {} for e in self.ENGINES}
        body(loop)
        self.loops.pop()
        self.waited = {e: {} for e in self.ENGINES}
        for sem, value in self.at.items():
            moved = value - before.get(sem, 0)
            loop.moved[sem] = moved
            self.at[sem] = before.get(sem, 0) + count * moved
        for e in self.ENGINES:
            loop.items[e] = self.queue[e]
            outer[e].append(loop)
        self.queue = outer
        return loop

    def emit(self, name, engine, sems, items=None):
        for item in self.queue[name] if items is None else items:
            if isinstance(item, Loop):
                if item.items[name]:
                    with engine.Fori(0, item.count) as i:
                        item.var[name] = i
                        self.emit(name, engine, sems, item.items[name])
                continue
            waits, fn, sem, by, loops = item
            for m in waits:
                value = m.const
                for lp in m.loops:
                    per = lp.moved.get(m.sem, 0)
                    if lp in loops:
                        if per:
                            value = lp.var[name] * per + value
                    else:
                        value += (lp.count - 1) * per
                engine.wait_ge(sems[m.sem], value)
            ins = fn(engine)
            if sem is not None:
                ins.then_inc(sems[sem], by)


def build_program(nc, wall, wada, layer_small, gate_b, b2_small, rows2, consts, dft, pos, c, x_in, out):
    rec = Recorder()
    step, mark = rec.step, rec.mark
    with ExitStack() as ctx:
        def sb(name, shape, dt=F32):
            return ctx.enter_context(nc.sbuf_tensor(name, shape, dt))

        stage = sb("stage", [P, STAGES, UNIT])
        w_hi = sb("w_hi", [P, SPLITS, HALF], F32R)
        w_lo = sb("w_lo", [P, SPLITS, HALF], F32R)
        X = sb("X", [P, NT, D])
        a_hi = sb("a_hi", [P, KD, T], F32R)
        a_lo = sb("a_lo", [P, KD, T], F32R)
        h_hi = sb("h_hi", [P, W // P, T], F32R)
        h_lo = sb("h_lo", [P, W // P, T], F32R)
        s_hi = sb("s_hi", [P, 8 * 36], F32R)
        s_lo = sb("s_lo", [P, 8 * 36], F32R)
        ada_cols = sb("ada_cols", [P, DEPTH, 32])
        csm = sb("csm", [P, CONST_N])
        lsm = sb("lsm", [P, max(LAYER_N, B2_N)])
        gm8 = sb("gm8", [P, P], U8)
        ones = sb("ones", [P, P])
        mhalf = sb("mhalf", [P, 16])
        cact = sb("cact", [P, KD])
        st = sb("st", [P, 256])
        fix = sb("fix", [P, 640])
        PR = sb("PR", [P, 10 * NT * W])
        G = sb("G", [P, NT, 3 * D])
        S = sb("S", [P, 5632])
        Gf = G[:, :, :].rearrange("p t n -> p (t n)")
        ada_rows = Gf[:, 0:4 * D].rearrange("p (c w) -> p c w", w=W)
        li_row = sb("li_row", [MH, T])
        BF16 = mybir.dt.bfloat16
        zrow = sb("zrow", [1, W], BF16)
        zcol = sb("zcol", [1, P], BF16)
        PS = ctx.enter_context(nc.psum_tensor("PS", [P, 8, W], F32))

        sem_names = (["pe", "act", "dve", "pool", "hi", "lo", "used", "ld_const", "ld_x", "ld_layer", "ld_gate",
                      "ld_b2", "ld_rows", "ld_dft", "ld_ada0", "ld_ada1", "ada_used", "st_out"]
                     + [f"landed{i}" for i in range(STAGES)])
        sems = {n: ctx.enter_context(nc.semaphore("s_" + n)) for n in sem_names}
        for n in sem_names:
            rec.at[n] = 0

        def const(name):
            a, b = CONST_AT[name]
            return csm[:, a:b]

        def lay(name):
            a, b = LAYER_AT[name]
            return lsm[:, a:b]

        def b2(name):
            a, b = B2_AT[name]
            return lsm[:, a:b]

        ident = const("ident")

        def proj(c, n=1):
            return PR[:, c * NT * W:(c + n) * NT * W]

        def chunk(c):
            return proj(c).rearrange("p (t w) -> p t w", t=NT)

        def act(out_, in_, func=ACT.Copy, after=(), sem=None, alone=False, **kw):
            return step("act", lambda e: e.activation(out_, in_, func, **kw), after, sem, alone=alone)

        def tt(out_, a, b, op, after=(), sem=None, alone=False):
            return step("dve", lambda e: e.tensor_tensor(out_, a, b, op), after, sem, alone=alone)

        def ts(out_, a, s1, s2, op0, op1=None, after=()):
            if op1 is None:
                return step("dve", lambda e: e.tensor_scalar(out_, a, s1, None, op0), after)
            return step("dve", lambda e: e.tensor_scalar(out_, a, s1, s2, op0, op1), after)

        def stt(out_, a, s, b, op0, op1, after=()):
            return step("dve", lambda e: e.scalar_tensor_tensor(out=out_, in0=a, scalar=s, in1=b,
                                                               op0=op0, op1=op1), after)

        def copy(out_, a, after=()):
            return step("dve", lambda e: e.tensor_copy(out_, a), after)

        def reduce(out_, a, op, after=(), negate=None):
            return step("dve", lambda e: e.tensor_reduce(out_, a, AX_X, op, negate=negate), after)

        def recip(out_, a, after=()):
            return step("dve", lambda e: e.reciprocal(out_, a), after)

        def fill(out_, v, after=()):
            return step("dve", lambda e: e.memset(out_, v), after)

        def mm(out_, lhsT, rhs, start=True, stop=True, after=(), signal=True):
            return step("pe", lambda e: e.matmul(out_, lhsT, rhs, start=start, stop=stop,
                                                 skip_group_check=True), after, by=int(signal))

        def turn(out_, in_, after=(), signal=True, n=P):
            return step("pe", lambda e: e.transpose(out_, in_, ident[0:n, 0:n]), after, by=int(signal))

        def r32(ap):
            return ap.bitcast(F32)

        passes, rest = divmod(UNITS, STAGES)

        def load_unit(e, unit, slot):
            return e.dma_start(stage[:, slot, :], wall[bass.ds(unit, 1), :, :].rearrange("o p n -> p (o n)"))

        def feed(e):
            def one(i, k):
                ahead = 2 * (k + 1)
                base = 2 * STAGES * i + ahead
                for name in ("hi", "lo"):
                    e.wait_ge(sems[name], base)
                load_unit(e, STAGES * i + STAGES + k, k).then_inc(sems[f"landed{k}"], 16)
            for k in range(STAGES):
                load_unit(e, k, k).then_inc(sems[f"landed{k}"], 16)
            with e.Fori(0, passes - 1) as i:
                for k in range(STAGES):
                    one(i, k)
            for k in range(rest):
                one(passes - 1, k)

        state = {"half": 0, "split": 0}

        def split_half():
            h = state["split"]
            if h >= 2 * UNITS:
                return
            state["split"] += 1
            slot, unit_slot, side = h % SPLITS, (h // 2) % STAGES, h % 2
            src = stage[:, unit_slot, side * HALF:(side + 1) * HALF]
            landed = at(f"landed{unit_slot}", 16 * (h // 2 // STAGES + 1))
            free = at("used", h - SPLITS + 1)
            rounded = act(w_hi[:, slot, :], src, after=(landed, free), sem="hi", alone=True)
            tt(w_lo[:, slot, :], src, r32(w_hi[:, slot, :]), ALU.subtract, after=(landed, free, rounded),
               sem="lo", alone=True)

        def at(sem, value):
            return Mark(sem, value, tuple(rec.loops)) if value > 0 else None

        def take_half():
            h = state["half"]
            return h % SPLITS, (at("hi", h + 1), at("lo", h + 1))

        def used_half(fn, after=()):
            m = step("pe", fn, after, sem="used")
            state["half"] += 1
            split_half()
            return m

        def stream_loop(count, body):
            start = state["half"]
            loop = rec.loop(count, body)
            moved = state["half"] - start
            assert moved % (2 * STAGES) == 0 and state["split"] - state["half"] == SPLITS
            for k in range(STAGES):
                loop.moved[f"landed{k}"] = 16 * moved // (2 * STAGES)
            state["half"] = start + count * moved
            state["split"] = state["half"] + SPLITS

        def product(accs, acts_hi, acts_lo, kt, slot, cols, first, last, after, signal):
            todo = []
            for t in range(NT):
                tok = slice(t * P, (t + 1) * P)
                ah, al = acts_hi[:, kt, tok], acts_lo[:, kt, tok]
                for acc, (a, b) in zip(accs[t], cols):
                    wh, wl = w_hi[:, slot, a:b], w_lo[:, slot, a:b]
                    todo += [(acc, ah, wh, first, False), (acc, ah, wl, False, False),
                             (acc, al, wh, False, last)]
            for n, (acc, a, w, s0, s1) in enumerate(todo):
                fn = (lambda e, acc=acc, a=a, w=w, s0=s0, s1=s1:
                      e.matmul(acc, a, w, start=s0, stop=s1, skip_group_check=True))
                if signal and n == len(todo) - 1:
                    return used_half(fn, after if n == 0 else ())
                step("pe", fn, after if n == 0 else (), by=0)

        def project(banks, nk, after=(), ah=a_hi, al=a_lo, k0=0):
            for half in range(nk // 2):
                slot, ready = take_half()
                for j in range(2):
                    kt = 2 * half + j
                    m = product([[PS[:, banks[t], :]] for t in range(NT)], ah, al, k0 + kt, slot,
                                [(j * W, (j + 1) * W)], kt == 0, kt == nk - 1,
                                tuple(ready) + (tuple(after) if kt == 0 else ()), j == 1)
                yield m

        def finish(gen):
            m = None
            for m in gen:
                pass
            return m

        step("act", lambda e: e.dma_start(X[:, :, :], x_in.rearrange("(t p) d -> p t d", p=P)), sem="ld_x", by=16)
        step("act", lambda e: e.dma_start(csm[:, :], consts), sem="ld_const", by=16)
        step("act", lambda e: e.dma_start(cact[:, :], c), sem="ld_const", by=16)
        loaded_const, loaded_x = mark("ld_const"), mark("ld_x")
        fill(ones[:, :], 1.0)
        fill(zrow[:, :], 0.0)
        fill(zcol[:, :], 0.0)
        ready_ones = fill(mhalf[:, :], -0.5)
        ts(gm8[:, :], const("lmask"), 0.0, None, ALU.is_equal, after=(loaded_const,))
        act(cact[:, :], cact[:, :], ACT.Silu, after=(loaded_const,))
        for _ in range(SPLITS):
            split_half()

        def rsqrt_mean(dst, ssum, n, width):
            m = ts(dst, ssum, 1.0 / n, EPS, ALU.mult, ALU.add)
            return step("pool", lambda e: e.tensor_tensor(dst, dst, mhalf[:, 0:width], ALU.pow), (m, ready_ones))

        def turn_split(src, nk, dst_hi, dst_lo, banks, after=(), scale=None, bias=None):
            out_ = []
            for b in range(nk // 2):
                bank = banks[b % len(banks)]
                reuse = out_[b - len(banks)] if b >= len(banks) else ()
                for j in range(2):
                    for t in range(NT):
                        m = turn(PS[:, bank, (2 * j + t) * P:(2 * j + t + 1) * P], src(t, 2 * b + j),
                                 tuple(after) + tuple(reuse), signal=(j == 1 and t == 1))
                if scale is None:
                    hi, lo = (d[:, 2 * b:2 * b + 2, :].rearrange("p k t -> p (k t)") for d in (dst_hi, dst_lo))
                    m1 = act(hi, PS[:, bank, :], after=(m,))
                    m2 = tt(lo, PS[:, bank, :], r32(hi), ALU.subtract, after=(m1, m))
                else:
                    ks = (2 * b, 2 * b + 1)
                    ps = {k: PS[:, bank, (k % 2) * T:(k % 2 + 1) * T] for k in ks}
                    for k in ks:
                        kw = {} if bias is None else dict(bias=bias[:, k:k + 1])
                        m1 = act(dst_hi[:, k, :], ps[k], ACT.Copy if bias is None else ACT.Identity, after=(m,),
                                 scale=scale[:, k:k + 1], **kw)
                    for k in ks:
                        if bias is None:
                            m2 = stt(dst_lo[:, k, :], ps[k], scale[:, k:k + 1], r32(dst_hi[:, k, :]), ALU.mult,
                                     ALU.subtract, after=(m1,))
                        else:
                            tmp = S[:, 2 * D + (k % 2) * T:2 * D + (k % 2 + 1) * T]
                            ts(tmp, ps[k], scale[:, k:k + 1], bias[:, k:k + 1], ALU.mult, ALU.add, after=(m1,))
                            m2 = tt(dst_lo[:, k, :], tmp, r32(dst_hi[:, k, :]), ALU.subtract)
                out_.append((m1, m2))
            return out_[-1]

        def norm_rows(after=()):
            xs = S[:, 0:NT * D].rearrange("p (t d) -> p t d", t=NT)
            for t in range(NT):
                m = step("act", lambda e, t=t: e.activation(xs[:, t, :], X[:, t, :], ACT.Square,
                                                            accum_out=st[:, t:t + 1]), after)
            ts(st[:, 2:4], st[:, 0:2], 1.0 / D, EPS, ALU.mult, ALU.add, after=(m,))
            m = step("pool", lambda e: e.tensor_tensor(st[:, 2:4], st[:, 2:4], mhalf[:, 0:2], ALU.pow),
                     (mark("dve"), ready_ones))
            for t in range(NT):
                mx = ts(xs[:, t, :], X[:, t, :], st[:, 2 + t:3 + t], None, ALU.mult, after=(m, mark("act")))
            return xs, mx

        def norm_turn(scale, bias=None, after=()):
            xs, m = norm_rows(after)
            return turn_split(lambda t, k: xs[:, t, k * P:(k + 1) * P], KD, a_hi, a_lo, [0, 1, 2, 3],
                              after=(m,), scale=scale, bias=bias)

        def head_norm(v, nh, hd, tmp, gain, after=()):
            tt(tmp, v, v, ALU.mult, after=after)
            reduce(st[:, 16:16 + nh], tmp, ALU.add)
            m = rsqrt_mean(st[:, 32:32 + nh], st[:, 16:16 + nh], hd, nh)
            tt(v, v, st[:, 32:32 + nh].unsqueeze(2).broadcast_to([P, nh, hd]), ALU.mult, after=(m,))
            return tt(v, v, gain.unsqueeze(1).broadcast_to([P, nh, hd]), ALU.mult)

        def softmax_heads(nh, qT, kT, values, dst, scale, causal, banks, after=(), pt_at=None):
            ba, bb, bt, bo = banks
            pbuf = lambda g: S[:, 4608 + (g % 2) * W:4608 + (g % 2 + 1) * W]
            pt_at = S[:, 0:2 * W] if pt_at is None else pt_at
            pt = lambda g: pt_at[:, (g % 2) * W:(g % 2 + 1) * W]
            outs_read = None
            group = [(4 * (g // 2) + g % 2, 4 * (g // 2) + g % 2 + 2) for g in range(nh // 2)]
            for t in range(NT):
                keys = (t + 1) * P if causal else T
                nj = keys // P
                scored, exps = {}, {}

                def scores(g):
                    bank = (ba, bb)[g % 2]
                    for j, h in enumerate(group[g]):
                        m = mm(PS[:, bank, j * T:j * T + keys], qT(h, t), kT(h, keys), signal=(j == 1),
                               after=tuple(after) + (exps.get(g - 2), mark("act"), mark("dve")) if j == 0 else ())
                    scored[g] = m

                scores(0)
                yield
                for g in range(nh // 2):
                    if g + 1 < nh // 2:
                        scores(g + 1)
                    ps = PS[:, (ba, bb)[g % 2], :].rearrange("p (j k) -> p j k", j=2)[:, :, 0:keys]
                    pv = pbuf(g).rearrange("p (j k) -> p j k", j=2)[:, :, 0:keys]
                    nm = st[:, 64 + 2 * g:66 + 2 * g]
                    if causal:
                        cm = const("cmask")[:, T - keys:T].unsqueeze(1).broadcast_to([P, 2, keys])
                        stt(pv, ps, scale, cm, ALU.mult, ALU.add, after=(scored[g],))
                        m = reduce(nm, pv, ALU.max, negate=True)
                        src, sc = pv, 1.0
                    else:
                        reduce(nm, ps, ALU.max, after=(scored[g],), negate=True)
                        m = ts(nm, nm, scale, None, ALU.mult)
                        src, sc = ps, scale
                    for j, h in enumerate(group[g]):
                        m = step("act", lambda e, j=j, h=h, pv=pv, src=src, sc=sc, g=g: e.activation(
                            pv[:, j, :], src[:, j, :], ACT.Exp, bias=st[:, 64 + 2 * g + j:65 + 2 * g + j], scale=sc,
                            accum_out=st[:, 80 + h:81 + h]), (m,) if j == 0 else ())
                    exps[g] = m
                    yield
                    for j in range(2):
                        for n in range(nj):
                            at = (j * nj + n) * P
                            m = turn(PS[:, bt, at:at + P], pv[:, j, n * P:(n + 1) * P],
                                     (exps[g], mark("dve")) if (j, n) == (0, 0) else (), signal=(j == 1 and n == nj - 1))
                    m = copy(pt(g)[:, 0:2 * keys], PS[:, bt, 0:2 * keys], after=(m,))
                    yield
                    for j, h in enumerate(group[g]):
                        for n in range(nj):
                            m = mm(PS[:, bo, h * HD:(h + 1) * HD], pt(g)[:, (j * nj + n) * P:(j * nj + n + 1) * P],
                                   values(h, n), start=(n == 0), stop=(n == nj - 1),
                                   after=(m, outs_read) if (j, n) == (0, 0) else (), signal=(j == 1 and n == nj - 1))
                recip(st[:, 96:96 + nh], st[:, 80:80 + nh], after=(mark("act"),))
                outs_read = tt(dst(t), PS[:, bo, :].rearrange("p (h d) -> p h d", h=nh),
                               st[:, 96:96 + nh].unsqueeze(2).broadcast_to([P, nh, HD]), ALU.mult, after=(m,))
                yield

        def evacuate(c, banks, m, after=()):
            m0 = act(chunk(c)[:, 0, :], PS[:, banks[0], :], after=(m,) + tuple(after))
            m1 = copy(chunk(c)[:, 1, :], PS[:, banks[1], :], after=(m,) + tuple(after))
            return (m0, m1)

        PAIRS = [(4, 5), (0, 1)]

        def gates_stream(n, free, bias, out_):
            for c in range(n):
                banks = PAIRS[c % 2]
                for n, m in enumerate(project(banks, KD, after=free[c % 2])):
                    if n + 1 < KD // 2:
                        yield
                cols = slice(c * W, (c + 1) * W)
                for t in (1, 0):
                    m1 = tt(out_[:, t, cols], PS[:, banks[t], :], out_[:, 0, cols], ALU.add, after=(m,) + tuple(bias))
                    act(out_[:, t, cols], out_[:, t, cols], ACT.Sigmoid, after=(m1,))
                free[c % 2] = (m1,)
                yield

        def interleave(main, filler):
            for _ in main:
                next(filler, None)
            return filler

        def branch_turn(c, k0):
            return turn_split(lambda t, k: chunk(c)[:, t, k * P:(k + 1) * P], 4, a_hi[:, k0:k0 + 4, :],
                              a_lo[:, k0:k0 + 4, :], [2, 3], after=(mark("act"), mark("dve")))

        def branch(b, ready, k0, free, first, acc, gate):
            for nh in range(D // W):
                banks = PAIRS[nh % 2]
                m = finish(project(banks, 4, after=tuple(free[nh % 2]) + tuple(ready), k0=k0))
                cols = slice(nh * W, (nh + 1) * W)
                for t in range(NT):
                    g = gate[:, t, b * D + nh * W:b * D + (nh + 1) * W]
                    m1 = tt(acc[:, t, cols] if first else g, PS[:, banks[t], :], g, ALU.mult, after=(m,))
                    if not first:
                        tt(acc[:, t, cols], acc[:, t, cols], g, ALU.add)
                free[nh % 2] = (m1,)

        def gla(sm):
            E = [S[:, 1024 * i:1024 * (i + 1)] for i in range(4)]
            Bc, E1, E2, E3 = E
            h4 = lambda a: a.rearrange("p (h t) -> p h t", h=GH)
            m = sm
            for h in range(GH):
                m = mm(PS[:, 6 + h // 2, (h % 2) * T:(h % 2 + 1) * T], lay("aup")[0:16, h * P:(h + 1) * P],
                       fix[0:16, 0:T], after=(sm,), signal=(h % 2 == 1))
                if h % 2:
                    for j in (h - 1, h):
                        ts(h4(Bc)[:, j, :], PS[:, 6 + j // 2, (j % 2) * T:(j % 2 + 1) * T],
                           lay("ab")[:, j:j + 1], None, ALU.add, after=(m,))
            m = stt(E1, Bc, -1.0, Bc, ALU.mult, ALU.max)
            m = act(E1, E1, ACT.Exp, after=(m,), scale=-1.0)
            m = act(E1, E1, ACT.Ln, bias=1.0)
            stt(Bc, Bc, 0.0, E1, ALU.min, ALU.subtract, after=(m,))
            yield
            for h in range(GH):
                step("dve", lambda e, h=h: e.tensor_tensor_scan(h4(E1)[:, h, :], const("reset"), h4(Bc)[:, h, :], 0.0,
                                                                ALU.mult, ALU.add))
            b3 = E1.rearrange("p (c l) -> p c l", l=L)
            m = tt(E3.rearrange("p (c l) -> p c l", l=L), b3[:, :, L - 1:L].broadcast_to([P, GH * NC, L]), b3,
                   ALU.subtract)
            dec = fix[:, 256:256 + GH * NC]
            act(dec.unsqueeze(2), b3[:, :, L - 1:L], ACT.Exp, after=(m,), scale=1.0 / 16)
            act(E3, E3, ACT.Exp, scale=1.0 / 16)
            act(E2, E1, ACT.Exp, scale=-1.0 / 16)
            me = act(E1, E1, ACT.Exp, scale=1.0 / 16)
            yield
            m = None
            for src, n0 in ((0, 0), (1, 1)):
                v = chunk(src)
                for b in range(2):
                    bank = 6 + b
                    for j in range(2):
                        for t in range(NT):
                            mt = turn(PS[:, bank, (2 * j + t) * P:(2 * j + t + 1) * P],
                                      v[:, t, (2 * b + j) * P:(2 * b + j + 1) * P],
                                      (mark("dve"), mark("act")), signal=(j == 1 and t == 1))
                    cols = slice(b * W, (b + 1) * W)
                    ps = PS[:, bank, :]
                    if src == 0:
                        m = stt(E1[:, cols], ps, float(GD) ** -0.5, E1[:, cols], ALU.mult, ALU.mult, after=(mt, me))
                    else:
                        tt(E2[:, cols], ps, E2[:, cols], ALU.mult, after=(mt, me))
                        m = tt(E3[:, cols], ps, E3[:, cols], ALU.mult)
                    yield
            ke = chunk(1)
            for t in range(NT):
                for h in range(GH):
                    mt = turn(PS[:, 6 + t, h * P:(h + 1) * P], h4(E3)[:, h, t * P:(t + 1) * P], (m,), signal=(h == GH - 1))
                m2 = act(ke[:, t, :], PS[:, 6 + t, :], after=(mt,))
            yield
            at = Bc.rearrange("p (t w) -> p t w", t=NT)
            m = fill(Bc, 0.0)
            for t in range(NT):
                for h in range(GH):
                    tok = slice(t * P, (t + 1) * P)
                    mt = mm(PS[:, 2 + t, h * P:(h + 1) * P], h4(E2)[:, h, tok], h4(E1)[:, h, tok],
                            after=(m, mark("act")), signal=(h == GH - 1))
                fill(st[:, 200:201], 0.0, after=(mt,))
                step("dve", lambda e, t=t: e.copy_predicated(
                    at[:, t, :].rearrange("p (h i) -> p h i", h=GH),
                    gm8[:, :].unsqueeze(1).broadcast_to([P, GH, P]),
                    PS[:, 2 + t, :].rearrange("p (h i) -> p h i", h=GH)), alone=True)
                yield
            q0 = proj(0)
            Sx = [q0[:, 0:W], q0[:, W:2 * W], S[:, 4096:4096 + W]]
            v = chunk(2)
            mS = None
            for cix in range(NC - 1):
                t, o = cix // 2, (cix % 2) * L
                bank = 6 + cix % 2
                for h in range(GH):
                    mt = mm(PS[:, bank, h * P:(h + 1) * P], ke[o:o + L, t, h * P:(h + 1) * P],
                            v[o:o + L, t, h * P:(h + 1) * P], after=(m2, mS, mark("dve")), signal=(h == GH - 1))
                if cix == 0:
                    mS = copy(Sx[0], PS[:, bank, :], after=(mt,))
                else:
                    for h in range(GH):
                        hc = slice(h * P, (h + 1) * P)
                        mS = stt(Sx[cix][:, hc], Sx[cix - 1][:, hc], dec[:, h * NC + cix:h * NC + cix + 1],
                                 PS[:, bank, hc], ALU.mult, ALU.add, after=(mt,))
                yield
            tmp = S[:, 4608:4608 + W]
            y = chunk(3)
            for t in range(NT):
                bank = 2 + t
                for h in range(GH):
                    hc = slice(h * P, (h + 1) * P)
                    parts = [(slice(0, P), at[:, t, hc], v[:, t, hc])]
                    for half in range(2):
                        cix = 2 * t + half
                        if cix:
                            parts.append((slice(half * L, half * L + L), h4(E1)[:, h, cix * L:(cix + 1) * L], Sx[cix - 1][:, hc]))
                    for n, (rows, a, b) in enumerate(parts):
                        mt = mm(PS[rows, bank, hc], a, b, start=(n == 0), stop=(n == len(parts) - 1),
                                after=(mS,), signal=(h == GH - 1 and n == len(parts) - 1))
                copy(S[:, 5120:5120 + W], PS[:, bank, :], after=(mt,))
                yield
                ov = S[:, 5120:5120 + W].rearrange("p (h d) -> p h d", h=GH)
                head_norm(ov, GH, GD, tmp.rearrange("p (h d) -> p h d", h=GH), lay("gn"))
                m = act(tmp, y[:, t, :], ACT.Silu, after=(mark("dve"),))
                tt(y[:, t, :], S[:, 5120:5120 + W], tmp, ALU.mult, after=(m,))
                yield

        def rope_heads(v, t, after=()):
            x = v[:, t, :].rearrange("p (h s d) -> p h s d", h=H8, s=2)
            A = S[:, 0:W].rearrange("p (h s d) -> p h s d", h=H8, s=2)
            B = S[:, W:2 * W].rearrange("p (h s d) -> p h s d", h=H8, s=2)
            cos, sin = (const(n)[:, t * 32:(t + 1) * 32] for n in ("cos", "sin"))
            b3 = lambda a: a.unsqueeze(1).broadcast_to([P, H8, 32])
            for s in range(2):
                tt(A[:, :, s, :], x[:, :, s, :], b3(cos), ALU.mult)
                tt(B[:, :, s, :], x[:, :, 1 - s, :], b3(sin), ALU.mult)
            tt(x[:, :, 0, :], A[:, :, 0, :], B[:, :, 0, :], ALU.subtract)
            return tt(x[:, :, 1, :], A[:, :, 1, :], B[:, :, 1, :], ALU.add)

        def moba():
            TQ = S[:, 2560:2560 + 1024].rearrange("p (g t) -> p g t", g=4)
            TK = S[:, 3584:3584 + 1024].rearrange("p (g t) -> p g t", g=4)
            for v, gain, dst in ((chunk(4), lay("qn"), TQ), (chunk(5), lay("kn"), TK)):
                for t in range(NT):
                    head_norm(v[:, t, :].rearrange("p (h d) -> p h d", h=H8), H8, HD,
                              S[:, 0:W].rearrange("p (h d) -> p h d", h=H8), gain, after=(mark("pe"),))
                    yield
                    m = rope_heads(v, t)
                    yield
                for b in range(2):
                    for j in range(2):
                        for t in range(NT):
                            g = 2 * b + j
                            mt = turn(PS[:, 6 + b, (2 * j + t) * P:(2 * j + t + 1) * P], v[:, t, g * P:(g + 1) * P],
                                      (m, mark("act")), signal=(j == 1 and t == 1))
                    ma = act(dst[:, 2 * b:2 * b + 2, :], PS[:, 6 + b, :].rearrange("p (g t) -> p g t", g=2), after=(mt,))
                    yield
            rows = lambda h: slice((h % 2) * HD, (h % 2 + 1) * HD)
            yield from softmax_heads(
                H8, lambda h, t: TQ[rows(h), h // 2, t * P:(t + 1) * P], lambda h, n: TK[rows(h), h // 2, 0:n],
                lambda h, t: chunk(6)[:, t, h * HD:(h + 1) * HD],
                lambda t: chunk(4)[:, t, :].rearrange("p (h d) -> p h d", h=H8), float(HD) ** -0.5, True,
                (2, 3, 6, 7), after=(ma, mark("dve")))

        def mlstm():
            NB = 4 * 260
            pad = S[:, 0:NB].rearrange("p (g t) -> p g t", g=4)
            qk = S[:, 1040:1040 + 1024].rearrange("p (g t) -> p g t", g=4)
            vx = S[:, 2064:2064 + NT * MH * 129].rearrange("p (t h v) -> p t h v", t=NT, h=MH)
            kw = S[:, 3096:3096 + NT * 256].rearrange("p (t c) -> p t c", t=NT)
            iwb = S[:, 3608:3608 + 2 * 260].rearrange("p (g t) -> p g t", g=2)
            Sx = [S[:, 4128 + 258 * i:4128 + 258 * (i + 1)].rearrange("p (g v) -> p g v", g=2) for i in range(3)]
            m = fill(pad[:, :, 0:3], 0.0, after=(mark("pe"), mark("act")))
            v = chunk(7)
            for b in range(2):
                for j in range(2):
                    for t in range(NT):
                        g = 2 * b + j
                        mt = turn(PS[:, 6 + b, (2 * j + t) * P:(2 * j + t + 1) * P], v[:, t, g * P:(g + 1) * P],
                                  (m, mark("act")), signal=(j == 1 and t == 1))
                ma = act(pad[:, 2 * b:2 * b + 2, 3:259], PS[:, 6 + b, :].rearrange("p (g t) -> p g t", g=2), after=(mt,))
            yield
            conv = lay("conv").rearrange("p (g j) -> p g j", g=4)
            for g in range(4):
                ts(qk[:, g, :], pad[:, g, 0:T], conv[:, g, 0:1], None, ALU.mult, after=(ma,))
                for j in range(1, 4):
                    stt(qk[:, g, :], pad[:, g, j:j + T], conv[:, g, j:j + 1], qk[:, g, :], ALU.mult, ALU.add)
                if g >= 2:
                    ts(qk[:, g, :], qk[:, g, :], float(MK) ** -0.5, None, ALU.mult)
                yield
            rows = proj(5, 2)[0:MH, :]
            iwa = rows[:, 0:260]
            b_, g_, u_, w2, emr, tmp = (rows[:, 264 + i * T:264 + (i + 1) * T] for i in range(6))
            lf = fix[0:MH, 288:288 + T]
            ts(g_, li_row[:, :], lay("ifb")[0:MH, 0:1], None, ALU.add, after=(mark("pe"),))
            ts(b_, lf, lay("ifb")[0:MH, 1:2], None, ALU.add)
            m = stt(tmp, b_, -1.0, b_, ALU.mult, ALU.max)
            act(tmp, tmp, ACT.Exp, after=(m,), scale=-1.0)
            m = act(tmp, tmp, ACT.Ln, bias=1.0)
            stt(tmp, b_, 0.0, tmp, ALU.min, ALU.subtract, after=(m,))
            step("dve", lambda e: e.tensor_tensor_scan(b_, const("reset")[0:MH, :], tmp, 0.0, ALU.mult, ALU.add))
            tt(g_, g_, b_, ALU.subtract)
            step("dve", lambda e: e.tensor_tensor_scan(u_, const("resetneg")[0:MH, :], g_, 0.0, ALU.add, ALU.max))
            yield
            c4 = lambda a: a.rearrange("p (c l) -> p c l", l=L)
            bl, ml = st[0:MH, 112:116], st[0:MH, 116:120]
            M, Mp = st[0:MH, 121:125], st[0:MH, 120:124]
            fill(st[0:MH, 120:121], 0.0)
            copy(bl.unsqueeze(2), c4(b_)[:, :, L - 1:L])
            tt(ml.unsqueeze(2), c4(b_)[:, :, L - 1:L], c4(u_)[:, :, L - 1:L], ALU.add)
            step("dve", lambda e: e.tensor_tensor_scan(M, bl, ml, 0.0, ALU.add, ALU.max))
            bc = lambda a: a.unsqueeze(2).broadcast_to([MH, NC, L])
            tt(c4(u_), c4(u_), bc(Mp), ALU.max)
            tt(st[0:MH, 128:132], bl, M, ALU.subtract)
            m = tt(c4(w2), c4(g_), bc(st[0:MH, 128:132]), ALU.add)
            act(w2, w2, ACT.Exp, after=(m,))
            tt(st[0:MH, 132:136], st[0:MH, 128:132], Mp, ALU.add)
            tt(c4(iwa[:, 0:T]), bc(Mp), c4(u_), ALU.subtract)
            m = copy(iwa[:, T:T + 4], st[0:MH, 132:136])
            act(iwa, iwa, ACT.Exp, after=(m,))
            m = tt(emr, b_, u_, ALU.add)
            ma = act(emr, emr, ACT.Exp, after=(m,), scale=-1.0)
            yield
            pick = lambda h, n: ident[0:MH, h:h + 1].broadcast_to([MH, n])
            for pr in range(2):
                for j in range(2):
                    mt = mm(PS[j * L:(j + 1) * L, 6 + pr, 0:260], pick(2 * pr + j, L), iwa, after=(ma, mark("dve")), signal=(j == 1))
                ma2 = act(iwb[:, pr, :], PS[:, 6 + pr, 0:260], after=(mt,))
            yield
            cols = st[:, 144:144 + 24].rearrange("p (w t h) -> p w t h", w=3, t=NT)
            for wi, a in enumerate((g_, w2, emr)):
                for t in range(NT):
                    mt = mm(PS[:, 6, (wi * NT + t) * MH:(wi * NT + t + 1) * MH], a[:, t * P:(t + 1) * P],
                            ident[0:MH, 0:MH], after=(ma2, mark("dve")), signal=(wi == 2 and t == 1))
            mc = copy(st[:, 144:168], PS[:, 6, 0:24], after=(mt,))
            for pr in range(2):
                for t in range(NT):
                    mt = turn(PS[:, 7, (t * 2 + pr) * P:(t * 2 + pr + 1) * P], qk[:, 2 + pr, t * P:(t + 1) * P],
                              (ma2, mark("dve")), signal=(pr == 1 and t == 1))
            for t in range(NT):
                mk = tt(kw[:, t, :].rearrange("p (h d) -> p h d", h=MH),
                        PS[:, 7, t * 256:(t + 1) * 256].rearrange("p (h d) -> p h d", h=MH),
                        cols[:, 1, t, :].unsqueeze(2).broadcast_to([P, MH, MK]), ALU.mult, after=(mt,))
            fill(vx[:, :, :, MV:MV + 1], 1.0)
            for t in range(NT):
                mv = copy(vx[:, t, :, 0:MV], chunk(8)[:, t, :].rearrange("p (h v) -> p h v", h=MH))
            yield
            mS = None
            for cix in range(NC - 1):
                t, o = cix // 2, (cix % 2) * L
                bank = 6 + cix % 2
                mm(PS[:, bank, 0:1], kw[o:o + L, t, 0:P], vx[o:o + L, t, 0, 0:1], after=(mv, mS, mark("act")), signal=False)
                for h in range(MH):
                    pr, r = h // 2, (h % 2) * L
                    mt = mm(PS[r:r + L, bank, pr * 129:(pr + 1) * 129], kw[o:o + L, t, h * MK:(h + 1) * MK],
                            vx[o:o + L, t, h, :], signal=(h == MH - 1))
                if cix == 0:
                    mS = copy(Sx[0].rearrange("p g v -> p (g v)"), PS[:, bank, 0:258], after=(mt,))
                else:
                    for pr in range(2):
                        mS = stt(Sx[cix][:, pr, :], Sx[cix - 1][:, pr, :], iwb[:, pr, T + cix:T + cix + 1],
                                 PS[:, bank, pr * 129:(pr + 1) * 129], ALU.mult, ALU.add, after=(mt,))
                yield
            q2 = S[:, 0:512].rearrange("p (g t) -> p g t", g=2)
            mq = tt(q2, qk[:, 0:2, :], iwb[:, :, 0:T], ALU.mult)
            y = chunk(9)
            hp = lambda h: slice((h % 2) * L, (h % 2 + 1) * L)
            for t in range(NT):
                tok = slice(t * P, (t + 1) * P)
                for h in range(MH):
                    mt = mm(PS[:, 6, h * P:(h + 1) * P], pick(h, P), u_[:, tok], after=(mS, mark("dve"), mark("act")),
                            signal=(h == MH - 1))
                dm = proj(7)[:, 0:W].rearrange("p (h i) -> p h i", h=MH)
                tt(dm, cols[:, 0, t, :].unsqueeze(2).broadcast_to([P, MH, P]),
                   PS[:, 6, :].rearrange("p (h i) -> p h i", h=MH), ALU.subtract, after=(mt,))
                m = stt(dm, dm, 0.0, const("lmask").unsqueeze(1).broadcast_to([P, MH, P]), ALU.min, ALU.add)
                m = act(dm, dm, ACT.Exp, after=(m,))
                for h in range(MH):
                    mt = mm(PS[:, 6 + h % 2, (h // 2) * P:(h // 2 + 1) * P], qk[hp(h), 2 + h // 2, tok],
                            qk[hp(h), h // 2, tok], after=(mark("dve"),), signal=(h == MH - 1))
                yield
                pairs = dm.rearrange("p (g s) i -> p g s i", s=2)
                for s in range(2):
                    sc = PS[:, 6 + s, 0:2 * P].rearrange("p (g i) -> p g i", g=2)
                    md = tt(pairs[:, :, s, :], sc, pairs[:, :, s, :], ALU.mult, after=(mt, m))
                m = md
                for h in range(MH):
                    bank, o = 2 + h % 2, (h // 2) * T
                    parts = [(slice(0, P), dm[:, h, :], vx[:, t, h, :])]
                    for half in range(2):
                        cix = 2 * t + half
                        if cix:
                            parts.append((slice(half * L, half * L + L), q2[hp(h), h // 2, cix * L:(cix + 1) * L],
                                          Sx[cix - 1][hp(h), h // 2, :]))
                    for n, (rows, a, b) in enumerate(parts):
                        mt = mm(PS[rows, bank, o:o + 129], a, b, start=(n == 0), stop=(n == len(parts) - 1),
                                after=(m, mq), signal=(h == MH - 1 and n == len(parts) - 1))
                yield
                o2 = PS[:, 2:4, :].rearrange("p b (j v) -> p j b v", j=2)
                den = st[:, 176:180]
                copy(den.rearrange("p (j b o) -> p j b o", j=2, o=1), o2[:, :, :, MV:MV + 1], after=(mt,))
                stt(den, den, -1.0, den, ALU.mult, ALU.max)
                tt(den, den, cols[:, 2, t, :], ALU.max)
                recip(den, den)
                hid = S[:, 512:1024].rearrange("p (h v) -> p h v", h=MH)
                for j in range(2):
                    tt(hid[:, 2 * j:2 * j + 2, :], o2[:, j, :, 0:MV],
                       den[:, 2 * j:2 * j + 2].unsqueeze(2).broadcast_to([P, 2, MV]), ALU.mult)
                head_norm(hid, MH, MV, dm, lay("mn"))
                m = act(y[:, t, :], y[:, t, :], ACT.Sigmoid)
                tt(y[:, t, :], S[:, 512:1024], y[:, t, :], ALU.mult, after=(m,))
                yield

        def narrow(name_cols, n, dst_bank, after=()):
            src, total = name_cols, KD * n
            m1 = act(s_hi[:, 0:total], src, after=after)
            m2 = tt(s_lo[:, 0:total], src, r32(s_hi[:, 0:total]), ALU.subtract, after=(m1,) + tuple(after))
            for t in range(NT):
                tok = slice(t * P, (t + 1) * P)
                todo = [(a, w, k) for k in range(KD) for a in (a_hi, a_lo) for w in (s_hi, s_lo)]
                for i, (a, w, k) in enumerate(todo):
                    m = mm(PS[:, dst_bank, t * 64:t * 64 + n], a[:, k, tok], w[:, k * n:(k + 1) * n],
                           start=(i == 0), stop=(i == len(todo) - 1), after=(m1, m2), signal=(i == len(todo) - 1))
            return m

        def index(loop, name, scale=1, offset=0):
            return (loop if isinstance(loop, int) else loop.var[name]) * scale + offset

        def ada_step(lp, cl):
            stg = proj(4, 4)
            acc = proj(8)[:, 0:W]
            landed = [step("act", lambda e, u=u: e.dma_start(
                stg[:, u * UNIT:(u + 1) * UNIT],
                wada[bass.ds((index(lp, "act", FF_CHUNKS) + index(cl, "act")) * 2 + u, 1), :, :]
                .rearrange("o p n -> p (o n)")), (mark("dve"), mark("pe")), sem=f"ld_ada{u}", by=16) for u in range(2)]
            yield
            for k in range(KD):
                src = stg[:, k * W:(k + 1) * W]
                if k == 0:
                    ts(acc, src, cact[:, 0:1], None, ALU.mult, after=(landed[0], mark("act")))
                else:
                    m = stt(acc, src, cact[:, k:k + 1], acc, ALU.mult, ALU.add, after=(landed[k // 4],))
                if k % 2:
                    yield
            for j in range(4):
                mm(PS[:, 6, j:j + 1], acc[:, j * P:(j + 1) * P], ones[:, 0:1], after=(m, mark("act")), signal=False)
            summed = mm(PS[:, 7, :], ones[:, :], acc)
            act_out = lambda e: ada_cols[:, bass.ds(index(lp, "act"), 1), bass.ds(index(cl, "act", 4), 4)]
            step("act", lambda e: e.activation(act_out(e), PS[:, 6, 0:4].unsqueeze(1), ACT.Copy), (summed,))
            step("act", lambda e: e.activation(ada_rows[:, bass.ds(index(cl, "act"), 1), :], PS[:, 7, :].unsqueeze(1),
                                               ACT.Copy))
            yield

        relu = proj(0).rearrange("p (t w) -> p t w", t=NT)
        hid = proj(1).rearrange("p (t w) -> p t w", t=NT)

        def up(after=()):
            return finish(project((4, 5), KD, after=after))

        def down(nk, ready, last, between=iter(())):
            accs = [[PS[:, 2 * t, :], PS[:, 2 * t + 1, :]] for t in range(NT)]
            for k in range(nk):
                slot, ok = take_half()
                m = product(accs, h_hi, h_lo, k, slot, [(0, W), (W, D)], False, last and k == nk - 1,
                            tuple(ok) + tuple(ready), True)
                next(between, None)
            return m

        def clear_sums(pad=False):
            for b in range(4):
                if pad:
                    _, ok = take_half()
                    used_half(lambda e, b=b: e.matmul(PS[:, b, :], zcol[0:1, :], zrow[0:1, :], start=True, stop=False,
                                                      skip_group_check=True), ok + (mark("act"), mark("dve")))
                    continue
                mm(PS[:, b, :], zcol[0:1, :], zrow[0:1, :], start=True, stop=False, signal=(b == 3),
                   after=(mark("act"), mark("dve")))

        def ff_hidden(m):
            for t in range(NT):
                m1 = act(relu[:, t, :], PS[:, 4 + t, :], ACT.Relu, after=(m, mark("dve")))
                tt(hid[:, t, :], relu[:, t, :], relu[:, t, :], ALU.mult, after=(m1,))

        def hid_turn(width):
            v = PR[:, NT * W:NT * W + NT * width].rearrange("p (t w) -> p t w", t=NT)
            return turn_split(lambda t, k: v[:, t, k * P:(k + 1) * P], width // P, h_hi, h_lo, [6, 7],
                              after=(mark("dve"), mark("act")))

        def add_to_x(m, gate_rows=None):
            for t in range(NT):
                for n in range(2):
                    cols = slice(n * W, (n + 1) * W)
                    if gate_rows is None:
                        last = tt(X[:, t, cols], PS[:, 2 * t + n, :], X[:, t, cols], ALU.add, after=(m,))
                    else:
                        tmp = S[:, 0:W]
                        tt(tmp, PS[:, 2 * t + n, :], gate_rows[:, n, :], ALU.mult, after=(m,))
                        last = tt(X[:, t, cols], tmp, X[:, t, cols], ALU.add)
            return last

        def mixed_out(mix, free, gate_rows=None):
            mT = turn_split(lambda t, k: mix[:, t, k * P:(k + 1) * P], KD, a_hi, a_lo, [2, 3, 6, 7],
                            after=(mark("dve"), mark("act")))
            for nh in range(D // W):
                banks = PAIRS[nh % 2]
                m = finish(project(banks, KD, after=tuple(free[nh % 2]) + tuple(mT)))
                for t in range(NT):
                    cols = slice(nh * W, (nh + 1) * W)
                    if gate_rows is None:
                        m1 = tt(X[:, t, cols], PS[:, banks[t], :], X[:, t, cols], ALU.add, after=(m,))
                    else:
                        tt(S[:, 0:W], PS[:, banks[t], :], gate_rows[:, nh, :], ALU.mult, after=(m,))
                        m1 = tt(X[:, t, cols], S[:, 0:W], X[:, t, cols], ALU.add)
            return m1

        def until(stream, progress, chunks):
            while progress[0] < chunks:
                next(stream)

        def layer(lp):
            small = step("act", lambda e: e.dma_start(
                lsm[:, 0:LAYER_N], layer_small[bass.ds(index(lp, "act"), 1), :, :].rearrange("o p n -> p (o n)")),
                (mark("pe"), mark("dve"), mark("pool")), sem="ld_layer", by=16)
            bias = step("act", lambda e: e.dma_start(
                G[:, 0, :], gate_b[bass.ds(index(lp, "act"), 1), :].broadcast_to([P, 3 * D])), sem="ld_gate", by=16)
            xT = norm_turn(lay("g1"), after=(small, loaded_x, loaded_const, mark("dve")))
            m = narrow(lay("wsm"), 24, 6, after=(small,))
            narrow_out = S[:, 0:48].rearrange("p (t n) -> p t n", t=NT)
            m = copy(narrow_out, PS[:, 6, 0:P].rearrange("p (t n) -> p t n", t=NT)[:, :, 0:24], after=(m,))
            for t in range(NT):
                turn(PS[0:16, 7, t * P:(t + 1) * P], narrow_out[:, t, 0:16], (m,), signal=False)
                turn(PS[0:MH, 7, T + t * P:T + (t + 1) * P], narrow_out[:, t, 16:20], signal=False)
                mt = turn(PS[0:MH, 6, T + t * P:T + (t + 1) * P], narrow_out[:, t, 20:24])
            copy(fix[0:MH, 288:288 + T], PS[0:MH, 6, T:2 * T], after=(mt,))
            copy(li_row[:, :], PS[0:MH, 7, T:2 * T])
            ga = copy(fix[0:16, 0:T], PS[0:16, 7, 0:T])
            free = [tuple(xT), tuple(xT)]
            progress = [0]

            def projections():
                for cix in range(10):
                    for m in project(PAIRS[cix % 2], KD, after=free[cix % 2] + tuple(xT)):
                        yield
                    free[cix % 2] = evacuate(cix, PAIRS[cix % 2], m)
                    progress[0] = cix + 1
                yield from gates_stream(6, free, (bias,), G)

            stream = projections()
            until(stream, progress, 4)
            interleave(gla(ga), stream)
            until(stream, progress, 7)
            interleave(moba(), stream)
            until(stream, progress, 10)
            interleave(mlstm(), stream)
            for _ in stream:
                pass
            mix = PR[:, 0:NT * D].rearrange("p (t d) -> p t d", t=NT)
            turns = {}
            turns[0] = branch_turn(3, 0)
            turns[1] = branch_turn(4, 4)
            branch(0, turns[0], 0, free, True, mix, G)
            turns[2] = branch_turn(9, 0)
            branch(1, turns[1], 4, free, False, mix, G)
            branch(2, turns[2], 0, free, False, mix, G)
            mixed_out(mix, free)
            norm_turn(lay("g2"), after=(mark("dve"),))

            m = up((mark("dve"), mark("act")))
            ff_hidden(m)
            hid_turn(W)
            clear_sums(pad=True)

            def ff_step(cl):
                ready = (mark("act"), mark("dve"))
                ada = ada_step(lp, cl)
                next(ada)
                ff_hidden(up(ready))
                down(W // P, ready, False, ada)
                for _ in ada:
                    pass
                hid_turn(W)

            stream_loop(FF_CHUNKS - 1, ff_step)
            ada = ada_step(lp, FF_CHUNKS - 1)
            next(ada)
            m = down(W // P, (mark("act"), mark("dve")), True, ada)
            for _ in ada:
                pass
            add_to_x(m)

        stream_loop(DEPTH, layer)

        def fourier(ld):
            ft = S[:, 2048:4096].rearrange("p (g n) -> p g n", g=4)
            u = chunk(5)
            C = dftc[:, 0:1024].rearrange("p (k n) -> p k n", k=NT)
            for g in range(4):
                for k in range(NT):
                    mt = mm(PS[:, 2 + g % 2, :], u[:, k, g * P:(g + 1) * P], C[:, k, :], start=(k == 0), stop=(k == 1),
                            after=(ld, mark("act"), mark("dve")), signal=(k == 1))
                m = act(ft[:, g, :], PS[:, 2 + g % 2, :], after=(mt,))
                yield
            fT = proj(5).rearrange("p (g t) -> p g t", g=4)
            for b in range(2):
                for j in range(2):
                    g = 2 * b + j
                    for s in range(2):
                        mt = mm(PS[:, 6 + b, j * T:(j + 1) * T], dftc[:, 1024 + s * P:1024 + (s + 1) * P],
                                ft[:, g, s * T:(s + 1) * T], start=(s == 0), stop=(s == 1), after=(m, mark("dve")),
                                signal=(s == 1))
                mf = act(fT[:, 2 * b:2 * b + 2, :], PS[:, 6 + b, :].rearrange("p (j t) -> p j t", j=2), after=(mt,))
                yield

        def angles(ld):
            pf, ang, n, r = (Gf[:, 5120 + 64 * i:5120 + 64 * (i + 1)] for i in range(4))
            twopi = 2 * np.pi
            c1 = float(np.float32(6.28125))
            c2 = float(np.float32(np.float32((twopi - c1) * 2 ** 24) // 2 ** 12 * 2 ** 12 / 2 ** 24))
            c3 = float(twopi - c1 - c2)
            magic = 1.5 * 2 ** 23
            lim = 3.1415925
            copy(pf[:, 0:NT], posi[:, :], after=(ld,))
            for t in range(NT):
                ts(ang[:, t * 16:(t + 1) * 16], const("invf"), pf[:, t:t + 1], None, ALU.mult)
            out_ = []
            for i, (quarter, shift) in enumerate(((0.25, np.pi / 2), (0.0, 0.0))):
                a, nn, rr = ang[:, 0:32], n[:, 0:32], r[:, 32 * i:32 * i + 32]
                ts(nn, a, 1 / twopi, quarter, ALU.mult, ALU.add)
                ts(nn, nn, magic, None, ALU.add)
                ts(nn, nn, -magic, None, ALU.add)
                stt(rr, nn, -c1, a, ALU.mult, ALU.add)
                stt(rr, nn, -c2, rr, ALU.mult, ALU.add)
                stt(rr, nn, -c3, rr, ALU.mult, ALU.add)
                ts(rr, rr, float(shift), lim, ALU.add, ALU.min)
                m = ts(rr, rr, -lim, None, ALU.max)
                m = act(rope2[:, i, :], rr, ACT.Sin, after=(m,))
            return m

        def rotate(x, n, cs, after=()):
            cos, sin = (a.unsqueeze(1).broadcast_to([P, n, 16]) for a in cs)
            w4 = [Gf[:, 5376 + 128 * i:5376 + 128 * i + 16 * n].rearrange("p (n d) -> p n d", n=n) for i in range(4)]
            x1, x2 = x[:, :, 0:16], x[:, :, 16:32]
            tt(w4[0], x1, cos, ALU.mult, after=after)
            tt(w4[1], x2, sin, ALU.mult)
            tt(w4[2], x2, cos, ALU.mult)
            tt(w4[3], x1, sin, ALU.mult)
            tt(x1, w4[0], w4[1], ALU.subtract)
            return tt(x2, w4[2], w4[3], ALU.add)

        posi = sb("posi", [P, NT], I32)
        rope2 = sb("rope2", [P, 2, 32])
        cond = sb("cond", [P, 32])
        dftc = S[:, 4096:4096 + 1280]
        mark_all = lambda: (mark("pe"), mark("act"), mark("dve"), mark("pool"))

        small = step("act", lambda e: e.dma_start(lsm[:, 0:B2_N], b2_small), mark_all(), sem="ld_b2", by=16)
        step("act", lambda e: e.dma_start(posi[:, :], pos), sem="ld_b2", by=16)
        ld_pos = mark("ld_b2")
        gates2 = PR[:, 0:NT * 2 * D].rearrange("p (t n) -> p t n", t=NT)
        bias2 = step("act", lambda e: e.dma_start(gates2[:, 0, :], rows2[0:1, 5 * D:7 * D].broadcast_to([P, 2 * D])),
                     sem="ld_gate", by=16)
        ld_rows = step("act", lambda e: e.dma_start(PR[:, 6144:6144 + 4 * D], rows2[0:1, 0:4 * D].broadcast_to([P, 4 * D])),
                       sem="ld_rows", by=16)
        ld_dft = step("act", lambda e: e.dma_start(dftc, dft), sem="ld_dft", by=16)
        tt(cond[:, 0:32], ada_cols[:, 0, :], b2("bcols"), ALU.add, after=(ld_pos, mark("act")))
        for at_, gain in ((8, "gmix"), (24, "gffn")):
            ts(cond[:, at_:at_ + 8], cond[:, at_:at_ + 8], 1.0, None, ALU.add)
            tt(cond[:, at_:at_ + 8], cond[:, at_:at_ + 8], b2(gain), ALU.mult)
        rows_flat = ada_rows.rearrange("p c w -> p (c w)")
        tt(rows_flat, rows_flat, PR[:, 6144:6144 + 4 * D], ALU.add, after=(ld_rows, mark("act")))
        uT = norm_turn(cond[:, 8:16], cond[:, 0:8], after=(mark("dve"),))
        m = narrow(b2("wkr"), 32, 6)
        kr = fix[:, 0:64].rearrange("p (t n) -> p t n", t=NT)
        copy(kr, PS[:, 6, 0:P].rearrange("p (t n) -> p t n", t=NT)[:, :, 0:32], after=(m,))

        free = [tuple(uT), tuple(uT)]
        for cix in (4, 5):
            m = finish(project(PAIRS[cix % 2], KD, after=free[cix % 2]))
            free[cix % 2] = evacuate(cix, PAIRS[cix % 2], m)
        stream = gates_stream(4, free, (bias2,), gates2)

        def latents():
            for t in range(NT):
                v = chunk(4)[:, t, :].rearrange("p (n d) -> p n d", n=2)
                tmp = S[:, 0:W].rearrange("p (n d) -> p n d", n=2)
                tt(tmp, v, v, ALU.mult, after=(mark("act"),))
                reduce(st[:, 16:18], tmp, ALU.add)
                m = rsqrt_mean(st[:, 32:34], st[:, 16:18], 256, 2)
                tt(v, v, st[:, 32:34].unsqueeze(2).broadcast_to([P, 2, 256]), ALU.mult, after=(m,))
                yield
            angles(ld_pos)
            yield
            turn_split(lambda t, k: chunk(4)[:, t, k * P:(k + 1) * P], 4, h_hi, h_lo, [6, 7],
                       after=(mark("dve"), mark("act")), scale=lsm[:, B2_AT["gq"][0]:B2_AT["gkv"][1]])
            yield

        lat = latents()
        done_lat = [False]
        for n in range(8):
            next(stream)
            if n % 2 == 1:
                next(lat, None)
        for _ in lat:
            pass
        Q = PR[:, 6144:6144 + NT * 768].rearrange("p (t n) -> p t n", t=NT)
        K = PR[:, 7680:7680 + NT * 768].rearrange("p (t n) -> p t n", t=NT)
        V = chunk(9)
        latent_ready = (mark("act"), mark("dve"))
        for half in range(4):
            banks = (PAIRS[0], PAIRS[1], (2, 3), (6, 7))[half]
            width, k0 = (4 * QK2, 0) if half < 2 else (W, 2)
            slot, ok = take_half()
            for k in range(2):
                m = product([[PS[:, banks[t], 0:width]] for t in range(NT)], h_hi, h_lo, k0 + k, slot,
                            [(k * width, (k + 1) * width)], k == 0, k == 1, tuple(ok) + latent_ready, k == 1)
            for t in range(NT):
                src = PS[:, banks[t], 0:width]
                if half < 2:
                    dst = Q[:, t, half * width:(half + 1) * width]
                elif half == 2:
                    dst = K[:, t, :].rearrange("p (h d) -> p h d", h=H8)[:, :, 0:HD]
                    src = src.rearrange("p (h d) -> p h d", h=H8)
                else:
                    dst = V[:, t, :]
                if t:
                    e2 = act(dst, src, after=(m,))
                else:
                    e1 = copy(dst, src, after=(m,))
            if half < 2:
                free[half] = (e1, e2)

        def mla():
            qkv = (mark("act"), mark("dve"))
            for t in range(NT):
                cs = (rope2[:, 0, t * 16:(t + 1) * 16], rope2[:, 1, t * 16:(t + 1) * 16])
                rotate(Q[:, t, :].rearrange("p (h d) -> p h d", h=H8)[:, :, HD:QK2], H8, cs, after=qkv)
                rotate(kr[:, t:t + 1, :], 1, cs)
                m = copy(K[:, t, :].rearrange("p (h d) -> p h d", h=H8)[:, :, HD:QK2],
                         kr[:, t:t + 1, :].broadcast_to([P, H8, 32]))
                yield
            QT = S[0:QK2, 0:2048].rearrange("p (h t) -> p h t", h=H8)
            KT = S[0:QK2, 2048:4096].rearrange("p (h t) -> p h t", h=H8)
            for src, dst in ((Q, QT), (K, KT)):
                for g in range(4):
                    for j in range(2):
                        for t in range(NT):
                            h = 2 * g + j
                            mt = turn(PS[0:QK2, 6 + g % 2, (2 * j + t) * P:(2 * j + t + 1) * P],
                                      src[:, t, h * QK2:(h + 1) * QK2], (m, mark("act")), signal=(j == 1 and t == 1))
                    ma = act(dst[:, 2 * g:2 * g + 2, :], PS[0:QK2, 6 + g % 2, :].rearrange("p (h t) -> p h t", h=2),
                             after=(mt,))
                    if g % 2:
                        yield
            yield from softmax_heads(
                H8, lambda h, t: QT[:, h, t * P:(t + 1) * P], lambda h, n: KT[:, h, 0:n],
                lambda h, t: V[:, t, h * HD:(h + 1) * HD],
                lambda t: chunk(4)[:, t, :].rearrange("p (h d) -> p h d", h=H8), float(QK2) ** -0.5, False,
                (2, 3, 6, 7), after=(ma, mark("dve")), pt_at=Gf[:, 4096:5120])

        interleave(fourier(ld_dft), stream)
        interleave(mla(), stream)
        for _ in stream:
            pass
        mix2 = PR[:, 6144:6144 + NT * D].rearrange("p (t d) -> p t d", t=NT)
        t0 = branch_turn(4, 0)
        fT = proj(5).rearrange("p (g t) -> p g t", g=4)
        for g in range(2):
            hi = act(a_hi[:, 4 + 2 * g:6 + 2 * g, :], fT[:, 2 * g:2 * g + 2, :], after=(mark("pe"),))
            t1 = (hi, tt(a_lo[:, 4 + 2 * g:6 + 2 * g, :], fT[:, 2 * g:2 * g + 2, :], r32(a_hi[:, 4 + 2 * g:6 + 2 * g, :]),
                         ALU.subtract, after=(hi, mark("pe"))))
        branch(0, t0, 0, free, True, mix2, gates2)
        branch(1, t1, 4, free, False, mix2, gates2)
        mixed_out(mix2, free, ada_rows[:, 0:2, :])
        norm_turn(cond[:, 24:32], cond[:, 16:24], after=(mark("dve"),))

        m = narrow(b2("wr"), 36, 6)
        lg = fix[:, 0:72].rearrange("p (t n) -> p t n", t=NT)
        tt(lg, PS[:, 6, 0:P].rearrange("p (t n) -> p t n", t=NT)[:, :, 0:36],
           b2("br").unsqueeze(1).broadcast_to([P, NT, 36]), ALU.add, after=(m,))
        gl, el = lg[:, :, 0:4], lg[:, :, 4:36].rearrange("p t (g e) -> p t g e", g=N_GROUPS)

        def spot(a, b, n):
            return fix[:, a:a + NT * n].rearrange("p (t n) -> p t n", t=NT)

        def first_max(x, n, best, onehot):
            reduce(best, x, ALU.max)
            tt(onehot, x, best.broadcast_to([P, NT, n]), ALU.is_equal)
            tt(onehot, onehot, const("desc")[:, 0:n].unsqueeze(1).broadcast_to([P, NT, n]), ALU.mult)
            reduce(spot(200, 0, 1), onehot, ALU.max)
            return tt(onehot, onehot, spot(200, 0, 1).broadcast_to([P, NT, n]), ALU.is_equal)

        gbest, gsum, ohg, eg = spot(204, 0, 1), spot(208, 0, 1), spot(212, 0, 4), spot(220, 0, 4)
        sel, oh1, oh2, m1_, m2_ = spot(228, 0, 8), spot(244, 0, 8), spot(260, 0, 8), spot(276, 0, 1), spot(278, 0, 1)
        first_max(gl, 4, gbest, ohg)
        m = tt(eg, gl, gbest.broadcast_to([P, NT, 4]), ALU.subtract)
        m = act(eg, eg, ACT.Exp, after=(m,))
        reduce(gsum, eg, ALU.add, after=(m,))
        recip(gsum, gsum)
        picked = fix[:, 300:364].rearrange("p (t g e) -> p t g e", t=NT, g=N_GROUPS)
        for t in range(NT):
            tt(picked[:, t], el[:, t], ohg[:, t, :].unsqueeze(2).broadcast_to([P, N_GROUPS, PER_GROUP]), ALU.mult)
            reduce(sel[:, t, :], picked[:, t].rearrange("p g e -> p e g"), ALU.add)
        first_max(sel, 8, m1_, oh1)
        for t in range(NT):
            stt(sel[:, t, :], oh1[:, t, :], NEG, sel[:, t, :], ALU.mult, ALU.add)
        first_max(sel, 8, m2_, oh2)
        m = tt(m2_, m2_, m1_, ALU.subtract)
        m = act(m2_, m2_, ACT.Exp, after=(m,))
        ts(m1_, m2_, 1.0, None, ALU.add, after=(m,))
        recip(m1_, m1_)
        tt(m1_, m1_, gsum, ALU.mult)
        tt(m2_, m2_, m1_, ALU.mult)
        tt(oh1, oh1, m1_.broadcast_to([P, NT, 8]), ALU.mult)
        tt(oh2, oh2, m2_.broadcast_to([P, NT, 8]), ALU.mult)
        tt(oh1, oh1, oh2, ALU.add)
        cw = fix[:, 400:400 + NT * EXPERTS].rearrange("p (t g e) -> p t g e", t=NT, g=N_GROUPS)
        for t in range(NT):
            tt(cw[:, t], ohg[:, t, :].unsqueeze(2).broadcast_to([P, N_GROUPS, PER_GROUP]),
               oh1[:, t, :].unsqueeze(1).broadcast_to([P, N_GROUPS, PER_GROUP]), ALU.mult)
        ld_final = step("act", lambda e: e.dma_start(PR[:, 6144:6144 + D], rows2[0:1, 4 * D:5 * D].broadcast_to([P, D])),
                        (mark("dve"), mark("pe")), sem="ld_rows", by=16)

        F = 256
        sg = PR[:, 0:NT * F].rearrange("p (t f) -> p t f", t=NT)
        eh = PR[:, NT * W:NT * W + NT * F].rearrange("p (t f) -> p t f", t=NT)

        def expert_hidden(m, loop, offset):
            for t in range(NT):
                m1 = act(sg[:, t, :], PS[:, 4 + t, 0:F], ACT.Silu, after=(m, mark("dve")))
                col = lambda e, t=t: fix[:, bass.ds(index(loop, "dve", 4, 400 + t * EXPERTS + offset), 1)]
                step("dve", lambda e, t=t, col=col: e.scalar_tensor_tensor(
                    out=eh[:, t, :], in0=sg[:, t, :], scalar=col(e), in1=PS[:, 4 + t, F:2 * F],
                    op0=ALU.mult, op1=ALU.mult), (m1,))

        def expert_step(loop, offset):
            ready = (mark("act"), mark("dve"))
            expert_hidden(up(ready), loop, offset)
            down(F // P, ready, False)
            hid_turn(F)

        expert_hidden(up((mark("dve"), mark("act"))), 0, 0)
        hid_turn(F)
        clear_sums()
        expert_step(0, 1)

        def four_experts(loop):
            for j in range(4):
                expert_step(loop, 2 + j)

        stream_loop(7, four_experts)
        expert_step(0, EXPERTS - 2)
        expert_step(0, EXPERTS - 1)
        m = down(F // P, (mark("act"), mark("dve")), True)
        add_to_x(m, ada_rows[:, 2:4, :])

        xs, m = norm_rows((mark("dve"),))
        gain = PR[:, 6144:6144 + D]
        scf, shf = ada_rows[:, 6:8, :].rearrange("p c w -> p (c w)"), ada_rows[:, 4:6, :].rearrange("p c w -> p (c w)")
        ts(scf, scf, 1.0, None, ALU.add)
        tt(gain, gain, scf, ALU.mult, after=(ld_final,))
        for t in range(NT):
            tt(xs[:, t, :], xs[:, t, :], gain, ALU.mult)
            m = tt(xs[:, t, :], xs[:, t, :], shf, ALU.add)
            step("act", lambda e, t=t: e.dma_start(out[t * P:(t + 1) * P, :], xs[:, t, :]), (m,), sem="st_out", by=16)

        block = ctx.enter_context(nc.Block())

        @block.sync
        def _(e):
            feed(e)
            e.wait_ge(sems["st_out"], rec.at["st_out"])

        @block.scalar
        def _(e):
            rec.emit("act", e, sems)

        @block.vector
        def _(e):
            rec.emit("dve", e, sems)

        @block.gpsimd
        def _(e):
            rec.emit("pool", e, sems)

        @block.tensor
        def _(e):
            rec.emit("pe", e, sems)


def _chunk(w):
    nk = w.shape[0] // P
    a = w.reshape(nk, P, w.shape[1]).transpose(1, 0, 2).reshape(P, -1, UNIT)
    return a.transpose(1, 0, 2)


def _cols(v):
    return v.reshape(-1, P).T


def _rows(v):
    return np.broadcast_to(v.reshape(1, -1), (P, v.size))


def _narrow(w):
    return w.reshape(KD, P, -1).transpose(1, 0, 2).reshape(P, -1)


def _lead(a):
    z = np.zeros((P, a.shape[1]), np.float32)
    z[:a.shape[0]] = a
    return z


def _constants():
    f = np.float32
    j, i = np.arange(P)[:, None], np.arange(P)[None, :]
    tri = np.where(i <= j, 0.0, NEG)
    lmask = np.where((j <= i) & (j // L == i // L), 0.0, NEG)
    start = (np.arange(T) % L == 0)[None, :]
    inv = (f(1.0) / np.power(f(10000.0), np.arange(0, HD, 2, dtype=f) / f(HD))).astype(f)
    ang = (np.arange(T, dtype=f)[:, None] * inv[None, :]).astype(f)
    tok = lambda a: a.reshape(NT, P, -1).transpose(1, 0, 2).reshape(P, -1)
    invf = np.power(f(10000.0), -np.arange(0, ROPE2, 2, dtype=f) / f(ROPE2)).astype(f)
    parts = dict(ident=np.eye(P), cmask=np.concatenate([np.zeros((P, P)), tri], 1), lmask=lmask,
                 reset=np.broadcast_to(np.where(start, 0.0, 1.0), (P, T)),
                 resetneg=np.broadcast_to(np.where(start, NEG, 0.0), (P, T)),
                 cos=tok(np.cos(ang)), sin=tok(np.sin(ang)),
                 desc=np.broadcast_to(8.0 - np.arange(8), (P, 8)), invf=np.broadcast_to(invf, (P, 16)))
    consts = np.concatenate([parts[n] for n in CONST_COLS], 1).astype(f)
    n = np.arange(T)
    a = 2 * np.pi * ((n[:, None] * n[None, :]) % T) / T
    d = np.arange(64)
    b = 2 * np.pi * ((d[:, None] * d[None, :]) % 64) / 64
    two = lambda m: np.kron(np.eye(2), m)
    scale = (T * 64) ** -0.5
    tokens = np.concatenate([np.cos(a), np.sin(a)], 1).reshape(NT, P, 2 * T).transpose(1, 0, 2).reshape(P, -1)
    dft = np.concatenate([tokens, two(np.cos(b)) * scale, two(-np.sin(b)) * scale], 1).astype(f)
    return consts, dft


def _layout(i):
    w_in, ff1, ff2 = i["w_in"], i["w_ff1"], i["w_ff2"]
    starts = [0, 512, 1024, 1536, 2064, 2576, 3088, 3600, 4112, 4624] + [5144 + W * k for k in range(6)]
    units = []
    for l in range(DEPTH):
        units += [_chunk(w_in[l][:, s:s + W]) for s in starts]
        for name in ("w_br_gla", "w_br_moba", "w_br_mlstm"):
            units += [_chunk(i[name][l][:, n:n + W]) for n in (0, W)]
        units += [_chunk(i["w_out"][l][:, n:n + W]) for n in (0, W)]
        units.append(_chunk(ff1[l][:, 0:W]))
        units.append(np.zeros((PAD_UNITS, P, UNIT), np.float32))
        for c in range(FF_CHUNKS):
            if c + 1 < FF_CHUNKS:
                units.append(_chunk(ff1[l][:, (c + 1) * W:(c + 2) * W]))
            units.append(_chunk(ff2[l][c * W:(c + 1) * W]))
    z = i["w_in_2"][0]
    gate_at = 256 + 256 + 32 + 512
    uq = i["w_uq_2"][0].reshape(2, P, 2, 4 * QK2).transpose(1, 2, 0, 3).reshape(P, 2, 8 * QK2)
    uq = np.concatenate([uq, np.zeros((P, 2, HALF - 8 * QK2), np.float32)], 2).reshape(1, P, UNIT)
    kv = [i[n][0].reshape(2, P, W).transpose(1, 0, 2).reshape(P, HALF) for n in ("w_uk_2", "w_uv_2")]
    units += [_chunk(z[:, 0:512]), _chunk(z[:, 544:1056])]
    units += [_chunk(z[:, gate_at + W * k:gate_at + W * (k + 1)]) for k in (0, 1)]
    units += [uq, np.concatenate(kv, 1)[None]]
    units += [_chunk(z[:, gate_at + W * k:gate_at + W * (k + 1)]) for k in (2, 3)]
    for name in ("w_branch_attn_2", "w_branch_fourier_2"):
        units += [_chunk(i[name][0][:, n:n + W]) for n in (0, W)]
    units += [_chunk(i["w_out_2"][0][:, n:n + W]) for n in (0, W)]
    gu = np.concatenate([i["w_expert_gate_2"][0], i["w_expert_up_2"][0]], 2)
    dn = i["w_expert_down_2"][0]
    units.append(_chunk(gu[0]))
    for e in range(EXPERTS):
        if e + 1 < EXPERTS:
            units.append(_chunk(gu[e + 1]))
        units.append(_chunk(dn[e]))
    wall = np.concatenate(units, 0)
    assert wall.shape == (UNITS, P, UNIT), (wall.shape, UNITS)

    layers = []
    for l in range(DEPTH):
        win = w_in[l]
        parts = dict(
            g1=_cols(i["norm1_g"][l]), g2=_cols(i["norm2_g"][l]), ab=_cols(i["gla_a_b"][l]),
            conv=i["mlstm_conv_w"][l].reshape(4, 4, P).transpose(2, 1, 0).reshape(P, 16),
            gn=_rows(i["gla_norm_g"][l]), qn=_rows(i["moba_qn_g"][l]), kn=_rows(i["moba_kn_g"][l]),
            mn=_rows(i["mlstm_norm_g"][l]),
            ifb=_lead(np.stack([i["mlstm_i_b"][l], i["mlstm_f_b"][l]], 1)), aup=_lead(i["gla_a_up"][l]),
            wsm=_narrow(np.concatenate([win[:, 2048:2064], win[:, 5136:5144]], 1)))
        layers.append(np.concatenate([parts[n] for n in LAYER_COLS], 1))
    b_ada, bf = i["b_ada_2"][0], i["b_ada_final_2"]
    six = [b_ada[k * D:(k + 1) * D] for k in range(6)]
    parts = dict(gmix=_cols(i["g_norm_mix_2"][0]), gffn=_cols(i["g_norm_ffn_2"][0]), gq=_cols(i["g_q_lat_2"][0]),
                 gkv=_cols(i["g_kv_lat_2"][0]),
                 bcols=np.concatenate([_cols(six[k]) for k in (0, 1, 3, 4)], 1),
                 wkr=_narrow(z[:, 512:544]),
                 wr=_narrow(np.concatenate([i["w_router_group_2"][0], i["w_router_expert_2"][0].reshape(D, 32)], 1)),
                 br=_rows(np.concatenate([i["b_router_group_2"][0], i["b_router_expert_2"][0].reshape(-1)])))
    b2_small = np.concatenate([parts[n] for n in B2_COLS], 1)
    rows2 = np.concatenate([six[2], six[5], bf[:D], bf[D:], i["g_norm_final_2"], i["b_gates_2"][0]])[None]
    wa, wf = i["w_ada_2"][0], i["w_ada_final_2"]
    order = [wa[:, k * D:(k + 1) * D] for k in (0, 1, 3, 4, 2, 5)] + [wf[:, :D], wf[:, D:]]
    wada = np.concatenate([_chunk(w[:, n:n + W]) for w in order for n in (0, W)], 0)
    consts, dft = _constants()
    return dict(wall=wall, wada=wada, layer_small=np.stack(layers), gate_b=i["gate_b"], b2_small=b2_small,
                rows2=rows2, consts=consts, dft=dft,
                pos=i["positions_2"].reshape(NT, P).T, c=_cols(i["c_2"].reshape(-1)), x_in=i["x"][0])


def kernel(**inputs):
    import concourse.bacc as bacc
    from concourse.bass_utils import run_bass_kernel_spmd

    arrays = _layout({k: np.asarray(v) for k, v in inputs.items()})
    arrays = {k: np.ascontiguousarray(v) for k, v in arrays.items()}
    nc = bacc.Bacc("TRN2", target_bir_lowering=False, num_devices=1)
    args = {n: nc.dram_tensor(n, a.shape, mybir.dt.from_np(a.dtype), kind="ExternalInput").ap()
            for n, a in arrays.items()}
    out = nc.dram_tensor("out", (T, D), F32, kind="ExternalOutput").ap()
    build_program(nc, out=out, **args)
    result = run_bass_kernel_spmd(nc, [arrays], core_ids=[0])
    return result.results[0]["out"].reshape(1, T, D)
```

```python
from contextlib import ExitStack

import numpy as np

import concourse.bass as bass
from concourse import mybir

F32 = mybir.dt.float32
F32R = mybir.dt.float32r
U8 = mybir.dt.uint8
I32 = mybir.dt.int32
ALU = mybir.AluOpType
ACT = mybir.ActivationFunctionType
AX_X = mybir.AxisListType.X

P = 128
T = 256
NT = T // P
D = 1024
KD = D // P
DEPTH = 2
L = 64
NC = T // L
W = 512
EPS = 1e-6
NEG = -1e30
FF_CHUNKS = 4 * D // W
EXPERTS = 32
N_GROUPS, PER_GROUP = 4, 8
H8, HD = 8, 64
GH, GD = 4, 128
MH, MK, MV = 4, 64, 128
ROPE2 = 32
QK2 = 96
ADA = 2 * FF_CHUNKS

UNIT = 2048
HALF = UNIT // 2
STAGES = 4
SPLITS = 4
PAD_UNITS = 2
LAYER_UNITS = 16 * 2 + 6 + 4 + 4 * FF_CHUNKS + PAD_UNITS
BLOCK2_UNITS = 12 + 2 + 4 + 4
UNITS = DEPTH * LAYER_UNITS + BLOCK2_UNITS + 3 * EXPERTS
assert T == 2 * P and LAYER_UNITS % STAGES == 0

LAYER_COLS = dict(g1=8, g2=8, ab=4, conv=16, gn=128, qn=64, kn=64, mn=128, ifb=2, aup=512, wsm=8 * 24)
B2_COLS = dict(gmix=8, gffn=8, gq=2, gkv=2, bcols=32, wkr=8 * 32, wr=8 * 36, br=36)
CONST_COLS = dict(ident=128, cmask=256, lmask=128, reset=256, resetneg=256, cos=64, sin=64,
                  desc=8, invf=16)


def offsets(cols):
    at, out = 0, {}
    for name, n in cols.items():
        out[name] = (at, at + n)
        at += n
    return out, at


LAYER_AT, LAYER_N = offsets(LAYER_COLS)
B2_AT, B2_N = offsets(B2_COLS)
CONST_AT, CONST_N = offsets(CONST_COLS)


class Loop:

    def __init__(self, count):
        self.count, self.var, self.moved, self.items = count, {}, {}, {}


class Mark:

    def __init__(self, sem, const, loops):
        self.sem, self.const, self.loops = sem, const, loops


class Recorder:

    ENGINES = ("pe", "act", "dve", "pool", "sp")

    def __init__(self):
        self.at = {}
        self.loops = []
        self.queue = {e: [] for e in self.ENGINES}
        self.waited = {e: {} for e in self.ENGINES}
        self.last = {}

    def mark(self, sem, ahead=0):
        return Mark(sem, self.at.get(sem, 0) + ahead, tuple(self.loops))

    def step(self, engine, fn, after=(), sem=None, by=1, alone=False):
        sem = sem or engine
        waits = [m for m in after if m is not None]
        if engine in ("act", "dve", "pool") and not alone and engine in self.at:
            waits.append(self.mark(engine))
        known = self.waited[engine]
        best = {}
        for m in waits:
            key = (m.sem, m.loops)
            if m.const <= known.get(key, 0):
                continue
            if key not in best or best[key].const < m.const:
                best[key] = m
        for key, m in best.items():
            known[key] = m.const
        self.queue[engine].append((list(best.values()), fn, sem if by else None, by,
                                   tuple(self.loops)))
        if not by:
            return None
        self.at[sem] = self.at.get(sem, 0) + by
        return self.mark(sem)

    def loop(self, count, body):
        loop = Loop(count)
        outer, before = self.queue, dict(self.at)
        self.queue = {e: [] for e in self.ENGINES}
        self.loops.append(loop)
        self.waited = {e: {} for e in self.ENGINES}
        body(loop)
        self.loops.pop()
        self.waited = {e: {} for e in self.ENGINES}
        for sem, value in self.at.items():
            moved = value - before.get(sem, 0)
            loop.moved[sem] = moved
            self.at[sem] = before.get(sem, 0) + count * moved
        for e in self.ENGINES:
            loop.items[e] = self.queue[e]
            outer[e].append(loop)
        self.queue = outer
        return loop

    def emit(self, name, engine, sems, items=None):
        for item in self.queue[name] if items is None else items:
            if isinstance(item, Loop):
                if item.items[name]:
                    with engine.Fori(0, item.count) as i:
                        item.var[name] = i
                        self.emit(name, engine, sems, item.items[name])
                continue
            waits, fn, sem, by, loops = item
            for m in waits:
                value = m.const
                for lp in m.loops:
                    per = lp.moved.get(m.sem, 0)
                    if lp in loops:
                        if per:
                            value = lp.var[name] * per + value
                    else:
                        value += (lp.count - 1) * per
                engine.wait_ge(sems[m.sem], value)
            ins = fn(engine)
            if sem is not None:
                ins.then_inc(sems[sem], by)


def build_program(nc, wall, wada, layer_small, gate_b, b2_small, rows2, consts, dft, pos, c, x_in, out):
    rec = Recorder()
    step, mark = rec.step, rec.mark
    with ExitStack() as ctx:
        def sb(name, shape, dt=F32):
            return ctx.enter_context(nc.sbuf_tensor(name, shape, dt))

        stage = sb("stage", [P, STAGES, UNIT])
        w_hi = sb("w_hi", [P, SPLITS, HALF], F32R)
        w_lo = sb("w_lo", [P, SPLITS, HALF], F32R)
        X = sb("X", [P, NT, D])
        a_hi = sb("a_hi", [P, KD, T], F32R)
        a_lo = sb("a_lo", [P, KD, T], F32R)
        h_hi = sb("h_hi", [P, W // P, T], F32R)
        h_lo = sb("h_lo", [P, W // P, T], F32R)
        ada_cols = sb("ada_cols", [P, DEPTH, 32])
        csm = sb("csm", [P, CONST_N])
        lsm = sb("lsm", [P, max(LAYER_N, B2_N)])
        gm8 = sb("gm8", [P, P], U8)
        ones = sb("ones", [P, P])
        mhalf = sb("mhalf", [P, 16])
        cact = sb("cact", [P, KD])
        st = sb("st", [P, 256])
        fix = sb("fix", [P, 640])
        PR = sb("PR", [P, 10 * NT * W])
        G = sb("G", [P, NT, 3 * D])
        S = sb("S", [P, 5632])
        MS = sb("MS", [P, 2592])
        Gf = G[:, :, :].rearrange("p t n -> p (t n)")
        ada_rows = Gf[:, 0:4 * D].rearrange("p (c w) -> p c w", w=W)
        s_hi, s_lo = (a[:, :, :].rearrange("p k t -> p (k t)") for a in (h_hi, h_lo))
        BF16 = mybir.dt.bfloat16
        zrow = sb("zrow", [1, W], BF16)
        zcol = sb("zcol", [1, P], BF16)
        PS = ctx.enter_context(nc.psum_tensor("PS", [P, 8, W], F32))

        sem_names = (["pe", "act", "dve", "pool", "hi", "lo", "used", "ld_const", "ld_x", "ld_layer", "ld_gate",
                      "ld_b2", "ld_rows", "ld_dft", "ld_ada0", "ld_ada1", "ada_used", "st_out"]
                     + [f"landed{i}" for i in range(STAGES)])
        sems = {n: ctx.enter_context(nc.semaphore("s_" + n)) for n in sem_names}
        for n in sem_names:
            rec.at[n] = 0

        def const(name):
            a, b = CONST_AT[name]
            return csm[:, a:b]

        def lay(name):
            a, b = LAYER_AT[name]
            return lsm[:, a:b]

        def b2(name):
            a, b = B2_AT[name]
            return lsm[:, a:b]

        ident = const("ident")

        def proj(c, n=1):
            return PR[:, c * NT * W:(c + n) * NT * W]

        def chunk(c):
            return proj(c).rearrange("p (t w) -> p t w", t=NT)

        def act(out_, in_, func=ACT.Copy, after=(), sem=None, alone=False, **kw):
            return step("act", lambda e: e.activation(out_, in_, func, **kw), after, sem, alone=alone)

        def tt(out_, a, b, op, after=(), sem=None, alone=False):
            return step("dve", lambda e: e.tensor_tensor(out_, a, b, op), after, sem, alone=alone)

        def gp(out_, a, b, op, after=()):
            return step("pool", lambda e: e.tensor_tensor(out_, a, b, op), after)

        def ts(out_, a, s1, s2, op0, op1=None, after=()):
            if op1 is None:
                return step("dve", lambda e: e.tensor_scalar(out_, a, s1, None, op0), after)
            return step("dve", lambda e: e.tensor_scalar(out_, a, s1, s2, op0, op1), after)

        def stt(out_, a, s, b, op0, op1, after=()):
            return step("dve", lambda e: e.scalar_tensor_tensor(out=out_, in0=a, scalar=s, in1=b,
                                                               op0=op0, op1=op1), after)

        def copy(out_, a, after=()):
            return step("dve", lambda e: e.tensor_copy(out_, a), after)

        def reduce(out_, a, op, after=(), negate=None):
            return step("dve", lambda e: e.tensor_reduce(out_, a, AX_X, op, negate=negate), after)

        def recip(out_, a, after=()):
            return step("dve", lambda e: e.reciprocal(out_, a), after)

        def fill(out_, v, after=()):
            return step("dve", lambda e: e.memset(out_, v), after)

        def mm(out_, lhsT, rhs, start=True, stop=True, after=(), signal=True):
            return step("pe", lambda e: e.matmul(out_, lhsT, rhs, start=start, stop=stop,
                                                 skip_group_check=True), after, by=int(signal))

        def turn(out_, in_, after=(), signal=True, n=P):
            return step("pe", lambda e: e.transpose(out_, in_, ident[0:n, 0:n]), after, by=int(signal))

        def r32(ap):
            return ap.bitcast(F32)

        passes, rest = divmod(UNITS, STAGES)

        def load_unit(e, unit, slot):
            return e.dma_start(stage[:, slot, :], wall[bass.ds(unit, 1), :, :].rearrange("o p n -> p (o n)"))

        def feed(e):
            def one(i, k):
                ahead = 2 * (k + 1)
                base = 2 * STAGES * i + ahead
                for name in ("hi", "lo"):
                    e.wait_ge(sems[name], base)
                load_unit(e, STAGES * i + STAGES + k, k).then_inc(sems[f"landed{k}"], 16)
            for k in range(STAGES):
                load_unit(e, k, k).then_inc(sems[f"landed{k}"], 16)
            with e.Fori(0, passes - 1) as i:
                for k in range(STAGES):
                    one(i, k)
            for k in range(rest):
                one(passes - 1, k)

        state = {"half": 0, "split": 0}

        def split_half():
            h = state["split"]
            if h >= 2 * UNITS:
                return
            state["split"] += 1
            slot, unit_slot, side = h % SPLITS, (h // 2) % STAGES, h % 2
            src = stage[:, unit_slot, side * HALF:(side + 1) * HALF]
            landed = at(f"landed{unit_slot}", 16 * (h // 2 // STAGES + 1))
            free = at("used", h - SPLITS + 1)
            rounded = act(w_hi[:, slot, :], src, after=(landed, free), sem="hi", alone=True)
            tt(w_lo[:, slot, :], src, r32(w_hi[:, slot, :]), ALU.subtract, after=(landed, free, rounded),
               sem="lo", alone=True)

        def at(sem, value):
            return Mark(sem, value, tuple(rec.loops)) if value > 0 else None

        def take_half():
            h = state["half"]
            return h % SPLITS, (at("hi", h + 1), at("lo", h + 1))

        def used_half(fn, after=()):
            m = step("pe", fn, after, sem="used")
            state["half"] += 1
            split_half()
            return m

        def stream_loop(count, body):
            start = state["half"]
            loop = rec.loop(count, body)
            moved = state["half"] - start
            assert moved % (2 * STAGES) == 0 and state["split"] - state["half"] == SPLITS
            for k in range(STAGES):
                loop.moved[f"landed{k}"] = 16 * moved // (2 * STAGES)
            state["half"] = start + count * moved
            state["split"] = state["half"] + SPLITS

        def product(accs, acts_hi, acts_lo, kt, slot, cols, first, last, after, signal):
            todo = []
            for t in range(NT):
                tok = slice(t * P, (t + 1) * P)
                ah, al = acts_hi[:, kt, tok], acts_lo[:, kt, tok]
                for acc, (a, b) in zip(accs[t], cols):
                    wh, wl = w_hi[:, slot, a:b], w_lo[:, slot, a:b]
                    todo += [(acc, ah, wh, first, False), (acc, ah, wl, False, False),
                             (acc, al, wh, False, last)]
            for n, (acc, a, w, s0, s1) in enumerate(todo):
                fn = (lambda e, acc=acc, a=a, w=w, s0=s0, s1=s1:
                      e.matmul(acc, a, w, start=s0, stop=s1, skip_group_check=True))
                if signal and n == len(todo) - 1:
                    return used_half(fn, after if n == 0 else ())
                step("pe", fn, after if n == 0 else (), by=0)

        def project(banks, nk, after=(), ah=a_hi, al=a_lo, k0=0):
            for half in range(nk // 2):
                slot, ready = take_half()
                for j in range(2):
                    kt = 2 * half + j
                    m = product([[PS[:, banks[t], :]] for t in range(NT)], ah, al, k0 + kt, slot,
                                [(j * W, (j + 1) * W)], kt == 0, kt == nk - 1,
                                tuple(ready) + (tuple(after) if kt == 0 else ()), j == 1)
                yield m

        def finish(gen):
            m = None
            for m in gen:
                pass
            return m

        step("act", lambda e: e.dma_start(X[:, :, :], x_in.rearrange("(t p) d -> p t d", p=P)), sem="ld_x", by=16)
        step("act", lambda e: e.dma_start(csm[:, :], consts), sem="ld_const", by=16)
        step("act", lambda e: e.dma_start(cact[:, :], c), sem="ld_const", by=16)
        loaded_const, loaded_x = mark("ld_const"), mark("ld_x")
        fill(ones[:, :], 1.0)
        fill(zrow[:, :], 0.0)
        fill(zcol[:, :], 0.0)
        ready_ones = fill(mhalf[:, :], -0.5)
        ts(gm8[:, :], const("lmask"), 0.0, None, ALU.is_equal, after=(loaded_const,))
        act(cact[:, :], cact[:, :], ACT.Silu, after=(loaded_const,))
        for _ in range(SPLITS):
            split_half()

        def rsqrt_mean(dst, ssum, n, width):
            m = ts(dst, ssum, 1.0 / n, EPS, ALU.mult, ALU.add)
            return step("pool", lambda e: e.tensor_tensor(dst, dst, mhalf[:, 0:width], ALU.pow), (m, ready_ones))

        def turn_split(src, nk, dst_hi, dst_lo, banks, after=(), scale=None, bias=None):
            out_ = []
            for b in range(nk // 2):
                bank = banks[b % len(banks)]
                reuse = out_[b - len(banks)] if b >= len(banks) else ()
                for j in range(2):
                    for t in range(NT):
                        m = turn(PS[:, bank, (2 * j + t) * P:(2 * j + t + 1) * P], src(t, 2 * b + j),
                                 tuple(after) + tuple(reuse), signal=(j == 1 and t == 1))
                if scale is None:
                    hi, lo = (d[:, 2 * b:2 * b + 2, :].rearrange("p k t -> p (k t)") for d in (dst_hi, dst_lo))
                    m1 = act(hi, PS[:, bank, :], after=(m,))
                    m2 = tt(lo, PS[:, bank, :], r32(hi), ALU.subtract, after=(m1, m))
                else:
                    ks = (2 * b, 2 * b + 1)
                    ps = {k: PS[:, bank, (k % 2) * T:(k % 2 + 1) * T] for k in ks}
                    for k in ks:
                        kw = {} if bias is None else dict(bias=bias[:, k:k + 1])
                        m1 = act(dst_hi[:, k, :], ps[k], ACT.Copy if bias is None else ACT.Identity, after=(m,),
                                 scale=scale[:, k:k + 1], **kw)
                    for k in ks:
                        if bias is None:
                            m2 = stt(dst_lo[:, k, :], ps[k], scale[:, k:k + 1], r32(dst_hi[:, k, :]), ALU.mult,
                                     ALU.subtract, after=(m1,))
                        else:
                            tmp = S[:, 2 * D + (k % 2) * T:2 * D + (k % 2 + 1) * T]
                            ts(tmp, ps[k], scale[:, k:k + 1], bias[:, k:k + 1], ALU.mult, ALU.add, after=(m1,))
                            m2 = tt(dst_lo[:, k, :], tmp, r32(dst_hi[:, k, :]), ALU.subtract)
                out_.append((m1, m2))
            return out_[-1]

        def norm_rows(after=()):
            xs = S[:, 0:NT * D].rearrange("p (t d) -> p t d", t=NT)
            m0 = step("act", lambda e: e.activation(xs[:, 0, :], X[:, 0, :], ACT.Square,
                                                    accum_out=st[:, 0:1]), after)
            step("dve", lambda e: e.tensor_tensor(xs[:, 1, :], X[:, 1, :], X[:, 1, :], ALU.mult), after)
            reduce(st[:, 1:2], xs[:, 1, :], ALU.add)
            ts(st[:, 2:4], st[:, 0:2], 1.0 / D, EPS, ALU.mult, ALU.add, after=(m0,))
            m = step("pool", lambda e: e.tensor_tensor(st[:, 2:4], st[:, 2:4], mhalf[:, 0:2], ALU.pow),
                     (mark("dve"), ready_ones))
            mx = (act(xs[:, 0, :], X[:, 0, :], scale=st[:, 2:3], after=(m,)),
                  ts(xs[:, 1, :], X[:, 1, :], st[:, 3:4], None, ALU.mult, after=(m,)))
            return xs, mx

        def norm_turn(scale, bias=None, after=()):
            xs, m = norm_rows(after)
            return turn_split(lambda t, k: xs[:, t, k * P:(k + 1) * P], KD, a_hi, a_lo, [0, 1, 2, 3],
                              after=m, scale=scale, bias=bias)

        def head_norm(v, nh, hd, tmp, gain, after=(), op=tt, at=16):
            ssum, scale = st[:, at:at + nh], st[:, at + nh:at + 2 * nh]
            m = op(tmp, v, v, ALU.mult, after=after)
            reduce(ssum, tmp, ALU.add, after=(m,))
            m = rsqrt_mean(scale, ssum, hd, nh)
            op(v, v, scale.unsqueeze(2).broadcast_to([P, nh, hd]), ALU.mult, after=(m,))
            return op(v, v, gain.unsqueeze(1).broadcast_to([P, nh, hd]), ALU.mult)

        def softmax_heads(nh, qT, kT, values, dst, scale, causal, banks, after=(), pt_at=None):
            ba, bb, bt, bo = banks
            pbuf = lambda g: S[:, 4608 + (g % 2) * W:4608 + (g % 2 + 1) * W]
            pt_at = S[:, 0:2 * W] if pt_at is None else pt_at
            pt = lambda g: pt_at[:, (g % 2) * W:(g % 2 + 1) * W]
            outs_read = copied = None
            exps = {}
            group = [(4 * (g // 2) + g % 2, 4 * (g // 2) + g % 2 + 2) for g in range(nh // 2)]
            for t in range(NT):
                keys = (t + 1) * P if causal else T
                nj = keys // P
                scored = {}

                def scores(g):
                    bank = (ba, bb)[g % 2]
                    for j, h in enumerate(group[g]):
                        m = mm(PS[:, bank, j * T:j * T + keys], qT(h, t), kT(h, keys), signal=(j == 1),
                               after=tuple(after) + (exps.get(g % 2),) if j == 0 else ())
                    scored[g] = m

                scores(0)
                yield
                for g in range(nh // 2):
                    if g + 1 < nh // 2:
                        scores(g + 1)
                    ps = PS[:, (ba, bb)[g % 2], :].rearrange("p (j k) -> p j k", j=2)[:, :, 0:keys]
                    pv = pbuf(g).rearrange("p (j k) -> p j k", j=2)[:, :, 0:keys]
                    nm = st[:, 64 + 2 * g:66 + 2 * g]
                    if causal:
                        cm = const("cmask")[:, T - keys:T].unsqueeze(1).broadcast_to([P, 2, keys])
                        stt(pv, ps, scale, cm, ALU.mult, ALU.add, after=(scored[g],))
                        m = reduce(nm, pv, ALU.max, negate=True)
                        src, sc = pv, 1.0
                    else:
                        reduce(nm, ps, ALU.max, after=(scored[g],), negate=True)
                        m = ts(nm, nm, scale, None, ALU.mult)
                        src, sc = ps, scale
                    for j, h in enumerate(group[g]):
                        m = step("act", lambda e, j=j, h=h, pv=pv, src=src, sc=sc, g=g: e.activation(
                            pv[:, j, :], src[:, j, :], ACT.Exp, bias=st[:, 64 + 2 * g + j:65 + 2 * g + j], scale=sc,
                            accum_out=st[:, 80 + h:81 + h]), (m,) if j == 0 else ())
                    exps[g % 2] = done = m
                    yield
                    for j in range(2):
                        for n in range(nj):
                            at = (j * nj + n) * P
                            m = turn(PS[:, bt, at:at + P], pv[:, j, n * P:(n + 1) * P],
                                     (done, copied) if (j, n) == (0, 0) else (), signal=(j == 1 and n == nj - 1))
                    m = copied = copy(pt(g)[:, 0:2 * keys], PS[:, bt, 0:2 * keys], after=(m,))
                    yield
                    for j, h in enumerate(group[g]):
                        for n in range(nj):
                            m = mm(PS[:, bo, h * HD:(h + 1) * HD], pt(g)[:, (j * nj + n) * P:(j * nj + n + 1) * P],
                                   values(h, n), start=(n == 0), stop=(n == nj - 1),
                                   after=(m, outs_read) if (j, n) == (0, 0) else (), signal=(j == 1 and n == nj - 1))
                recip(st[:, 96:96 + nh], st[:, 80:80 + nh], after=(mark("act"),))
                outs_read = tt(dst(t), PS[:, bo, :].rearrange("p (h d) -> p h d", h=nh),
                               st[:, 96:96 + nh].unsqueeze(2).broadcast_to([P, nh, HD]), ALU.mult, after=(m,))
                yield

        def evacuate(c, banks, m, after=()):
            m0 = act(chunk(c)[:, 0, :], PS[:, banks[0], :], after=(m,) + tuple(after))
            m1 = copy(chunk(c)[:, 1, :], PS[:, banks[1], :], after=(m,) + tuple(after))
            return (m0, m1)

        PAIRS = [(4, 5), (0, 1)]

        def gates_stream(n, free, bias, out_, alone=(False,)):
            for c in range(n):
                pair = 0 if alone[0] else c % 2
                banks = PAIRS[pair]
                for n, m in enumerate(project(banks, KD, after=free[pair])):
                    if n + 1 < KD // 2:
                        yield
                cols = slice(c * W, (c + 1) * W)
                for t in (1, 0):
                    m1 = tt(out_[:, t, cols], PS[:, banks[t], :], out_[:, 0, cols], ALU.add, after=(m,) + tuple(bias))
                    act(out_[:, t, cols], out_[:, t, cols], ACT.Sigmoid, after=(m1,))
                free[pair] = (m1,)
                yield

        def interleave(mains, filler):
            mains = list(mains)
            while mains:
                mains = [g for g in mains if next(g, "end") != "end"]
                next(filler, None)

        def branch_turn(c, hi, lo, banks):
            return turn_split(lambda t, k: chunk(c)[:, t, k * P:(k + 1) * P], 4, hi, lo, banks,
                              after=(mark("act"), mark("dve")))

        def branch(b, ready, ah, al, free, first, acc, gate):
            for nh in range(D // W):
                banks = PAIRS[nh % 2]
                m = finish(project(banks, 4, after=tuple(free[nh % 2]) + tuple(ready), ah=ah, al=al))
                cols = slice(nh * W, (nh + 1) * W)
                for t in range(NT):
                    g = gate[:, t, b * D + nh * W:b * D + (nh + 1) * W]
                    m1 = tt(acc[:, t, cols] if first else g, PS[:, banks[t], :], g, ALU.mult, after=(m,))
                    if not first:
                        tt(acc[:, t, cols], acc[:, t, cols], g, ALU.add)
                free[nh % 2] = (m1,)

        def gla(sm, progress, evac):
            E = [S[:, 1024 * i:1024 * (i + 1)] for i in range(4)]
            Bc, E1, E2, E3 = E
            h4 = lambda a: a.rearrange("p (h t) -> p h t", h=GH)
            m = sm
            for h in range(GH):
                m = mm(PS[:, 6 + h // 2, (h % 2) * T:(h % 2 + 1) * T], lay("aup")[0:16, h * P:(h + 1) * P],
                       fix[0:16, 0:T], after=(sm,), signal=(h % 2 == 1))
                if h % 2:
                    for j in (h - 1, h):
                        ts(h4(Bc)[:, j, :], PS[:, 6 + j // 2, (j % 2) * T:(j % 2 + 1) * T],
                           lay("ab")[:, j:j + 1], None, ALU.add, after=(m,))
            m = stt(E1, Bc, -1.0, Bc, ALU.mult, ALU.max)
            m = act(E1, E1, ACT.Exp, after=(m,), scale=-1.0)
            m = act(E1, E1, ACT.Ln, bias=1.0)
            stt(Bc, Bc, 0.0, E1, ALU.min, ALU.subtract, after=(m,))
            yield
            for h in range(GH):
                step("dve", lambda e, h=h: e.tensor_tensor_scan(h4(E1)[:, h, :], const("reset"), h4(Bc)[:, h, :], 0.0,
                                                                ALU.mult, ALU.add))
            b3 = E1.rearrange("p (c l) -> p c l", l=L)
            m = tt(E3.rearrange("p (c l) -> p c l", l=L), b3[:, :, L - 1:L].broadcast_to([P, GH * NC, L]), b3,
                   ALU.subtract)
            dec = fix[:, 256:256 + GH * NC]
            act(dec.unsqueeze(2), b3[:, :, L - 1:L], ACT.Exp, after=(m,), scale=1.0 / 16)
            act(E3, E3, ACT.Exp, scale=1.0 / 16)
            act(E2, E1, ACT.Exp, scale=-1.0 / 16)
            me = act(E1, E1, ACT.Exp, scale=1.0 / 16)
            yield
            read = {6: me, 7: me}
            for src in range(2):
                while progress[0] <= src:
                    yield
                v = chunk(src)
                for b in range(2):
                    bank = 6 + b
                    for j in range(2):
                        for t in range(NT):
                            mt = turn(PS[:, bank, (2 * j + t) * P:(2 * j + t + 1) * P],
                                      v[:, t, (2 * b + j) * P:(2 * b + j + 1) * P],
                                      evac[src] + (read[bank],), signal=(j == 1 and t == 1))
                    cols = slice(b * W, (b + 1) * W)
                    ps = PS[:, bank, :]
                    if src == 0:
                        m = stt(E1[:, cols], ps, float(GD) ** -0.5, E1[:, cols], ALU.mult, ALU.mult, after=(mt, me))
                    else:
                        tt(E2[:, cols], ps, E2[:, cols], ALU.mult, after=(mt, me))
                        m = tt(E3[:, cols], ps, E3[:, cols], ALU.mult)
                    read[bank] = m
                    yield
            ke = chunk(1)
            for t in range(NT):
                for h in range(GH):
                    mt = turn(PS[:, 6 + t, h * P:(h + 1) * P], h4(E3)[:, h, t * P:(t + 1) * P], (m,), signal=(h == GH - 1))
                m2 = act(ke[:, t, :], PS[:, 6 + t, :], after=(mt,))
            yield
            at = Bc.rearrange("p (t w) -> p t w", t=NT)
            m = fill(Bc, 0.0)
            yield
            for t in range(NT):
                for h in range(GH):
                    tok = slice(t * P, (t + 1) * P)
                    mt = mm(PS[:, 2 + t, h * P:(h + 1) * P], h4(E2)[:, h, tok], h4(E1)[:, h, tok],
                            after=(m,), signal=(h == GH - 1))
                fill(st[:, 200:201], 0.0, after=(mt,))
                step("dve", lambda e, t=t: e.copy_predicated(
                    at[:, t, :].rearrange("p (h i) -> p h i", h=GH),
                    gm8[:, :].unsqueeze(1).broadcast_to([P, GH, P]),
                    PS[:, 2 + t, :].rearrange("p (h i) -> p h i", h=GH)), alone=True)
                yield
            q0 = proj(0)
            Sx = [q0[:, 0:W], q0[:, W:2 * W], S[:, 4096:4096 + W]]
            while progress[0] <= 3:
                yield
            v = chunk(2)
            mS, states = None, {}
            for cix in range(NC - 1):
                t, o = cix // 2, (cix % 2) * L
                bank = 6 + cix % 2
                for h in range(GH):
                    mt = mm(PS[:, bank, h * P:(h + 1) * P], ke[o:o + L, t, h * P:(h + 1) * P],
                            v[o:o + L, t, h * P:(h + 1) * P], after=(m2, states.get(cix - 2)) + evac[2],
                            signal=(h == GH - 1))
                if cix == 0:
                    mS = copy(Sx[0], PS[:, bank, :], after=(mt,))
                else:
                    for h in range(GH):
                        hc = slice(h * P, (h + 1) * P)
                        mS = stt(Sx[cix][:, hc], Sx[cix - 1][:, hc], dec[:, h * NC + cix:h * NC + cix + 1],
                                 PS[:, bank, hc], ALU.mult, ALU.add, after=(mt,))
                states[cix] = mS
                yield
            tmp = S[:, 4608:4608 + W]
            y = chunk(3)
            for t in range(NT):
                bank = 2 + t
                for h in range(GH):
                    hc = slice(h * P, (h + 1) * P)
                    parts = [(slice(0, P), at[:, t, hc], v[:, t, hc])]
                    for half in range(2):
                        cix = 2 * t + half
                        if cix:
                            parts.append((slice(half * L, half * L + L), h4(E1)[:, h, cix * L:(cix + 1) * L], Sx[cix - 1][:, hc]))
                    for n, (rows, a, b) in enumerate(parts):
                        mt = mm(PS[rows, bank, hc], a, b, start=(n == 0), stop=(n == len(parts) - 1),
                                after=(mS,), signal=(h == GH - 1 and n == len(parts) - 1))
                copy(S[:, 5120:5120 + W], PS[:, bank, :], after=(mt,))
                yield
                ov = S[:, 5120:5120 + W].rearrange("p (h d) -> p h d", h=GH)
                head_norm(ov, GH, GD, tmp.rearrange("p (h d) -> p h d", h=GH), lay("gn"))
                m = act(tmp, y[:, t, :], ACT.Silu, after=(mark("dve"),))
                tt(y[:, t, :], S[:, 5120:5120 + W], tmp, ALU.mult, after=(m,))
                yield

        def rope_heads(v, t):
            x = v[:, t, :].rearrange("p (h s d) -> p h s d", h=H8, s=2)
            A = MS[:, 0:W].rearrange("p (h s d) -> p h s d", h=H8, s=2)
            B = MS[:, W:2 * W].rearrange("p (h s d) -> p h s d", h=H8, s=2)
            cos, sin = (const(n)[:, t * 32:(t + 1) * 32] for n in ("cos", "sin"))
            b3 = lambda a: a.unsqueeze(1).broadcast_to([P, H8, 32])
            for s in range(2):
                gp(A[:, :, s, :], x[:, :, s, :], b3(cos), ALU.mult)
                gp(B[:, :, s, :], x[:, :, 1 - s, :], b3(sin), ALU.mult)
            gp(x[:, :, 0, :], A[:, :, 0, :], B[:, :, 0, :], ALU.subtract)
            return gp(x[:, :, 1, :], A[:, :, 1, :], B[:, :, 1, :], ALU.add)

        def moba_prepare(progress, evac, done):
            for c, gain in ((4, lay("qn")), (5, lay("kn"))):
                while progress[0] <= c:
                    yield
                written = evac[c]
                v = chunk(c)
                for t in range(NT):
                    head_norm(v[:, t, :].rearrange("p (h d) -> p h d", h=H8), H8, HD,
                              MS[:, 0:W].rearrange("p (h d) -> p h d", h=H8), gain, after=written, op=gp, at=224)
                    yield
                    done[c] = rope_heads(v, t)
                    yield

        def moba(done):
            TQ = S[:, 2560:2560 + 1024].rearrange("p (g t) -> p g t", g=4)
            TK = S[:, 3584:3584 + 1024].rearrange("p (g t) -> p g t", g=4)
            start = (mark("act"), mark("dve"))
            for c, dst, banks in ((4, TQ, (6, 7)), (5, TK, (2, 3))):
                for b in range(2):
                    for j in range(2):
                        for t in range(NT):
                            g = 2 * b + j
                            mt = turn(PS[:, banks[b], (2 * j + t) * P:(2 * j + t + 1) * P],
                                      chunk(c)[:, t, g * P:(g + 1) * P], (done[c],) + start,
                                      signal=(j == 1 and t == 1))
                    ma = act(dst[:, 2 * b:2 * b + 2, :], PS[:, banks[b], :].rearrange("p (g t) -> p g t", g=2), after=(mt,))
                yield
            rows = lambda h: slice((h % 2) * HD, (h % 2 + 1) * HD)
            yield from softmax_heads(
                H8, lambda h, t: TQ[rows(h), h // 2, t * P:(t + 1) * P], lambda h, n: TK[rows(h), h // 2, 0:n],
                lambda h, t: chunk(6)[:, t, h * HD:(h + 1) * HD],
                lambda t: chunk(4)[:, t, :].rearrange("p (h d) -> p h d", h=H8), float(HD) ** -0.5, True,
                (2, 3, 6, 7), after=(ma, mark("dve")))

        def mlstm(progress):
            NB = 4 * 260
            pad = MS[:, 0:NB].rearrange("p (g t) -> p g t", g=4)
            qk = proj(0).rearrange("p (g t) -> p g t", g=4)
            vx = MS[:, 1040:1040 + NT * MH * 129].rearrange("p (t h v) -> p t h v", t=NT, h=MH)
            kw = proj(1)[:, 0:NT * 256].rearrange("p (t c) -> p t c", t=NT)
            iwb = MS[:, 2072:2072 + 2 * 260].rearrange("p (g t) -> p g t", g=2)
            Sx = [proj(5)[:, 258 * i:258 * (i + 1)].rearrange("p (g v) -> p g v", g=2) for i in range(3)]
            m = fill(pad[:, :, 0:3], 0.0, after=(mark("pe"), mark("act"), mark("pool")))
            v = chunk(7)
            for b in range(2):
                for j in range(2):
                    for t in range(NT):
                        g = 2 * b + j
                        mt = turn(PS[:, b, (2 * j + t) * P:(2 * j + t + 1) * P], v[:, t, g * P:(g + 1) * P],
                                  (m, mark("act")), signal=(j == 1 and t == 1))
                ma = act(pad[:, 2 * b:2 * b + 2, 3:259], PS[:, b, :].rearrange("p (g t) -> p g t", g=2), after=(mt,))
            yield
            conv = lay("conv").rearrange("p (g j) -> p g j", g=4)
            for g in range(4):
                ts(qk[:, g, :], pad[:, g, 0:T], conv[:, g, 0:1], None, ALU.mult, after=(ma,))
                for j in range(1, 4):
                    stt(qk[:, g, :], pad[:, g, j:j + T], conv[:, g, j:j + 1], qk[:, g, :], ALU.mult, ALU.add)
                if g >= 2:
                    ts(qk[:, g, :], qk[:, g, :], float(MK) ** -0.5, None, ALU.mult)
                yield
            iwa = proj(1)[0:MH, 512:772]
            b_, g_, u_, w2, emr, tmp = (S[0:MH, 1024 + i * T:1024 + (i + 1) * T] for i in range(6))
            lf = fix[0:MH, 288:288 + T]
            ts(g_, li_row, lay("ifb")[0:MH, 0:1], None, ALU.add, after=(mark("pe"),))
            ts(b_, lf, lay("ifb")[0:MH, 1:2], None, ALU.add)
            m = stt(tmp, b_, -1.0, b_, ALU.mult, ALU.max)
            act(tmp, tmp, ACT.Exp, after=(m,), scale=-1.0)
            m = act(tmp, tmp, ACT.Ln, bias=1.0)
            stt(tmp, b_, 0.0, tmp, ALU.min, ALU.subtract, after=(m,))
            step("dve", lambda e: e.tensor_tensor_scan(b_, const("reset")[0:MH, :], tmp, 0.0, ALU.mult, ALU.add))
            tt(g_, g_, b_, ALU.subtract)
            step("dve", lambda e: e.tensor_tensor_scan(u_, const("resetneg")[0:MH, :], g_, 0.0, ALU.add, ALU.max))
            yield
            c4 = lambda a: a.rearrange("p (c l) -> p c l", l=L)
            bl, ml = st[0:MH, 112:116], st[0:MH, 116:120]
            M, Mp = st[0:MH, 121:125], st[0:MH, 120:124]
            fill(st[0:MH, 120:121], 0.0)
            copy(bl.unsqueeze(2), c4(b_)[:, :, L - 1:L])
            tt(ml.unsqueeze(2), c4(b_)[:, :, L - 1:L], c4(u_)[:, :, L - 1:L], ALU.add)
            step("dve", lambda e: e.tensor_tensor_scan(M, bl, ml, 0.0, ALU.add, ALU.max))
            bc = lambda a: a.unsqueeze(2).broadcast_to([MH, NC, L])
            tt(c4(u_), c4(u_), bc(Mp), ALU.max)
            tt(st[0:MH, 128:132], bl, M, ALU.subtract)
            m = tt(c4(w2), c4(g_), bc(st[0:MH, 128:132]), ALU.add)
            act(w2, w2, ACT.Exp, after=(m,))
            tt(st[0:MH, 132:136], st[0:MH, 128:132], Mp, ALU.add)
            tt(c4(iwa[:, 0:T]), bc(Mp), c4(u_), ALU.subtract)
            m = copy(iwa[:, T:T + 4], st[0:MH, 132:136])
            act(iwa, iwa, ACT.Exp, after=(m,))
            m = tt(emr, b_, u_, ALU.add)
            ma = act(emr, emr, ACT.Exp, after=(m,), scale=-1.0)
            yield
            pick = lambda h, n: ident[0:MH, h:h + 1].broadcast_to([MH, n])
            for pr in range(2):
                for j in range(2):
                    mt = mm(PS[j * L:(j + 1) * L, pr, 0:260], pick(2 * pr + j, L), iwa, after=(ma, mark("dve")), signal=(j == 1))
                ma2 = act(iwb[:, pr, :], PS[:, pr, 0:260], after=(mt,))
            yield
            cols = st[:, 144:144 + 24].rearrange("p (w t h) -> p w t h", w=3, t=NT)
            for wi, a in enumerate((g_, w2, emr)):
                for t in range(NT):
                    mt = mm(PS[:, 0, (wi * NT + t) * MH:(wi * NT + t + 1) * MH], a[:, t * P:(t + 1) * P],
                            ident[0:MH, 0:MH], after=(ma2, mark("dve")), signal=(wi == 2 and t == 1))
            mc = copy(st[:, 144:168], PS[:, 0, 0:24], after=(mt,))
            for pr in range(2):
                for t in range(NT):
                    mt = turn(PS[:, 1, (t * 2 + pr) * P:(t * 2 + pr + 1) * P], qk[:, 2 + pr, t * P:(t + 1) * P],
                              (ma2, mark("dve")), signal=(pr == 1 and t == 1))
            for t in range(NT):
                mk = tt(kw[:, t, :].rearrange("p (h d) -> p h d", h=MH),
                        PS[:, 1, t * 256:(t + 1) * 256].rearrange("p (h d) -> p h d", h=MH),
                        cols[:, 1, t, :].unsqueeze(2).broadcast_to([P, MH, MK]), ALU.mult, after=(mt,))
            fill(vx[:, :, :, MV:MV + 1], 1.0)
            while progress[0] <= 8:
                yield
            for t in range(NT):
                mv = copy(vx[:, t, :, 0:MV], chunk(8)[:, t, :].rearrange("p (h v) -> p h v", h=MH))
            yield
            mS = None
            for cix in range(NC - 1):
                t, o = cix // 2, (cix % 2) * L
                bank = cix % 2
                mm(PS[:, bank, 0:1], kw[o:o + L, t, 0:P], vx[o:o + L, t, 0, 0:1], after=(mv, mS, ma2), signal=False)
                for h in range(MH):
                    pr, r = h // 2, (h % 2) * L
                    mt = mm(PS[r:r + L, bank, pr * 129:(pr + 1) * 129], kw[o:o + L, t, h * MK:(h + 1) * MK],
                            vx[o:o + L, t, h, :], signal=(h == MH - 1))
                if cix == 0:
                    mS = copy(Sx[0].rearrange("p g v -> p (g v)"), PS[:, bank, 0:258], after=(mt,))
                else:
                    for pr in range(2):
                        mS = stt(Sx[cix][:, pr, :], Sx[cix - 1][:, pr, :], iwb[:, pr, T + cix:T + cix + 1],
                                 PS[:, bank, pr * 129:(pr + 1) * 129], ALU.mult, ALU.add, after=(mt,))
                yield
            q2 = MS[:, 0:512].rearrange("p (g t) -> p g t", g=2)
            mq = tt(q2, qk[:, 0:2, :], iwb[:, :, 0:T], ALU.mult)
            while progress[0] <= 9:
                yield
            y = chunk(9)
            hp = lambda h: slice((h % 2) * L, (h % 2 + 1) * L)
            for t in range(NT):
                tok = slice(t * P, (t + 1) * P)
                for h in range(MH):
                    mt = mm(PS[:, 0, h * P:(h + 1) * P], pick(h, P), u_[:, tok], after=(mS, mark("dve"), mark("act")),
                            signal=(h == MH - 1))
                dm = proj(7)[:, 0:W].rearrange("p (h i) -> p h i", h=MH)
                tt(dm, cols[:, 0, t, :].unsqueeze(2).broadcast_to([P, MH, P]),
                   PS[:, 0, :].rearrange("p (h i) -> p h i", h=MH), ALU.subtract, after=(mt,))
                m = stt(dm, dm, 0.0, const("lmask").unsqueeze(1).broadcast_to([P, MH, P]), ALU.min, ALU.add)
                m = act(dm, dm, ACT.Exp, after=(m,))
                for h in range(MH):
                    mt = mm(PS[:, h % 2, (h // 2) * P:(h // 2 + 1) * P], qk[hp(h), 2 + h // 2, tok],
                            qk[hp(h), h // 2, tok], after=(mark("dve"),), signal=(h == MH - 1))
                yield
                pairs = dm.rearrange("p (g s) i -> p g s i", s=2)
                for s in range(2):
                    sc = PS[:, s, 0:2 * P].rearrange("p (g i) -> p g i", g=2)
                    md = tt(pairs[:, :, s, :], sc, pairs[:, :, s, :], ALU.mult, after=(mt, m))
                m = md
                yield
                for h in range(MH):
                    bank, o = h % 2, (h // 2) * T
                    parts = [(slice(0, P), dm[:, h, :], vx[:, t, h, :])]
                    for half in range(2):
                        cix = 2 * t + half
                        if cix:
                            parts.append((slice(half * L, half * L + L), q2[hp(h), h // 2, cix * L:(cix + 1) * L],
                                          Sx[cix - 1][hp(h), h // 2, :]))
                    for n, (rows, a, b) in enumerate(parts):
                        mt = mm(PS[rows, bank, o:o + 129], a, b, start=(n == 0), stop=(n == len(parts) - 1),
                                after=(m, mq), signal=(h == MH - 1 and n == len(parts) - 1))
                yield
                o2 = PS[:, 0:2, :].rearrange("p b (j v) -> p j b v", j=2)
                den = st[:, 176:180]
                copy(den.rearrange("p (j b o) -> p j b o", j=2, o=1), o2[:, :, :, MV:MV + 1], after=(mt,))
                stt(den, den, -1.0, den, ALU.mult, ALU.max)
                tt(den, den, cols[:, 2, t, :], ALU.max)
                recip(den, den)
                hid = MS[:, 512:1024].rearrange("p (h v) -> p h v", h=MH)
                for j in range(2):
                    tt(hid[:, 2 * j:2 * j + 2, :], o2[:, j, :, 0:MV],
                       den[:, 2 * j:2 * j + 2].unsqueeze(2).broadcast_to([P, 2, MV]), ALU.mult)
                head_norm(hid, MH, MV, dm, lay("mn"))
                m = act(y[:, t, :], y[:, t, :], ACT.Sigmoid)
                tt(y[:, t, :], MS[:, 512:1024], y[:, t, :], ALU.mult, after=(m,))
                yield

        def narrow(src, groups, width, after=()):
            hi, lo = (a[:, 0:KD * width].rearrange("p (k n) -> p k n", k=KD) for a in (s_hi, s_lo))
            read = (mark("pe"),) + tuple(after)
            if sum(n for _, n, _ in groups) < width:
                m = act(s_hi[:, 0:KD * width], csm[:, 0:KD * width], after=read, scale=0.0)
                act(s_lo[:, 0:KD * width], csm[:, 0:KD * width], scale=0.0)
            for a, n, row in groups:
                m1 = act(hi[:, :, row:row + n], src[:, :, a:a + n], after=read)
                m2 = tt(lo[:, :, row:row + n], src[:, :, a:a + n], r32(hi[:, :, row:row + n]), ALU.subtract,
                        after=(m1,) + read)
            todo = [(a, w, k) for k in range(KD) for a, w in ((a_hi, hi), (a_hi, lo), (a_lo, hi))]
            for i, (a, w, k) in enumerate(todo):
                m = mm(PS[0:width, 6, 0:T], w[:, k, :], a[:, k, :], start=(i == 0), stop=(i == len(todo) - 1),
                       after=(m1, m2), signal=(i == len(todo) - 1))
            return m

        def narrow_tokens(name, n):
            m = narrow(b2(name).rearrange("p (k n) -> p k n", k=KD), ((0, n, 0),), n)
            m = copy(MS[0:n, 0:T], PS[0:n, 6, 0:T], after=(m,))
            for t in range(NT):
                m2 = turn(PS[:, 7, t * 64:t * 64 + n], MS[0:n, t * P:(t + 1) * P], (m,), n=n)
            return m2, PS[:, 7, 0:P].rearrange("p (t n) -> p t n", t=NT)[:, :, 0:n]

        li_row = MS[0:MH, 2072:2072 + T]

        def index(loop, name, scale=1, offset=0):
            return (loop if isinstance(loop, int) else loop.var[name]) * scale + offset

        ada_stage, acc = proj(4, 4), proj(8)[:, 0:W]

        def load_ada(lp, cl, ahead, after):
            for u in range(2):
                step("pool", lambda e, u=u: e.dma_start(
                    ada_stage[:, u * UNIT:(u + 1) * UNIT],
                    wada[bass.ds((index(lp, "pool", FF_CHUNKS) + index(cl, "pool", 1, ahead)) * 2 + u, 1), :, :]
                    .rearrange("o p n -> p (o n)")), after, sem=f"ld_ada{u}", by=16)

        def ada_step(lp, cl, more=True):
            landed = [mark(f"ld_ada{u}") for u in range(2)]
            for k in range(KD):
                src = ada_stage[:, k * W:(k + 1) * W]
                if k == 0:
                    ts(acc, src, cact[:, 0:1], None, ALU.mult, after=(landed[0],))
                else:
                    m = stt(acc, src, cact[:, k:k + 1], acc, ALU.mult, ALU.add, after=(landed[k // 4],))
                if k % 2:
                    yield
            if more:
                load_ada(lp, cl, 1, (m,))
            yield
            for j in range(4):
                mm(PS[:, 6, j:j + 1], acc[:, j * P:(j + 1) * P], ones[:, 0:1], after=(m, mark("act")), signal=False)
            summed = mm(PS[:, 7, :], ones[:, :], acc)
            act_out = lambda e: ada_cols[:, bass.ds(index(lp, "act"), 1), bass.ds(index(cl, "act", 4), 4)]
            step("act", lambda e: e.activation(act_out(e), PS[:, 6, 0:4].unsqueeze(1), ACT.Copy), (summed,))
            step("act", lambda e: e.activation(ada_rows[:, bass.ds(index(cl, "act"), 1), :], PS[:, 7, :].unsqueeze(1),
                                               ACT.Copy))
            yield

        relu = proj(0).rearrange("p (t w) -> p t w", t=NT)
        hid = proj(1).rearrange("p (t w) -> p t w", t=NT)

        def up(after=(), between=iter(())):
            for m in project((4, 5), KD, after=after):
                next(between, None)
            return m

        def down(nk, ready, last, between=iter(())):
            accs = [[PS[:, 2 * t, :], PS[:, 2 * t + 1, :]] for t in range(NT)]
            for k in range(nk):
                slot, ok = take_half()
                m = product(accs, h_hi, h_lo, k, slot, [(0, W), (W, D)], False, last and k == nk - 1,
                            tuple(ok) + tuple(ready), True)
                next(between, None)
            return m

        def clear_sums(pad=False):
            for b in range(4):
                if pad:
                    _, ok = take_half()
                    used_half(lambda e, b=b: e.matmul(PS[:, b, :], zcol[0:1, :], zrow[0:1, :], start=True, stop=False,
                                                      skip_group_check=True), ok + (mark("act"), mark("dve")))
                    continue
                mm(PS[:, b, :], zcol[0:1, :], zrow[0:1, :], start=True, stop=False, signal=(b == 3),
                   after=(mark("act"), mark("dve")))

        def ff_hidden(m, read=None):
            for t in range(NT):
                m1 = act(relu[:, t, :], PS[:, 4 + t, :], ACT.Relu, after=(m, read))
                m2 = tt(hid[:, t, :], relu[:, t, :], relu[:, t, :], ALU.mult, after=(m1,))
            return (m2,)

        def before_turn(width):
            return mark("act", -(width // T)), mark("dve", -(width // T))

        def hid_turn(width, after=()):
            v = PR[:, NT * W:NT * W + NT * width].rearrange("p (t w) -> p t w", t=NT)
            return turn_split(lambda t, k: v[:, t, k * P:(k + 1) * P], width // P, h_hi, h_lo, [6, 7],
                              after=after or (mark("dve"), mark("act")))

        def add_to_x(m, gate_rows=None):
            for t in range(NT):
                for n in range(2):
                    cols = slice(n * W, (n + 1) * W)
                    if gate_rows is None:
                        last = tt(X[:, t, cols], PS[:, 2 * t + n, :], X[:, t, cols], ALU.add, after=(m,))
                    else:
                        tmp = S[:, 0:W]
                        tt(tmp, PS[:, 2 * t + n, :], gate_rows[:, n, :], ALU.mult, after=(m,))
                        last = tt(X[:, t, cols], tmp, X[:, t, cols], ALU.add)
            return last

        def mixed_out(mix, free, gate_rows=None):
            mT = turn_split(lambda t, k: mix[:, t, k * P:(k + 1) * P], KD, a_hi, a_lo, [2, 3, 6, 7],
                            after=(mark("dve"), mark("act")))
            for nh in range(D // W):
                banks = PAIRS[nh % 2]
                m = finish(project(banks, KD, after=tuple(free[nh % 2]) + tuple(mT)))
                for t in range(NT):
                    cols = slice(nh * W, (nh + 1) * W)
                    if gate_rows is None:
                        m1 = tt(X[:, t, cols], PS[:, banks[t], :], X[:, t, cols], ALU.add, after=(m,))
                    else:
                        tt(S[:, 0:W], PS[:, banks[t], :], gate_rows[:, nh, :], ALU.mult, after=(m,))
                        m1 = tt(X[:, t, cols], S[:, 0:W], X[:, t, cols], ALU.add)
            return m1

        def until(stream, progress, chunks):
            while progress[0] < chunks:
                next(stream)

        def layer(lp):
            small = step("act", lambda e: e.dma_start(
                lsm[:, 0:LAYER_N], layer_small[bass.ds(index(lp, "act"), 1), :, :].rearrange("o p n -> p (o n)")),
                (mark("pe"), mark("dve"), mark("pool")), sem="ld_layer", by=16)
            bias = step("act", lambda e: e.dma_start(
                G[:, 0, :], gate_b[bass.ds(index(lp, "act"), 1), :].broadcast_to([P, 3 * D])), sem="ld_gate", by=16)
            xT = norm_turn(lay("g1"), after=(small, loaded_x, loaded_const, mark("dve")))
            m = narrow(lay("wsm").rearrange("p (k n) -> p k n", k=KD), ((0, 16, 0), (16, MH, 32), (20, MH, 64)),
                       64 + MH, after=(small,))
            copy(fix[0:MH, 288:288 + T], PS[64:64 + MH, 6, 0:T], after=(m,))
            copy(li_row, PS[32:32 + MH, 6, 0:T])
            ga = copy(fix[0:16, 0:T], PS[0:16, 6, 0:T])
            free = [tuple(xT), tuple(xT)]
            progress, alone, evac = [0], [False], {}

            def projections():
                for cix in range(10):
                    pair = 0 if alone[0] else cix % 2
                    for n, m in enumerate(project(PAIRS[pair], KD, after=free[pair] + tuple(xT))):
                        if n + 1 < KD // 2:
                            yield
                    free[pair] = evac[cix] = evacuate(cix, PAIRS[pair], m)
                    progress[0] = cix + 1
                    yield
                yield from gates_stream(6, free, (bias,), G, alone)

            stream = projections()
            done = {}
            interleave((gla(ga, progress, evac), moba_prepare(progress, evac, done)), stream)
            until(stream, progress, 8)
            alone[0] = True
            interleave((moba(done), mlstm(progress)), stream)
            alone[0] = False
            mix = PR[:, 0:NT * D].rearrange("p (t d) -> p t d", t=NT)
            operands = [(3, h_hi, h_lo), (4, a_hi[:, 0:4, :], a_lo[:, 0:4, :]), (9, a_hi[:, 4:8, :], a_lo[:, 4:8, :])]
            turns = [branch_turn(*operands[0], (2, 3))]
            for _ in stream:
                pass
            turns += [branch_turn(*operands[1], (6, 7)), branch_turn(*operands[2], (2, 3))]
            for n, (c, hi, lo) in enumerate(operands):
                branch(n, turns[n], hi, lo, free, n == 0, mix, G)
            mixed_out(mix, free)
            norm_turn(lay("g2"), after=(mark("dve"),))

            load_ada(lp, 0, 0, (mark("dve"), mark("pe")))
            m = up((mark("dve"), mark("act")))
            ff_hidden(m)
            hid_turn(W)
            clear_sums(pad=True)

            def ff_step(cl):
                read, ready = before_turn(W), (mark("act"), mark("dve"))
                ada = ada_step(lp, cl)
                squared = ff_hidden(up(read, ada), read[1])
                down(W // P, ready, False, ada)
                hid_turn(W, squared + (mark("act"),))

            stream_loop(FF_CHUNKS - 1, ff_step)
            ada = ada_step(lp, FF_CHUNKS - 1, more=False)
            m = down(W // P, (mark("act"), mark("dve")), True, ada)
            add_to_x(m)
            for _ in ada:
                pass

        stream_loop(DEPTH, layer)

        def fourier(ld):
            ft = S[:, 2048:4096].rearrange("p (g n) -> p g n", g=4)
            u = chunk(5)
            C = dftc[:, 0:1024].rearrange("p (k n) -> p k n", k=NT)
            for g in range(4):
                for k in range(NT):
                    mt = mm(PS[:, 2 + g % 2, :], u[:, k, g * P:(g + 1) * P], C[:, k, :], start=(k == 0), stop=(k == 1),
                            after=(ld, mark("act"), mark("dve")), signal=(k == 1))
                m = act(ft[:, g, :], PS[:, 2 + g % 2, :], after=(mt,))
                yield
            fT = proj(5).rearrange("p (g t) -> p g t", g=4)
            for b in range(2):
                for j in range(2):
                    g = 2 * b + j
                    for s in range(2):
                        mt = mm(PS[:, 6 + b, j * T:(j + 1) * T], dftc[:, 1024 + s * P:1024 + (s + 1) * P],
                                ft[:, g, s * T:(s + 1) * T], start=(s == 0), stop=(s == 1), after=(m, mark("dve")),
                                signal=(s == 1))
                mf = act(fT[:, 2 * b:2 * b + 2, :], PS[:, 6 + b, :].rearrange("p (j t) -> p j t", j=2), after=(mt,))
                yield

        def angles(ld):
            pf, ang, n, r = (Gf[:, 5120 + 64 * i:5120 + 64 * (i + 1)] for i in range(4))
            twopi = 2 * np.pi
            c1 = float(np.float32(6.28125))
            c2 = float(np.float32(np.float32((twopi - c1) * 2 ** 24) // 2 ** 12 * 2 ** 12 / 2 ** 24))
            c3 = float(twopi - c1 - c2)
            magic = 1.5 * 2 ** 23
            lim = 3.1415925
            copy(pf[:, 0:NT], posi, after=(ld,))
            for t in range(NT):
                ts(ang[:, t * 16:(t + 1) * 16], const("invf"), pf[:, t:t + 1], None, ALU.mult)
            out_ = []
            for i, (quarter, shift) in enumerate(((0.25, np.pi / 2), (0.0, 0.0))):
                a, nn, rr = ang[:, 0:32], n[:, 0:32], r[:, 32 * i:32 * i + 32]
                ts(nn, a, 1 / twopi, quarter, ALU.mult, ALU.add)
                ts(nn, nn, magic, None, ALU.add)
                ts(nn, nn, -magic, None, ALU.add)
                stt(rr, nn, -c1, a, ALU.mult, ALU.add)
                stt(rr, nn, -c2, rr, ALU.mult, ALU.add)
                stt(rr, nn, -c3, rr, ALU.mult, ALU.add)
                ts(rr, rr, float(shift), lim, ALU.add, ALU.min)
                m = ts(rr, rr, -lim, None, ALU.max)
                m = act(rope2[:, i, :], rr, ACT.Sin, after=(m,))
            return m

        def rotate(x, n, cs, after=()):
            cos, sin = (a.unsqueeze(1).broadcast_to([P, n, 16]) for a in cs)
            w4 = [Gf[:, 5376 + 128 * i:5376 + 128 * i + 16 * n].rearrange("p (n d) -> p n d", n=n) for i in range(4)]
            x1, x2 = x[:, :, 0:16], x[:, :, 16:32]
            tt(w4[0], x1, cos, ALU.mult, after=after)
            tt(w4[1], x2, sin, ALU.mult)
            tt(w4[2], x2, cos, ALU.mult)
            tt(w4[3], x1, sin, ALU.mult)
            tt(x1, w4[0], w4[1], ALU.subtract)
            return tt(x2, w4[2], w4[3], ALU.add)

        posi = fix[:, 464:466].bitcast(I32)
        rope2 = fix[:, 544:608].rearrange("p (s n) -> p s n", s=2)
        cond = fix[:, 608:640]
        dftc = S[:, 4096:4096 + 1280]
        mark_all = lambda: (mark("pe"), mark("act"), mark("dve"), mark("pool"))

        small = step("act", lambda e: e.dma_start(lsm[:, 0:B2_N], b2_small), mark_all(), sem="ld_b2", by=16)
        step("act", lambda e: e.dma_start(posi, pos), sem="ld_b2", by=16)
        ld_pos = mark("ld_b2")
        gates2 = PR[:, 0:NT * 2 * D].rearrange("p (t n) -> p t n", t=NT)
        bias2 = step("act", lambda e: e.dma_start(gates2[:, 0, :], rows2[0:1, 5 * D:7 * D].broadcast_to([P, 2 * D])),
                     sem="ld_gate", by=16)
        ld_rows = step("act", lambda e: e.dma_start(PR[:, 6144:6144 + 4 * D], rows2[0:1, 0:4 * D].broadcast_to([P, 4 * D])),
                       sem="ld_rows", by=16)
        ld_dft = step("act", lambda e: e.dma_start(dftc, dft), sem="ld_dft", by=16)
        tt(cond[:, 0:32], ada_cols[:, 0, :], b2("bcols"), ALU.add, after=(ld_pos, mark("act")))
        for at_, gain in ((8, "gmix"), (24, "gffn")):
            ts(cond[:, at_:at_ + 8], cond[:, at_:at_ + 8], 1.0, None, ALU.add)
            tt(cond[:, at_:at_ + 8], cond[:, at_:at_ + 8], b2(gain), ALU.mult)
        rows_flat = ada_rows.rearrange("p c w -> p (c w)")
        tt(rows_flat, rows_flat, PR[:, 6144:6144 + 4 * D], ALU.add, after=(ld_rows, mark("act")))
        uT = norm_turn(cond[:, 8:16], cond[:, 0:8], after=(mark("dve"),))
        m, narrow_out = narrow_tokens("wkr", ROPE2)
        kr = fix[:, 0:64].rearrange("p (t n) -> p t n", t=NT)
        copy(kr, narrow_out, after=(m,))

        free = [tuple(uT), tuple(uT)]
        for cix in (4, 5):
            m = finish(project(PAIRS[cix % 2], KD, after=free[cix % 2]))
            free[cix % 2] = evacuate(cix, PAIRS[cix % 2], m)
        stream = gates_stream(4, free, (bias2,), gates2)

        def latents():
            for t in range(NT):
                v = chunk(4)[:, t, :].rearrange("p (n d) -> p n d", n=2)
                tmp = S[:, 0:W].rearrange("p (n d) -> p n d", n=2)
                tt(tmp, v, v, ALU.mult, after=(mark("act"),))
                reduce(st[:, 16:18], tmp, ALU.add)
                m = rsqrt_mean(st[:, 32:34], st[:, 16:18], 256, 2)
                tt(v, v, st[:, 32:34].unsqueeze(2).broadcast_to([P, 2, 256]), ALU.mult, after=(m,))
                yield
            angles(ld_pos)
            yield
            turn_split(lambda t, k: chunk(4)[:, t, k * P:(k + 1) * P], 4, h_hi, h_lo, [6, 7],
                       after=(mark("dve"), mark("act")), scale=lsm[:, B2_AT["gq"][0]:B2_AT["gkv"][1]])
            yield

        lat = latents()
        done_lat = [False]
        for n in range(8):
            next(stream)
            if n % 2 == 1:
                next(lat, None)
        for _ in lat:
            pass
        Q = PR[:, 6144:6144 + NT * 768].rearrange("p (t n) -> p t n", t=NT)
        K = PR[:, 7680:7680 + NT * 768].rearrange("p (t n) -> p t n", t=NT)
        V = chunk(9)
        latent_ready = (mark("act"), mark("dve"))
        for half in range(4):
            banks = (PAIRS[0], PAIRS[1], (2, 3), (6, 7))[half]
            width, k0 = (4 * QK2, 0) if half < 2 else (W, 2)
            slot, ok = take_half()
            for k in range(2):
                m = product([[PS[:, banks[t], 0:width]] for t in range(NT)], h_hi, h_lo, k0 + k, slot,
                            [(k * width, (k + 1) * width)], k == 0, k == 1, tuple(ok) + latent_ready, k == 1)
            for t in range(NT):
                src = PS[:, banks[t], 0:width]
                if half < 2:
                    dst = Q[:, t, half * width:(half + 1) * width]
                elif half == 2:
                    dst = K[:, t, :].rearrange("p (h d) -> p h d", h=H8)[:, :, 0:HD]
                    src = src.rearrange("p (h d) -> p h d", h=H8)
                else:
                    dst = V[:, t, :]
                if t:
                    e2 = act(dst, src, after=(m,))
                else:
                    e1 = copy(dst, src, after=(m,))
            if half < 2:
                free[half] = (e1, e2)
        latents_used = m

        def mla():
            qkv = (mark("act"), mark("dve"))
            for t in range(NT):
                cs = (rope2[:, 0, t * 16:(t + 1) * 16], rope2[:, 1, t * 16:(t + 1) * 16])
                rotate(Q[:, t, :].rearrange("p (h d) -> p h d", h=H8)[:, :, HD:QK2], H8, cs, after=qkv)
                rotate(kr[:, t:t + 1, :], 1, cs)
                m = copy(K[:, t, :].rearrange("p (h d) -> p h d", h=H8)[:, :, HD:QK2],
                         kr[:, t:t + 1, :].broadcast_to([P, H8, 32]))
                yield
            QT = S[0:QK2, 0:2048].rearrange("p (h t) -> p h t", h=H8)
            KT = S[0:QK2, 2048:4096].rearrange("p (h t) -> p h t", h=H8)
            for src, dst in ((Q, QT), (K, KT)):
                for g in range(4):
                    for j in range(2):
                        for t in range(NT):
                            h = 2 * g + j
                            mt = turn(PS[0:QK2, 6 + g % 2, (2 * j + t) * P:(2 * j + t + 1) * P],
                                      src[:, t, h * QK2:(h + 1) * QK2], (m, mark("act")), signal=(j == 1 and t == 1))
                    ma = act(dst[:, 2 * g:2 * g + 2, :], PS[0:QK2, 6 + g % 2, :].rearrange("p (h t) -> p h t", h=2),
                             after=(mt,))
                    if g % 2:
                        yield
            yield from softmax_heads(
                H8, lambda h, t: QT[:, h, t * P:(t + 1) * P], lambda h, n: KT[:, h, 0:n],
                lambda h, t: V[:, t, h * HD:(h + 1) * HD],
                lambda t: chunk(4)[:, t, :].rearrange("p (h d) -> p h d", h=H8), float(QK2) ** -0.5, False,
                (2, 3, 6, 7), after=(ma, mark("dve")), pt_at=Gf[:, 4096:5120])

        interleave((fourier(ld_dft),), stream)
        fT = proj(5).rearrange("p (g t) -> p g t", g=4)
        for g in range(2):
            pair = slice(2 * g, 2 * g + 2)
            rounded = act(h_hi[:, pair, :], fT[:, pair, :], after=(latents_used,))
            fourier_split = (rounded, tt(h_lo[:, pair, :], fT[:, pair, :], r32(h_hi[:, pair, :]), ALU.subtract,
                                         after=(rounded, latents_used)))
        interleave((mla(),), stream)
        for _ in stream:
            pass
        mix2 = PR[:, 6144:6144 + NT * D].rearrange("p (t d) -> p t d", t=NT)
        t0 = branch_turn(4, a_hi[:, 0:4, :], a_lo[:, 0:4, :], (2, 3))
        branch(1, fourier_split, h_hi, h_lo, free, True, mix2, gates2)
        branch(0, t0, a_hi, a_lo, free, False, mix2, gates2)
        mixed_out(mix2, free, ada_rows[:, 0:2, :])
        norm_turn(cond[:, 24:32], cond[:, 16:24], after=(mark("dve"),))

        m, narrow_out = narrow_tokens("wr", 36)
        lg = fix[:, 0:72].rearrange("p (t n) -> p t n", t=NT)
        tt(lg, narrow_out,
           b2("br").unsqueeze(1).broadcast_to([P, NT, 36]), ALU.add, after=(m,))
        gl, el = lg[:, :, 0:4], lg[:, :, 4:36].rearrange("p t (g e) -> p t g e", g=N_GROUPS)

        def spot(a, b, n):
            return fix[:, a:a + NT * n].rearrange("p (t n) -> p t n", t=NT)

        def first_max(x, n, best, onehot):
            reduce(best, x, ALU.max)
            tt(onehot, x, best.broadcast_to([P, NT, n]), ALU.is_equal)
            tt(onehot, onehot, const("desc")[:, 0:n].unsqueeze(1).broadcast_to([P, NT, n]), ALU.mult)
            reduce(spot(200, 0, 1), onehot, ALU.max)
            return tt(onehot, onehot, spot(200, 0, 1).broadcast_to([P, NT, n]), ALU.is_equal)

        gbest, gsum, ohg, eg = spot(204, 0, 1), spot(208, 0, 1), spot(212, 0, 4), spot(220, 0, 4)
        sel, oh1, oh2, m1_, m2_ = spot(228, 0, 8), spot(244, 0, 8), spot(260, 0, 8), spot(276, 0, 1), spot(278, 0, 1)
        first_max(gl, 4, gbest, ohg)
        m = tt(eg, gl, gbest.broadcast_to([P, NT, 4]), ALU.subtract)
        m = act(eg, eg, ACT.Exp, after=(m,))
        reduce(gsum, eg, ALU.add, after=(m,))
        recip(gsum, gsum)
        picked = fix[:, 300:364].rearrange("p (t g e) -> p t g e", t=NT, g=N_GROUPS)
        for t in range(NT):
            tt(picked[:, t], el[:, t], ohg[:, t, :].unsqueeze(2).broadcast_to([P, N_GROUPS, PER_GROUP]), ALU.mult)
            reduce(sel[:, t, :], picked[:, t].rearrange("p g e -> p e g"), ALU.add)
        first_max(sel, 8, m1_, oh1)
        for t in range(NT):
            stt(sel[:, t, :], oh1[:, t, :], NEG, sel[:, t, :], ALU.mult, ALU.add)
        first_max(sel, 8, m2_, oh2)
        m = tt(m2_, m2_, m1_, ALU.subtract)
        m = act(m2_, m2_, ACT.Exp, after=(m,))
        ts(m1_, m2_, 1.0, None, ALU.add, after=(m,))
        recip(m1_, m1_)
        tt(m1_, m1_, gsum, ALU.mult)
        tt(m2_, m2_, m1_, ALU.mult)
        tt(oh1, oh1, m1_.broadcast_to([P, NT, 8]), ALU.mult)
        tt(oh2, oh2, m2_.broadcast_to([P, NT, 8]), ALU.mult)
        tt(oh1, oh1, oh2, ALU.add)
        cw = fix[:, 400:400 + NT * EXPERTS].rearrange("p (t g e) -> p t g e", t=NT, g=N_GROUPS)
        for t in range(NT):
            tt(cw[:, t], ohg[:, t, :].unsqueeze(2).broadcast_to([P, N_GROUPS, PER_GROUP]),
               oh1[:, t, :].unsqueeze(1).broadcast_to([P, N_GROUPS, PER_GROUP]), ALU.mult)
        ld_final = step("act", lambda e: e.dma_start(PR[:, 6144:6144 + D], rows2[0:1, 4 * D:5 * D].broadcast_to([P, D])),
                        (mark("dve"), mark("pe")), sem="ld_rows", by=16)

        F = 256
        sg = PR[:, 0:NT * F].rearrange("p (t f) -> p t f", t=NT)
        eh = PR[:, NT * W:NT * W + NT * F].rearrange("p (t f) -> p t f", t=NT)

        def expert_hidden(m, loop, offset):
            for t in range(NT):
                m1 = act(sg[:, t, :], PS[:, 4 + t, 0:F], ACT.Silu, after=(m, mark("dve")))
                col = lambda e, t=t: fix[:, bass.ds(index(loop, "dve", 4, 400 + t * EXPERTS + offset), 1)]
                m2 = step("dve", lambda e, t=t, col=col: e.scalar_tensor_tensor(
                    out=eh[:, t, :], in0=sg[:, t, :], scalar=col(e), in1=PS[:, 4 + t, F:2 * F],
                    op0=ALU.mult, op1=ALU.mult), (m1,))
            return (m2,)

        def expert_step(loop, offset):
            read, ready = before_turn(F), (mark("act"), mark("dve"))
            gated = expert_hidden(up(read), loop, offset)
            down(F // P, ready, False)
            hid_turn(F, gated)

        expert_hidden(up((mark("dve"), mark("act"))), 0, 0)
        hid_turn(F)
        clear_sums()
        expert_step(0, 1)

        def four_experts(loop):
            for j in range(4):
                expert_step(loop, 2 + j)

        stream_loop(7, four_experts)
        expert_step(0, EXPERTS - 2)
        expert_step(0, EXPERTS - 1)
        m = down(F // P, (mark("act"), mark("dve")), True)
        add_to_x(m, ada_rows[:, 2:4, :])

        xs, scaled = norm_rows((mark("dve"),))
        gain = PR[:, 6144:6144 + D]
        scf, shf = ada_rows[:, 6:8, :].rearrange("p c w -> p (c w)"), ada_rows[:, 4:6, :].rearrange("p c w -> p (c w)")
        ts(scf, scf, 1.0, None, ALU.add)
        tt(gain, gain, scf, ALU.mult, after=(ld_final,) + scaled)
        for t in range(NT):
            tt(xs[:, t, :], xs[:, t, :], gain, ALU.mult)
            m = tt(xs[:, t, :], xs[:, t, :], shf, ALU.add)
            step("act", lambda e, t=t: e.dma_start(out[t * P:(t + 1) * P, :], xs[:, t, :]), (m,), sem="st_out", by=16)

        block = ctx.enter_context(nc.Block())

        @block.sync
        def _(e):
            feed(e)
            e.wait_ge(sems["st_out"], rec.at["st_out"])

        @block.scalar
        def _(e):
            rec.emit("act", e, sems)

        @block.vector
        def _(e):
            rec.emit("dve", e, sems)

        @block.gpsimd
        def _(e):
            rec.emit("pool", e, sems)

        @block.tensor
        def _(e):
            rec.emit("pe", e, sems)


def _chunk(w):
    nk = w.shape[0] // P
    a = w.reshape(nk, P, w.shape[1]).transpose(1, 0, 2).reshape(P, -1, UNIT)
    return a.transpose(1, 0, 2)


def _cols(v):
    return v.reshape(-1, P).T


def _rows(v):
    return np.broadcast_to(v.reshape(1, -1), (P, v.size))


def _narrow(w):
    return w.reshape(KD, P, -1).transpose(1, 0, 2).reshape(P, -1)


def _lead(a):
    z = np.zeros((P, a.shape[1]), np.float32)
    z[:a.shape[0]] = a
    return z


def _constants():
    f = np.float32
    j, i = np.arange(P)[:, None], np.arange(P)[None, :]
    tri = np.where(i <= j, 0.0, NEG)
    lmask = np.where((j <= i) & (j // L == i // L), 0.0, NEG)
    start = (np.arange(T) % L == 0)[None, :]
    inv = (f(1.0) / np.power(f(10000.0), np.arange(0, HD, 2, dtype=f) / f(HD))).astype(f)
    ang = (np.arange(T, dtype=f)[:, None] * inv[None, :]).astype(f)
    tok = lambda a: a.reshape(NT, P, -1).transpose(1, 0, 2).reshape(P, -1)
    invf = np.power(f(10000.0), -np.arange(0, ROPE2, 2, dtype=f) / f(ROPE2)).astype(f)
    parts = dict(ident=np.eye(P), cmask=np.concatenate([np.zeros((P, P)), tri], 1), lmask=lmask,
                 reset=np.broadcast_to(np.where(start, 0.0, 1.0), (P, T)),
                 resetneg=np.broadcast_to(np.where(start, NEG, 0.0), (P, T)),
                 cos=tok(np.cos(ang)), sin=tok(np.sin(ang)),
                 desc=np.broadcast_to(8.0 - np.arange(8), (P, 8)), invf=np.broadcast_to(invf, (P, 16)))
    consts = np.concatenate([parts[n] for n in CONST_COLS], 1).astype(f)
    n = np.arange(T)
    a = 2 * np.pi * ((n[:, None] * n[None, :]) % T) / T
    d = np.arange(64)
    b = 2 * np.pi * ((d[:, None] * d[None, :]) % 64) / 64
    two = lambda m: np.kron(np.eye(2), m)
    scale = (T * 64) ** -0.5
    tokens = np.concatenate([np.cos(a), np.sin(a)], 1).reshape(NT, P, 2 * T).transpose(1, 0, 2).reshape(P, -1)
    dft = np.concatenate([tokens, two(np.cos(b)) * scale, two(-np.sin(b)) * scale], 1).astype(f)
    return consts, dft


def _layout(i):
    w_in, ff1, ff2 = i["w_in"], i["w_ff1"], i["w_ff2"]
    starts = [0, 512, 1024, 1536, 2064, 2576, 3088, 3600, 4112, 4624] + [5144 + W * k for k in range(6)]
    units = []
    for l in range(DEPTH):
        units += [_chunk(w_in[l][:, s:s + W]) for s in starts]
        for name in ("w_br_gla", "w_br_moba", "w_br_mlstm"):
            units += [_chunk(i[name][l][:, n:n + W]) for n in (0, W)]
        units += [_chunk(i["w_out"][l][:, n:n + W]) for n in (0, W)]
        units.append(_chunk(ff1[l][:, 0:W]))
        units.append(np.zeros((PAD_UNITS, P, UNIT), np.float32))
        for c in range(FF_CHUNKS):
            if c + 1 < FF_CHUNKS:
                units.append(_chunk(ff1[l][:, (c + 1) * W:(c + 2) * W]))
            units.append(_chunk(ff2[l][c * W:(c + 1) * W]))
    z = i["w_in_2"][0]
    gate_at = 256 + 256 + 32 + 512
    uq = i["w_uq_2"][0].reshape(2, P, 2, 4 * QK2).transpose(1, 2, 0, 3).reshape(P, 2, 8 * QK2)
    uq = np.concatenate([uq, np.zeros((P, 2, HALF - 8 * QK2), np.float32)], 2).reshape(1, P, UNIT)
    kv = [i[n][0].reshape(2, P, W).transpose(1, 0, 2).reshape(P, HALF) for n in ("w_uk_2", "w_uv_2")]
    units += [_chunk(z[:, 0:512]), _chunk(z[:, 544:1056])]
    units += [_chunk(z[:, gate_at + W * k:gate_at + W * (k + 1)]) for k in (0, 1)]
    units += [uq, np.concatenate(kv, 1)[None]]
    units += [_chunk(z[:, gate_at + W * k:gate_at + W * (k + 1)]) for k in (2, 3)]
    for name in ("w_branch_fourier_2", "w_branch_attn_2"):
        units += [_chunk(i[name][0][:, n:n + W]) for n in (0, W)]
    units += [_chunk(i["w_out_2"][0][:, n:n + W]) for n in (0, W)]
    gu = np.concatenate([i["w_expert_gate_2"][0], i["w_expert_up_2"][0]], 2)
    dn = i["w_expert_down_2"][0]
    units.append(_chunk(gu[0]))
    for e in range(EXPERTS):
        if e + 1 < EXPERTS:
            units.append(_chunk(gu[e + 1]))
        units.append(_chunk(dn[e]))
    wall = np.concatenate(units, 0)
    assert wall.shape == (UNITS, P, UNIT), (wall.shape, UNITS)

    layers = []
    for l in range(DEPTH):
        win = w_in[l]
        parts = dict(
            g1=_cols(i["norm1_g"][l]), g2=_cols(i["norm2_g"][l]), ab=_cols(i["gla_a_b"][l]),
            conv=i["mlstm_conv_w"][l].reshape(4, 4, P).transpose(2, 1, 0).reshape(P, 16),
            gn=_rows(i["gla_norm_g"][l]), qn=_rows(i["moba_qn_g"][l]), kn=_rows(i["moba_kn_g"][l]),
            mn=_rows(i["mlstm_norm_g"][l]),
            ifb=_lead(np.stack([i["mlstm_i_b"][l], i["mlstm_f_b"][l]], 1)), aup=_lead(i["gla_a_up"][l]),
            wsm=_narrow(np.concatenate([win[:, 2048:2064], win[:, 5136:5144]], 1)))
        layers.append(np.concatenate([parts[n] for n in LAYER_COLS], 1))
    b_ada, bf = i["b_ada_2"][0], i["b_ada_final_2"]
    six = [b_ada[k * D:(k + 1) * D] for k in range(6)]
    parts = dict(gmix=_cols(i["g_norm_mix_2"][0]), gffn=_cols(i["g_norm_ffn_2"][0]), gq=_cols(i["g_q_lat_2"][0]),
                 gkv=_cols(i["g_kv_lat_2"][0]),
                 bcols=np.concatenate([_cols(six[k]) for k in (0, 1, 3, 4)], 1),
                 wkr=_narrow(z[:, 512:544]),
                 wr=_narrow(np.concatenate([i["w_router_group_2"][0], i["w_router_expert_2"][0].reshape(D, 32)], 1)),
                 br=_rows(np.concatenate([i["b_router_group_2"][0], i["b_router_expert_2"][0].reshape(-1)])))
    b2_small = np.concatenate([parts[n] for n in B2_COLS], 1)
    rows2 = np.concatenate([six[2], six[5], bf[:D], bf[D:], i["g_norm_final_2"], i["b_gates_2"][0]])[None]
    wa, wf = i["w_ada_2"][0], i["w_ada_final_2"]
    order = [wa[:, k * D:(k + 1) * D] for k in (0, 1, 3, 4, 2, 5)] + [wf[:, :D], wf[:, D:]]
    wada = np.concatenate([_chunk(w[:, n:n + W]) for w in order for n in (0, W)], 0)
    consts, dft = _constants()
    return dict(wall=wall, wada=wada, layer_small=np.stack(layers), gate_b=i["gate_b"], b2_small=b2_small,
                rows2=rows2, consts=consts, dft=dft,
                pos=i["positions_2"].reshape(NT, P).T, c=_cols(i["c_2"].reshape(-1)), x_in=i["x"][0])


def kernel(**inputs):
    import concourse.bacc as bacc
    from concourse.bass_utils import run_bass_kernel_spmd

    arrays = _layout({k: np.asarray(v) for k, v in inputs.items()})
    arrays = {k: np.ascontiguousarray(v) for k, v in arrays.items()}
    nc = bacc.Bacc("TRN2", target_bir_lowering=False, num_devices=1)
    args = {n: nc.dram_tensor(n, a.shape, mybir.dt.from_np(a.dtype), kind="ExternalInput").ap()
            for n, a in arrays.items()}
    out = nc.dram_tensor("out", (T, D), F32, kind="ExternalOutput").ap()
    build_program(nc, out=out, **args)
    result = run_bass_kernel_spmd(nc, [arrays], core_ids=[0])
    return result.results[0]["out"].reshape(1, T, D)
```

```python
from contextlib import ExitStack

import numpy as np

import concourse.bass as bass
from concourse import mybir

F32 = mybir.dt.float32
F32R = mybir.dt.float32r
U8 = mybir.dt.uint8
I32 = mybir.dt.int32
ALU = mybir.AluOpType
ACT = mybir.ActivationFunctionType
AX_X = mybir.AxisListType.X

P = 128
T = 256
NT = T // P
D = 1024
KD = D // P
DEPTH = 2
L = 64
NC = T // L
W = 512
EPS = 1e-6
NEG = -1e30
FF_CHUNKS = 4 * D // W
GLA_PACE = 5
EXPERTS = 32
N_GROUPS, PER_GROUP = 4, 8
H8, HD = 8, 64
GH, GD = 4, 128
MH, MK, MV = 4, 64, 128
ROPE2 = 32
QK2 = 96
ADA = 2 * FF_CHUNKS

UNIT = 2048
HALF = UNIT // 2
STAGES = 4
SPLITS = 4
PAD_UNITS = 2
LAYER_UNITS = 16 * 2 + 6 + 4 + 4 * FF_CHUNKS + PAD_UNITS
BLOCK2_UNITS = 12 + 2 + 4 + 4
UNITS = DEPTH * LAYER_UNITS + BLOCK2_UNITS + 3 * EXPERTS
assert T == 2 * P and LAYER_UNITS % STAGES == 0

LAYER_COLS = dict(g1=8, g2=8, ab=4, conv=16, gn=128, qn=64, kn=64, mn=128, ifb=2, aup=512, wsm=8 * 24)
B2_COLS = dict(gmix=8, gffn=8, gq=2, gkv=2, bcols=32, wkr=8 * 32, wr=8 * 36, br=36)
CONST_COLS = dict(ident=128, cmask=256, lmask=128, reset=256, resetneg=256, cos=64, sin=64,
                  desc=8, invf=16)


def offsets(cols):
    at, out = 0, {}
    for name, n in cols.items():
        out[name] = (at, at + n)
        at += n
    return out, at


LAYER_AT, LAYER_N = offsets(LAYER_COLS)
B2_AT, B2_N = offsets(B2_COLS)
CONST_AT, CONST_N = offsets(CONST_COLS)


class Loop:

    def __init__(self, count):
        self.count, self.var, self.moved, self.items = count, {}, {}, {}


class Mark:

    def __init__(self, sem, const, loops):
        self.sem, self.const, self.loops = sem, const, loops


class Recorder:

    ENGINES = ("pe", "act", "dve", "pool", "sp")

    def __init__(self):
        self.at = {}
        self.loops = []
        self.queue = {e: [] for e in self.ENGINES}
        self.waited = {e: {} for e in self.ENGINES}
        self.last = {}

    def mark(self, sem, ahead=0):
        return Mark(sem, self.at.get(sem, 0) + ahead, tuple(self.loops))

    def step(self, engine, fn, after=(), sem=None, by=1, alone=False):
        sem = sem or engine
        waits = [m for m in after if m is not None]
        if engine in ("act", "dve", "pool") and not alone and engine in self.at:
            waits.append(self.mark(engine))
        known = self.waited[engine]
        best = {}
        for m in waits:
            key = (m.sem, m.loops)
            if m.const <= known.get(key, 0):
                continue
            if key not in best or best[key].const < m.const:
                best[key] = m
        for key, m in best.items():
            known[key] = m.const
        self.queue[engine].append((list(best.values()), fn, sem if by else None, by,
                                   tuple(self.loops)))
        if not by:
            return None
        self.at[sem] = self.at.get(sem, 0) + by
        return self.mark(sem)

    def loop(self, count, body):
        loop = Loop(count)
        outer, before = self.queue, dict(self.at)
        self.queue = {e: [] for e in self.ENGINES}
        self.loops.append(loop)
        self.waited = {e: {} for e in self.ENGINES}
        body(loop)
        self.loops.pop()
        self.waited = {e: {} for e in self.ENGINES}
        for sem, value in self.at.items():
            moved = value - before.get(sem, 0)
            loop.moved[sem] = moved
            self.at[sem] = before.get(sem, 0) + count * moved
        for e in self.ENGINES:
            loop.items[e] = self.queue[e]
            outer[e].append(loop)
        self.queue = outer
        return loop

    def emit(self, name, engine, sems, items=None):
        for item in self.queue[name] if items is None else items:
            if isinstance(item, Loop):
                if item.items[name]:
                    with engine.Fori(0, item.count) as i:
                        item.var[name] = i
                        self.emit(name, engine, sems, item.items[name])
                continue
            waits, fn, sem, by, loops = item
            for m in waits:
                value = m.const
                for lp in m.loops:
                    per = lp.moved.get(m.sem, 0)
                    if lp in loops:
                        if per:
                            value = lp.var[name] * per + value
                    else:
                        value += (lp.count - 1) * per
                engine.wait_ge(sems[m.sem], value)
            ins = fn(engine)
            if sem is not None:
                ins.then_inc(sems[sem], by)


def build_program(nc, wall, wada, small, gate_b, rows2, consts, dft, pos, c, x_in, out):
    rec = Recorder()
    step, mark = rec.step, rec.mark
    with ExitStack() as ctx:
        def sb(name, shape, dt=F32):
            return ctx.enter_context(nc.sbuf_tensor(name, shape, dt))

        stage = sb("stage", [P, STAGES, UNIT])
        w_hi = sb("w_hi", [P, SPLITS, HALF], F32R)
        w_lo = sb("w_lo", [P, SPLITS, HALF], F32R)
        X = sb("X", [P, NT, D])
        a_hi = sb("a_hi", [P, KD, T], F32R)
        a_lo = sb("a_lo", [P, KD, T], F32R)
        h_hi = sb("h_hi", [P, W // P, T], F32R)
        h_lo = sb("h_lo", [P, W // P, T], F32R)
        ada_cols = sb("ada_cols", [P, DEPTH, 32])
        csm = sb("csm", [P, CONST_N])
        lsm = sb("lsm", [P, LAYER_N])
        gm8 = sb("gm8", [P, P], U8)
        ones = sb("ones", [P, P])
        mhalf = sb("mhalf", [P, 16])
        cact = sb("cact", [P, KD])
        st = sb("st", [P, 256])
        fix = sb("fix", [P, 640])
        PR = sb("PR", [P, 10 * NT * W])
        G = sb("G", [P, NT, 3 * D])
        S = sb("S", [P, 5632])
        MS = sb("MS", [P, 2592])
        Gf = G[:, :, :].rearrange("p t n -> p (t n)")
        ada_rows = Gf[:, 0:4 * D].rearrange("p (c w) -> p c w", w=W)
        s_hi, s_lo = (a[:, :, :].rearrange("p k t -> p (k t)") for a in (h_hi, h_lo))
        zrow = sb("zrow", [1, W], mybir.dt.bfloat16)
        zcol = sb("zcol", [1, P], mybir.dt.bfloat16)
        PS = ctx.enter_context(nc.psum_tensor("PS", [P, 8, W], F32))

        sem_names = (["pe", "act", "dve", "pool", "hi", "lo", "used", "ld_const", "ld_x", "ld_small", "ld_gate",
                      "ld_pos", "ld_rows", "ld_dft", "ld_ada0", "ld_ada1", "st_out"]
                     + [f"landed{i}" for i in range(STAGES)])
        sems = {n: ctx.enter_context(nc.semaphore("s_" + n)) for n in sem_names}
        for n in sem_names:
            rec.at[n] = 0

        def const(name):
            a, b = CONST_AT[name]
            return csm[:, a:b]

        def lay(name):
            a, b = LAYER_AT[name]
            return lsm[:, a:b]

        def b2(name):
            a, b = B2_AT[name]
            return lsm[:, a:b]

        ident = const("ident")

        def proj(c, n=1):
            return PR[:, c * NT * W:(c + n) * NT * W]

        def chunk(c):
            return proj(c).rearrange("p (t w) -> p t w", t=NT)

        def act(out_, in_, func=ACT.Copy, after=(), sem=None, alone=False, **kw):
            return step("act", lambda e: e.activation(out_, in_, func, **kw), after, sem, alone=alone)

        def tt(out_, a, b, op, after=(), sem=None, alone=False):
            return step("dve", lambda e: e.tensor_tensor(out_, a, b, op), after, sem, alone=alone)

        def gp(out_, a, b, op, after=()):
            return step("pool", lambda e: e.tensor_tensor(out_, a, b, op), after)

        def ts(out_, a, s1, s2, op0, op1=None, after=()):
            if op1 is None:
                return step("dve", lambda e: e.tensor_scalar(out_, a, s1, None, op0), after)
            return step("dve", lambda e: e.tensor_scalar(out_, a, s1, s2, op0, op1), after)

        def stt(out_, a, s, b, op0, op1, after=()):
            return step("dve", lambda e: e.scalar_tensor_tensor(out=out_, in0=a, scalar=s, in1=b,
                                                               op0=op0, op1=op1), after)

        def copy(out_, a, after=()):
            return step("dve", lambda e: e.tensor_copy(out_, a), after)

        def reduce(out_, a, op, after=(), negate=None):
            return step("dve", lambda e: e.tensor_reduce(out_, a, AX_X, op, negate=negate), after)

        def recip(out_, a, after=()):
            return step("dve", lambda e: e.reciprocal(out_, a), after)

        def fill(out_, v, after=()):
            return step("dve", lambda e: e.memset(out_, v), after)

        def mm(out_, lhsT, rhs, start=True, stop=True, after=(), signal=True):
            return step("pe", lambda e: e.matmul(out_, lhsT, rhs, start=start, stop=stop,
                                                 skip_group_check=True), after, by=int(signal))

        def turn(out_, in_, after=(), signal=True, n=P):
            return step("pe", lambda e: e.transpose(out_, in_, ident[0:n, 0:n]), after, by=int(signal))

        def r32(ap):
            return ap.bitcast(F32)

        passes, rest = divmod(UNITS, STAGES)

        def load_unit(e, unit, slot):
            return e.dma_start(stage[:, slot, :], wall[bass.ds(unit, 1), :, :].rearrange("o p n -> p (o n)"))

        def feed(e):
            def one(i, k):
                ahead = 2 * (k + 1)
                base = 2 * STAGES * i + ahead
                for name in ("hi", "lo"):
                    e.wait_ge(sems[name], base)
                load_unit(e, STAGES * i + STAGES + k, k).then_inc(sems[f"landed{k}"], 16)
            e.wait_ge(sems["ld_x"], 16)
            for k in range(STAGES):
                load_unit(e, k, k).then_inc(sems[f"landed{k}"], 16)
            with e.Fori(0, passes - 1) as i:
                for k in range(STAGES):
                    one(i, k)
            for k in range(rest):
                one(passes - 1, k)

        state = {"half": 0, "split": 0}

        def split_half():
            h = state["split"]
            if h >= 2 * UNITS:
                return
            state["split"] += 1
            slot, unit_slot, side = h % SPLITS, (h // 2) % STAGES, h % 2
            src = stage[:, unit_slot, side * HALF:(side + 1) * HALF]
            landed = at(f"landed{unit_slot}", 16 * (h // 2 // STAGES + 1))
            free = at("used", h - SPLITS + 1)
            rounded = act(w_hi[:, slot, :], src, after=(landed, free), sem="hi", alone=True)
            tt(w_lo[:, slot, :], src, r32(w_hi[:, slot, :]), ALU.subtract, after=(landed, free, rounded),
               sem="lo", alone=True)

        def at(sem, value):
            return Mark(sem, value, tuple(rec.loops)) if value > 0 else None

        def take_half():
            h = state["half"]
            return h % SPLITS, (at("hi", h + 1), at("lo", h + 1))

        def used_half(fn, after=()):
            m = step("pe", fn, after, sem="used")
            state["half"] += 1
            split_half()
            return m

        def stream_loop(count, body):
            start = state["half"]
            loop = rec.loop(count, body)
            moved = state["half"] - start
            assert moved % (2 * STAGES) == 0 and state["split"] - state["half"] == SPLITS
            for k in range(STAGES):
                loop.moved[f"landed{k}"] = 16 * moved // (2 * STAGES)
            state["half"] = start + count * moved
            state["split"] = state["half"] + SPLITS

        def product(accs, acts_hi, acts_lo, kt, slot, cols, first, last, after, signal):
            todo = []
            for t in range(NT):
                tok = slice(t * P, (t + 1) * P)
                ah, al = acts_hi[:, kt, tok], acts_lo[:, kt, tok]
                for acc, (a, b) in zip(accs[t], cols):
                    wh, wl = w_hi[:, slot, a:b], w_lo[:, slot, a:b]
                    todo += [(acc, ah, wh, first, False), (acc, ah, wl, False, False),
                             (acc, al, wh, False, last)]
            for n, (acc, a, w, s0, s1) in enumerate(todo):
                fn = (lambda e, acc=acc, a=a, w=w, s0=s0, s1=s1:
                      e.matmul(acc, a, w, start=s0, stop=s1, skip_group_check=True))
                if signal and n == len(todo) - 1:
                    return used_half(fn, after if n == 0 else ())
                step("pe", fn, after if n == 0 else (), by=0)

        def project(banks, nk, after=(), ah=a_hi, al=a_lo, acts=()):
            for kt in range(nk):
                if kt % 2 == 0:
                    slot, ready = take_half()
                    ready += tuple(acts[kt // 2]) if acts else ()
                    if kt == 0:
                        ready += tuple(after)
                j = kt % 2
                m = product([[PS[:, banks[t], :]] for t in range(NT)], ah, al, kt, slot,
                            [(j * W, (j + 1) * W)], kt == 0, kt == nk - 1, ready if j == 0 else (), j == 1)
                yield m

        def finish(gen):
            m = None
            for m in gen:
                pass
            return m

        step("act", lambda e: e.dma_start(X[:, :, :], x_in.rearrange("(t p) d -> p t d", p=P)), sem="ld_x", by=16)
        step("act", lambda e: e.dma_start(csm[:, :], consts), sem="ld_const", by=16)
        step("act", lambda e: e.dma_start(lsm[:, :], small[0:1, :, :].rearrange("o p n -> p (o n)")), sem="ld_small",
             by=16)
        step("act", lambda e: e.dma_start(cact[:, :], c), sem="ld_const", by=16)
        loaded_const, loaded_x = mark("ld_const"), mark("ld_x")
        fill(ones[:, :], 1.0)
        fill(zrow[:, :], 0.0)
        fill(zcol[:, :], 0.0)
        ready_ones = fill(mhalf[:, :], -0.5)
        ts(gm8[:, :], const("lmask"), 0.0, None, ALU.is_equal, after=(loaded_const,))
        act(cact[:, :], cact[:, :], ACT.Silu, after=(loaded_const,))
        for _ in range(SPLITS):
            split_half()

        def rsqrt_mean(dst, ssum, n, width):
            m = ts(dst, ssum, 1.0 / n, EPS, ALU.mult, ALU.add)
            return step("pool", lambda e: e.tensor_tensor(dst, dst, mhalf[:, 0:width], ALU.pow), (m, ready_ones))

        def turn_split(src, nk, dst_hi, dst_lo, banks, after=(), scale=None, bias=None, ready=None):
            out_ = []
            for b in range(nk // 2):
                bank = banks[b % len(banks)]
                reuse = out_[b - len(banks)] if b >= len(banks) else ()
                for j in range(2):
                    for t in range(NT):
                        m = turn(PS[:, bank, (2 * j + t) * P:(2 * j + t + 1) * P], src(t, 2 * b + j),
                                 tuple(after) + tuple(reuse) + (tuple(ready[b]) if ready else ()),
                                 signal=(j == 1 and t == 1))
                if scale is None:
                    hi, lo = (d[:, 2 * b:2 * b + 2, :].rearrange("p k t -> p (k t)") for d in (dst_hi, dst_lo))
                    m1 = act(hi, PS[:, bank, :], after=(m,))
                    m2 = tt(lo, PS[:, bank, :], r32(hi), ALU.subtract, after=(m1, m))
                else:
                    ks = (2 * b, 2 * b + 1)
                    ps = {k: PS[:, bank, (k % 2) * T:(k % 2 + 1) * T] for k in ks}
                    for k in ks:
                        kw = {} if bias is None else dict(bias=bias[:, k:k + 1])
                        m1 = act(dst_hi[:, k, :], ps[k], ACT.Copy if bias is None else ACT.Identity, after=(m,),
                                 scale=scale[:, k:k + 1], **kw)
                    for k in ks:
                        if bias is None:
                            m2 = stt(dst_lo[:, k, :], ps[k], scale[:, k:k + 1], r32(dst_hi[:, k, :]), ALU.mult,
                                     ALU.subtract, after=(m1,))
                        else:
                            tmp = S[:, 2 * D + (k % 2) * T:2 * D + (k % 2 + 1) * T]
                            ts(tmp, ps[k], scale[:, k:k + 1], bias[:, k:k + 1], ALU.mult, ALU.add, after=(m1,))
                            m2 = tt(dst_lo[:, k, :], tmp, r32(dst_hi[:, k, :]), ALU.subtract)
                out_.append((m1, m2))
            return out_

        def norm_rows(after=(), x_done=()):
            xs = S[:, 0:NT * D].rearrange("p (t d) -> p t d", t=NT)
            for t in range(NT):
                m = step("act", lambda e, t=t: e.activation(xs[:, t, :], X[:, t, :], ACT.Square,
                                                            accum_out=st[:, t:t + 1]), tuple(after) + tuple(x_done[t:t + 1]))
            ts(st[:, 2:4], st[:, 0:2], 1.0 / D, EPS, ALU.mult, ALU.add, after=(m,))
            m = step("pool", lambda e: e.tensor_tensor(st[:, 2:4], st[:, 2:4], mhalf[:, 0:2], ALU.pow),
                     (mark("dve"), ready_ones))
            mx = (act(xs[:, 0, :], X[:, 0, :], scale=st[:, 2:3], after=(m,)),
                  ts(xs[:, 1, :], X[:, 1, :], st[:, 3:4], None, ALU.mult, after=(m,)))
            return xs, mx

        def norm_turn(scale, bias=None, after=(), x_done=()):
            xs, m = norm_rows(after, x_done)
            return turn_split(lambda t, k: xs[:, t, k * P:(k + 1) * P], KD, a_hi, a_lo, [0, 1, 2, 3],
                              after=m, scale=scale, bias=bias)

        def head_norm(v, nh, hd, tmp, gain, after=(), op=tt, at=16):
            ssum, scale = st[:, at:at + nh], st[:, at + nh:at + 2 * nh]
            m = op(tmp, v, v, ALU.mult, after=after)
            reduce(ssum, tmp, ALU.add, after=(m,))
            m = rsqrt_mean(scale, ssum, hd, nh)
            op(v, v, scale.unsqueeze(2).broadcast_to([P, nh, hd]), ALU.mult, after=(m,))
            return op(v, v, gain.unsqueeze(1).broadcast_to([P, nh, hd]), ALU.mult)

        def softmax_heads(nh, qT, kT, values, dst, scale, causal, banks, after=(), pt_at=None):
            ba, bb, bt, bo = banks
            pbuf = lambda g: S[:, 4608 + (g % 2) * W:4608 + (g % 2 + 1) * W]
            pt_at = S[:, 0:2 * W] if pt_at is None else pt_at
            pt = lambda g: pt_at[:, (g % 2) * W:(g % 2 + 1) * W]
            outs_read = copied = None
            exps, weighed = {}, {}
            group = [(4 * (g // 2) + g % 2, 4 * (g // 2) + g % 2 + 2) for g in range(nh // 2)]
            for t in range(NT):
                keys = (t + 1) * P if causal else T
                nj = keys // P
                scored = {}

                def scores(g):
                    bank = (ba, bb)[g % 2]
                    for j, h in enumerate(group[g]):
                        m = mm(PS[:, bank, j * T:j * T + keys], qT(h, t), kT(h, keys), signal=(j == 1),
                               after=tuple(after) + (exps.get(g % 2),) if j == 0 else ())
                    scored[g] = m

                turned = {}

                def weigh(g):
                    for j, h in enumerate(group[g]):
                        for n in range(nj):
                            at = (j * nj + n) * P
                            m = mm(PS[:, bo, h * HD:(h + 1) * HD], pt(g)[:, at:at + P], values(h, n), start=(n == 0),
                                   stop=(n == nj - 1), after=(turned[g], outs_read) if (j, n) == (0, 0) else (),
                                   signal=(j == 1 and n == nj - 1))
                    weighed[g % 2] = m

                scores(0)
                yield
                for g in range(nh // 2):
                    if g + 1 < nh // 2:
                        scores(g + 1)
                    ps = PS[:, (ba, bb)[g % 2], :].rearrange("p (j k) -> p j k", j=2)[:, :, 0:keys]
                    pv = pbuf(g).rearrange("p (j k) -> p j k", j=2)[:, :, 0:keys]
                    nm = st[:, 64 + 2 * g:66 + 2 * g]
                    if causal:
                        cm = const("cmask")[:, T - keys:T].unsqueeze(1).broadcast_to([P, 2, keys])
                        stt(pv, ps, scale, cm, ALU.mult, ALU.add, after=(scored[g],))
                        m = reduce(nm, pv, ALU.max, negate=True)
                        src, sc = pv, 1.0
                    else:
                        reduce(nm, ps, ALU.max, after=(scored[g],), negate=True)
                        m = ts(nm, nm, scale, None, ALU.mult)
                        src, sc = ps, scale
                    for j, h in enumerate(group[g]):
                        m = step("act", lambda e, j=j, h=h, pv=pv, src=src, sc=sc, g=g: e.activation(
                            pv[:, j, :], src[:, j, :], ACT.Exp, bias=st[:, 64 + 2 * g + j:65 + 2 * g + j], scale=sc,
                            accum_out=st[:, 80 + h:81 + h]), (m,) if j == 0 else ())
                    exps[g % 2] = done = m
                    yield
                    if g:
                        weigh(g - 1)
                    for j in range(2):
                        for n in range(nj):
                            at = (j * nj + n) * P
                            m = turn(PS[:, bt, at:at + P], pv[:, j, n * P:(n + 1) * P],
                                     (done, copied) if (j, n) == (0, 0) else (), signal=(j == 1 and n == nj - 1))
                    m = copied = act(pt(g)[:, 0:2 * keys], PS[:, bt, 0:2 * keys], after=(m, weighed.get(g % 2)))
                    turned[g] = copied
                weigh(nh // 2 - 1)
                recip(st[:, 96:96 + nh], st[:, 80:80 + nh], after=(mark("act"),))
                outs_read = tt(dst(t), PS[:, bo, :].rearrange("p (h d) -> p h d", h=nh),
                               st[:, 96:96 + nh].unsqueeze(2).broadcast_to([P, nh, HD]), ALU.mult,
                               after=tuple(weighed.values()))
                yield

        def evacuate(c, banks, m, after=()):
            m0 = act(chunk(c)[:, 0, :], PS[:, banks[0], :], after=(m,) + tuple(after))
            m1 = copy(chunk(c)[:, 1, :], PS[:, banks[1], :], after=(m,) + tuple(after))
            return (m0, m1)

        PAIRS, SPARE = [(4, 5), (0, 1)], (6, 7)

        def gates_stream(n, free, bias, out_, lanes=None, done=None):
            for c in range(n):
                banks = (lanes or PAIRS)[c % len(lanes or PAIRS)]
                for n, m in enumerate(project(banks, KD, after=free[banks])):
                    if n + 1 < KD:
                        yield
                cols = slice(c * W, (c + 1) * W)
                for t in (1, 0):
                    m1 = tt(out_[:, t, cols], PS[:, banks[t], :], out_[:, 0, cols], ALU.add, after=(m,) + tuple(bias))
                    act(out_[:, t, cols], out_[:, t, cols], ACT.Sigmoid, after=(m1,))
                free[banks] = (m1,)
                if done:
                    done[0] = c + 1
                yield

        def interleave(mains, filler, quarters=1):
            mains = list(mains)
            while mains:
                mains = [g for g in mains if next(g, "end") != "end"]
                for _ in range(quarters):
                    next(filler, None)

        def branch_turn(c, hi, lo, banks, after=None):
            return turn_split(lambda t, k: chunk(c)[:, t, k * P:(k + 1) * P], 4, hi, lo, banks,
                              after=after or (mark("act"), mark("dve")))

        def branch(b, ready, ah, al, free, first, acc, gate):
            mixed = {}
            for nh in range(D // W):
                banks = PAIRS[nh % 2]
                m = finish(project(banks, 4, after=free[banks], ah=ah, al=al, acts=ready))
                cols = slice(nh * W, (nh + 1) * W)
                for t in range(NT):
                    g = gate[:, t, b * D + nh * W:b * D + (nh + 1) * W]
                    m1 = tt(acc[:, t, cols] if first else g, PS[:, banks[t], :], g, ALU.mult, after=(m,))
                    if not first:
                        tt(acc[:, t, cols], acc[:, t, cols], g, ALU.add)
                free[banks] = (m1,)
                mixed[nh] = mark("dve")
            return mixed

        def gla(sm, progress, evac, done):
            E = [S[:, 1024 * i:1024 * (i + 1)] for i in range(4)]
            Bc, E1, E2, E3 = E
            h4 = lambda a: a.rearrange("p (h t) -> p h t", h=GH)
            m = sm
            for h in range(GH):
                m = mm(PS[:, 6 + h // 2, (h % 2) * T:(h % 2 + 1) * T], lay("aup")[0:16, h * P:(h + 1) * P],
                       fix[0:16, 0:T], after=(sm,), signal=(h % 2 == 1))
                if h % 2:
                    for j in (h - 1, h):
                        ts(h4(Bc)[:, j, :], PS[:, 6 + j // 2, (j % 2) * T:(j % 2 + 1) * T],
                           lay("ab")[:, j:j + 1], None, ALU.add, after=(m,))
            m = stt(E1, Bc, -1.0, Bc, ALU.mult, ALU.max)
            m = act(E1, E1, ACT.Exp, after=(m,), scale=-1.0)
            m = act(E1, E1, ACT.Ln, bias=1.0)
            stt(Bc, Bc, 0.0, E1, ALU.min, ALU.subtract, after=(m,))
            yield
            for h in range(GH):
                step("dve", lambda e, h=h: e.tensor_tensor_scan(h4(E1)[:, h, :], const("reset"), h4(Bc)[:, h, :], 0.0,
                                                                ALU.mult, ALU.add))
            b3 = E1.rearrange("p (c l) -> p c l", l=L)
            m = tt(E3.rearrange("p (c l) -> p c l", l=L), b3[:, :, L - 1:L].broadcast_to([P, GH * NC, L]), b3,
                   ALU.subtract)
            dec = fix[:, 256:256 + GH * NC]
            act(dec.unsqueeze(2), b3[:, :, L - 1:L], ACT.Exp, after=(m,), scale=1.0 / 16)
            act(E3, E3, ACT.Exp, scale=1.0 / 16)
            act(E2, E1, ACT.Exp, scale=-1.0 / 16)
            me = act(E1, E1, ACT.Exp, scale=1.0 / 16)
            yield
            read = {6: me, 7: me}
            for src in range(2):
                while progress[0] <= src:
                    yield
                v = chunk(src)
                for b in range(2):
                    bank = 6 + b
                    for j in range(2):
                        for t in range(NT):
                            mt = turn(PS[:, bank, (2 * j + t) * P:(2 * j + t + 1) * P],
                                      v[:, t, (2 * b + j) * P:(2 * b + j + 1) * P],
                                      evac[src] + (read[bank],), signal=(j == 1 and t == 1))
                    cols = slice(b * W, (b + 1) * W)
                    ps = PS[:, bank, :]
                    if src == 0:
                        m = stt(E1[:, cols], ps, float(GD) ** -0.5, E1[:, cols], ALU.mult, ALU.mult, after=(mt, me))
                    else:
                        tt(E2[:, cols], ps, E2[:, cols], ALU.mult, after=(mt, me))
                        m = tt(E3[:, cols], ps, E3[:, cols], ALU.mult)
                    read[bank] = m
                    yield
            ke = chunk(1)
            for t in range(NT):
                for h in range(GH):
                    mt = turn(PS[:, 6 + t, h * P:(h + 1) * P], h4(E3)[:, h, t * P:(t + 1) * P], (m,), signal=(h == GH - 1))
                m2 = act(ke[:, t, :], PS[:, 6 + t, :], after=(mt,))
            yield
            at = Bc.rearrange("p (t w) -> p t w", t=NT)
            m = fill(Bc, 0.0)
            yield
            for t in range(NT):
                for h in range(GH):
                    tok = slice(t * P, (t + 1) * P)
                    mt = mm(PS[:, 2 + t, h * P:(h + 1) * P], h4(E2)[:, h, tok], h4(E1)[:, h, tok],
                            after=(m,), signal=(h == GH - 1))
                fill(st[:, 200:201], 0.0, after=(mt,))
                step("dve", lambda e, t=t: e.copy_predicated(
                    at[:, t, :].rearrange("p (h i) -> p h i", h=GH),
                    gm8[:, :].unsqueeze(1).broadcast_to([P, GH, P]),
                    PS[:, 2 + t, :].rearrange("p (h i) -> p h i", h=GH)), alone=True)
                yield
            q0 = proj(0)
            Sx = [q0[:, 0:W], q0[:, W:2 * W], S[:, 4096:4096 + W]]
            while progress[0] <= 3:
                yield
            v = chunk(2)
            mS, states = None, {}
            for cix in range(NC - 1):
                t, o = cix // 2, (cix % 2) * L
                bank = 6 + cix % 2
                for h in range(GH):
                    mt = mm(PS[:, bank, h * P:(h + 1) * P], ke[o:o + L, t, h * P:(h + 1) * P],
                            v[o:o + L, t, h * P:(h + 1) * P], after=(m2, states.get(cix - 2)) + evac[2],
                            signal=(h == GH - 1))
                if cix == 0:
                    mS = copy(Sx[0], PS[:, bank, :], after=(mt,))
                else:
                    for h in range(GH):
                        hc = slice(h * P, (h + 1) * P)
                        mS = stt(Sx[cix][:, hc], Sx[cix - 1][:, hc], dec[:, h * NC + cix:h * NC + cix + 1],
                                 PS[:, bank, hc], ALU.mult, ALU.add, after=(mt,))
                states[cix] = mS
                yield
            tmp = S[:, 4608:4608 + W]
            y = chunk(3)
            for t in range(NT):
                bank = 2 + t
                for h in range(GH):
                    hc = slice(h * P, (h + 1) * P)
                    parts = [(slice(0, P), at[:, t, hc], v[:, t, hc])]
                    for half in range(2):
                        cix = 2 * t + half
                        if cix:
                            parts.append((slice(half * L, half * L + L), h4(E1)[:, h, cix * L:(cix + 1) * L], Sx[cix - 1][:, hc]))
                    for n, (rows, a, b) in enumerate(parts):
                        mt = mm(PS[rows, bank, hc], a, b, start=(n == 0), stop=(n == len(parts) - 1),
                                after=(mS,), signal=(h == GH - 1 and n == len(parts) - 1))
                done["gla"] = (copy(S[:, 5120:5120 + W], PS[:, bank, :], after=(mt,)), mark("act"))
                yield
                ov = S[:, 5120:5120 + W].rearrange("p (h d) -> p h d", h=GH)
                head_norm(ov, GH, GD, tmp.rearrange("p (h d) -> p h d", h=GH), lay("gn"))
                m = act(tmp, y[:, t, :], ACT.Silu, after=(mark("dve"),))
                tt(y[:, t, :], S[:, 5120:5120 + W], tmp, ALU.mult, after=(m,))
                yield

        def rope_heads(v, t):
            x = v[:, t, :].rearrange("p (h s d) -> p h s d", h=H8, s=2)
            A = MS[:, 0:W].rearrange("p (h s d) -> p h s d", h=H8, s=2)
            B = MS[:, W:2 * W].rearrange("p (h s d) -> p h s d", h=H8, s=2)
            cos, sin = (const(n)[:, t * 32:(t + 1) * 32] for n in ("cos", "sin"))
            b3 = lambda a: a.unsqueeze(1).broadcast_to([P, H8, 32])
            for s in range(2):
                gp(A[:, :, s, :], x[:, :, s, :], b3(cos), ALU.mult)
                gp(B[:, :, s, :], x[:, :, 1 - s, :], b3(sin), ALU.mult)
            gp(x[:, :, 0, :], A[:, :, 0, :], B[:, :, 0, :], ALU.subtract)
            return gp(x[:, :, 1, :], A[:, :, 1, :], B[:, :, 1, :], ALU.add)

        def moba_prepare(progress, evac, done):
            for c, gain in ((4, lay("qn")), (5, lay("kn"))):
                while progress[0] <= c:
                    yield
                written = evac[c]
                v = chunk(c)
                for t in range(NT):
                    head_norm(v[:, t, :].rearrange("p (h d) -> p h d", h=H8), H8, HD,
                              MS[:, 0:W].rearrange("p (h d) -> p h d", h=H8), gain, after=written, op=gp, at=224)
                    yield
                    done[c] = rope_heads(v, t)
                    yield

        def moba(done):
            TQ = S[:, 2560:2560 + 1024].rearrange("p (g t) -> p g t", g=4)
            TK = S[:, 3584:3584 + 1024].rearrange("p (g t) -> p g t", g=4)
            start = done["gla"]
            for c, dst, banks in ((4, TQ, (6, 7)), (5, TK, (2, 3))):
                for b in range(2):
                    for j in range(2):
                        for t in range(NT):
                            g = 2 * b + j
                            mt = turn(PS[:, banks[b], (2 * j + t) * P:(2 * j + t + 1) * P],
                                      chunk(c)[:, t, g * P:(g + 1) * P], (done[c],) + start,
                                      signal=(j == 1 and t == 1))
                    ma = act(dst[:, 2 * b:2 * b + 2, :], PS[:, banks[b], :].rearrange("p (g t) -> p g t", g=2), after=(mt,))
                yield
            rows = lambda h: slice((h % 2) * HD, (h % 2 + 1) * HD)
            yield from softmax_heads(
                H8, lambda h, t: TQ[rows(h), h // 2, t * P:(t + 1) * P], lambda h, n: TK[rows(h), h // 2, 0:n],
                lambda h, t: chunk(6)[:, t, h * HD:(h + 1) * HD],
                lambda t: chunk(4)[:, t, :].rearrange("p (h d) -> p h d", h=H8), float(HD) ** -0.5, True,
                (2, 3, 6, 7), after=(ma, mark("dve")))

        def mlstm(progress, evac, banks_free, done):
            NB = 4 * 260
            pad = MS[:, 0:NB].rearrange("p (g t) -> p g t", g=4)
            qk = proj(0).rearrange("p (g t) -> p g t", g=4)
            vx = MS[:, 1040:1040 + NT * MH * 129].rearrange("p (t h v) -> p t h v", t=NT, h=MH)
            kw = proj(1)[:, 0:NT * 256].rearrange("p (t c) -> p t c", t=NT)
            iwb = MS[:, 2072:2072 + 2 * 260].rearrange("p (g t) -> p g t", g=2)
            Sx = [proj(5)[:, 258 * i:258 * (i + 1)].rearrange("p (g v) -> p g v", g=2) for i in range(3)]
            m = fill(pad[:, :, 0:3], 0.0, after=(mark("pool"),) + done["gla"])
            v = chunk(7)
            for b in range(2):
                for j in range(2):
                    for t in range(NT):
                        g = 2 * b + j
                        mt = turn(PS[:, b, (2 * j + t) * P:(2 * j + t + 1) * P], v[:, t, g * P:(g + 1) * P],
                                  evac[7] + tuple(banks_free), signal=(j == 1 and t == 1))
                ma = act(pad[:, 2 * b:2 * b + 2, 3:259], PS[:, b, :].rearrange("p (g t) -> p g t", g=2),
                         after=(mt, m))
            yield
            conv = lay("conv").rearrange("p (g j) -> p g j", g=4)
            for g in range(4):
                ts(qk[:, g, :], pad[:, g, 0:T], conv[:, g, 0:1], None, ALU.mult, after=(ma,))
                for j in range(1, 4):
                    stt(qk[:, g, :], pad[:, g, j:j + T], conv[:, g, j:j + 1], qk[:, g, :], ALU.mult, ALU.add)
                if g >= 2:
                    ts(qk[:, g, :], qk[:, g, :], float(MK) ** -0.5, None, ALU.mult)
                yield
            iwa = proj(1)[0:MH, 512:772]
            b_, g_, u_, w2, emr, tmp = (S[0:MH, 1024 + i * T:1024 + (i + 1) * T] for i in range(6))
            lf = fix[0:MH, 288:288 + T]
            ts(g_, li_row, lay("ifb")[0:MH, 0:1], None, ALU.add, after=(mark("pe"),))
            ts(b_, lf, lay("ifb")[0:MH, 1:2], None, ALU.add)
            m = stt(tmp, b_, -1.0, b_, ALU.mult, ALU.max)
            act(tmp, tmp, ACT.Exp, after=(m,), scale=-1.0)
            m = act(tmp, tmp, ACT.Ln, bias=1.0)
            stt(tmp, b_, 0.0, tmp, ALU.min, ALU.subtract, after=(m,))
            step("dve", lambda e: e.tensor_tensor_scan(b_, const("reset")[0:MH, :], tmp, 0.0, ALU.mult, ALU.add))
            tt(g_, g_, b_, ALU.subtract)
            step("dve", lambda e: e.tensor_tensor_scan(u_, const("resetneg")[0:MH, :], g_, 0.0, ALU.add, ALU.max))
            yield
            c4 = lambda a: a.rearrange("p (c l) -> p c l", l=L)
            bl, ml = st[0:MH, 112:116], st[0:MH, 116:120]
            M, Mp = st[0:MH, 121:125], st[0:MH, 120:124]
            fill(st[0:MH, 120:121], 0.0)
            copy(bl.unsqueeze(2), c4(b_)[:, :, L - 1:L])
            tt(ml.unsqueeze(2), c4(b_)[:, :, L - 1:L], c4(u_)[:, :, L - 1:L], ALU.add)
            step("dve", lambda e: e.tensor_tensor_scan(M, bl, ml, 0.0, ALU.add, ALU.max))
            bc = lambda a: a.unsqueeze(2).broadcast_to([MH, NC, L])
            tt(c4(u_), c4(u_), bc(Mp), ALU.max)
            tt(st[0:MH, 128:132], bl, M, ALU.subtract)
            m = tt(c4(w2), c4(g_), bc(st[0:MH, 128:132]), ALU.add)
            act(w2, w2, ACT.Exp, after=(m,))
            tt(st[0:MH, 132:136], st[0:MH, 128:132], Mp, ALU.add)
            tt(c4(iwa[:, 0:T]), bc(Mp), c4(u_), ALU.subtract)
            m = copy(iwa[:, T:T + 4], st[0:MH, 132:136])
            act(iwa, iwa, ACT.Exp, after=(m,))
            m = tt(emr, b_, u_, ALU.add)
            ma = act(emr, emr, ACT.Exp, after=(m,), scale=-1.0)
            yield
            pick = lambda h, n: ident[0:MH, h:h + 1].broadcast_to([MH, n])
            for pr in range(2):
                for j in range(2):
                    mt = mm(PS[j * L:(j + 1) * L, pr, 0:260], pick(2 * pr + j, L), iwa, after=(ma, mark("dve")), signal=(j == 1))
                ma2 = act(iwb[:, pr, :], PS[:, pr, 0:260], after=(mt,))
            yield
            cols = st[:, 144:144 + 24].rearrange("p (w t h) -> p w t h", w=3, t=NT)
            for wi, a in enumerate((g_, w2, emr)):
                for t in range(NT):
                    mt = mm(PS[:, 0, (wi * NT + t) * MH:(wi * NT + t + 1) * MH], a[:, t * P:(t + 1) * P],
                            ident[0:MH, 0:MH], after=(ma2, mark("dve")), signal=(wi == 2 and t == 1))
            mc = copy(st[:, 144:168], PS[:, 0, 0:24], after=(mt,))
            for pr in range(2):
                for t in range(NT):
                    mt = turn(PS[:, 1, (t * 2 + pr) * P:(t * 2 + pr + 1) * P], qk[:, 2 + pr, t * P:(t + 1) * P],
                              (ma2, mark("dve")), signal=(pr == 1 and t == 1))
            for t in range(NT):
                mk = tt(kw[:, t, :].rearrange("p (h d) -> p h d", h=MH),
                        PS[:, 1, t * 256:(t + 1) * 256].rearrange("p (h d) -> p h d", h=MH),
                        cols[:, 1, t, :].unsqueeze(2).broadcast_to([P, MH, MK]), ALU.mult, after=(mt,))
            m_ones = fill(vx[:, :, :, MV:MV + 1], 1.0)
            while progress[0] <= 8:
                yield
            for t in range(NT):
                mv = act(vx[:, t, :, 0:MV], chunk(8)[:, t, :].rearrange("p (h v) -> p h v", h=MH), after=(m_ones,) + evac[8])
            yield
            mS = None
            for cix in range(NC - 1):
                t, o = cix // 2, (cix % 2) * L
                bank = cix % 2
                mm(PS[:, bank, 0:1], kw[o:o + L, t, 0:P], vx[o:o + L, t, 0, 0:1], after=(mv, mS, ma2), signal=False)
                for h in range(MH):
                    pr, r = h // 2, (h % 2) * L
                    mt = mm(PS[r:r + L, bank, pr * 129:(pr + 1) * 129], kw[o:o + L, t, h * MK:(h + 1) * MK],
                            vx[o:o + L, t, h, :], signal=(h == MH - 1))
                if cix == 0:
                    mS = copy(Sx[0].rearrange("p g v -> p (g v)"), PS[:, bank, 0:258], after=(mt,))
                else:
                    for pr in range(2):
                        mS = stt(Sx[cix][:, pr, :], Sx[cix - 1][:, pr, :], iwb[:, pr, T + cix:T + cix + 1],
                                 PS[:, bank, pr * 129:(pr + 1) * 129], ALU.mult, ALU.add, after=(mt,))
                yield
            q2 = MS[:, 0:512].rearrange("p (g t) -> p g t", g=2)
            mq = tt(q2, qk[:, 0:2, :], iwb[:, :, 0:T], ALU.mult)
            while progress[0] <= 9:
                yield
            y, hid_done = chunk(9), None
            hp = lambda h: slice((h % 2) * L, (h % 2 + 1) * L)
            for t in range(NT):
                tok = slice(t * P, (t + 1) * P)
                for h in range(MH):
                    mt = mm(PS[:, 0, h * P:(h + 1) * P], pick(h, P), u_[:, tok], after=(mS, mq, hid_done),
                            signal=(h == MH - 1))
                dm = proj(7)[:, 0:W].rearrange("p (h i) -> p h i", h=MH)
                tt(dm, cols[:, 0, t, :].unsqueeze(2).broadcast_to([P, MH, P]),
                   PS[:, 0, :].rearrange("p (h i) -> p h i", h=MH), ALU.subtract, after=(mt,))
                m = stt(dm, dm, 0.0, const("lmask").unsqueeze(1).broadcast_to([P, MH, P]), ALU.min, ALU.add)
                m = act(dm, dm, ACT.Exp, after=(m,))
                for h in range(MH):
                    mt = mm(PS[:, h % 2, (h // 2) * P:(h // 2 + 1) * P], qk[hp(h), 2 + h // 2, tok],
                            qk[hp(h), h // 2, tok], after=(mark("dve"),), signal=(h == MH - 1))
                yield
                pairs = dm.rearrange("p (g s) i -> p g s i", s=2)
                for s in range(2):
                    sc = PS[:, s, 0:2 * P].rearrange("p (g i) -> p g i", g=2)
                    md = tt(pairs[:, :, s, :], sc, pairs[:, :, s, :], ALU.mult, after=(mt, m))
                m = md
                yield
                for h in range(MH):
                    bank, o = h % 2, (h // 2) * T
                    parts = [(slice(0, P), dm[:, h, :], vx[:, t, h, :])]
                    for half in range(2):
                        cix = 2 * t + half
                        if cix:
                            parts.append((slice(half * L, half * L + L), q2[hp(h), h // 2, cix * L:(cix + 1) * L],
                                          Sx[cix - 1][hp(h), h // 2, :]))
                    for n, (rows, a, b) in enumerate(parts):
                        mt = mm(PS[rows, bank, o:o + 129], a, b, start=(n == 0), stop=(n == len(parts) - 1),
                                after=(m, mq), signal=(h == MH - 1 and n == len(parts) - 1))
                yield
                o2 = PS[:, 0:2, :].rearrange("p b (j v) -> p j b v", j=2)
                den = st[:, 176:180]
                copy(den.rearrange("p (j b o) -> p j b o", j=2, o=1), o2[:, :, :, MV:MV + 1], after=(mt,))
                stt(den, den, -1.0, den, ALU.mult, ALU.max)
                tt(den, den, cols[:, 2, t, :], ALU.max)
                recip(den, den)
                hid = MS[:, 512:1024].rearrange("p (h v) -> p h v", h=MH)
                for j in range(2):
                    tt(hid[:, 2 * j:2 * j + 2, :], o2[:, j, :, 0:MV],
                       den[:, 2 * j:2 * j + 2].unsqueeze(2).broadcast_to([P, 2, MV]), ALU.mult)
                hid_done = mark("dve")
                head_norm(hid, MH, MV, dm, lay("mn"))
                m = act(y[:, t, :], y[:, t, :], ACT.Sigmoid)
                tt(y[:, t, :], MS[:, 512:1024], y[:, t, :], ALU.mult, after=(m,))
                yield

        def narrow_weights(src, groups, width, read):
            hi, lo = (a[:, 0:KD * width].rearrange("p (k n) -> p k n", k=KD) for a in (s_hi, s_lo))
            if sum(n for _, n, _ in groups) < width:
                act(s_hi[:, 0:KD * width], csm[:, 0:KD * width], after=read, scale=0.0)
                act(s_lo[:, 0:KD * width], csm[:, 0:KD * width], scale=0.0)
            for a, n, row in groups:
                m1 = act(hi[:, :, row:row + n], src[:, :, a:a + n], after=read)
                m2 = tt(lo[:, :, row:row + n], src[:, :, a:a + n], r32(hi[:, :, row:row + n]), ALU.subtract,
                        after=(m1,) + read)
            return hi, lo, width, (m1, m2)

        def narrow(weights):
            hi, lo, width, ready = weights
            todo = [(a, w, k) for k in range(KD) for a, w in ((a_hi, hi), (a_hi, lo), (a_lo, hi))]
            for i, (a, w, k) in enumerate(todo):
                m = mm(PS[0:width, 6, 0:T], w[:, k, :], a[:, k, :], start=(i == 0), stop=(i == len(todo) - 1),
                       after=ready, signal=(i == len(todo) - 1))
            return m

        def block2_weights(name, n, read):
            return narrow_weights(b2(name).rearrange("p (k n) -> p k n", k=KD), ((0, n, 0),), n, read)

        def narrow_tokens(weights):
            m, n = narrow(weights), weights[2]
            m = copy(MS[0:n, 0:T], PS[0:n, 6, 0:T], after=(m,))
            for t in range(NT):
                m2 = turn(PS[:, 7, t * 64:t * 64 + n], MS[0:n, t * P:(t + 1) * P], (m,), n=n)
            return m2, PS[:, 7, 0:P].rearrange("p (t n) -> p t n", t=NT)[:, :, 0:n]

        li_row = MS[0:MH, 2072:2072 + T]

        def index(loop, name, scale=1, offset=0):
            return (loop if isinstance(loop, int) else loop.var[name]) * scale + offset

        ada_stage, acc = proj(4, 4), proj(8)[:, 0:W]

        def load_ada(lp, cl, ahead, after):
            for u in range(2):
                step("pool", lambda e, u=u: e.dma_start(
                    ada_stage[:, u * UNIT:(u + 1) * UNIT],
                    wada[bass.ds((index(lp, "pool", FF_CHUNKS) + index(cl, "pool", 1, ahead)) * 2 + u, 1), :, :]
                    .rearrange("o p n -> p (o n)")), after, sem=f"ld_ada{u}", by=16)

        def ada_step(lp, cl, more=True):
            landed = [mark(f"ld_ada{u}") for u in range(2)]
            for k in range(KD):
                src = ada_stage[:, k * W:(k + 1) * W]
                if k == 0:
                    ts(acc, src, cact[:, 0:1], None, ALU.mult, after=(landed[0],))
                else:
                    m = stt(acc, src, cact[:, k:k + 1], acc, ALU.mult, ALU.add, after=(landed[k // 4],))
                if k % 2:
                    yield
            if more:
                load_ada(lp, cl, 1, (m,))
            yield
            for j in range(4):
                mm(PS[:, 6, j:j + 1], acc[:, j * P:(j + 1) * P], ones[:, 0:1], after=(m, mark("act")), signal=False)
            summed = mm(PS[:, 7, :], ones[:, :], acc)
            act_out = lambda e: ada_cols[:, bass.ds(index(lp, "act"), 1), bass.ds(index(cl, "act", 4), 4)]
            step("act", lambda e: e.activation(act_out(e), PS[:, 6, 0:4].unsqueeze(1), ACT.Copy), (summed,))
            step("act", lambda e: e.activation(ada_rows[:, bass.ds(index(cl, "act"), 1), :], PS[:, 7, :].unsqueeze(1),
                                               ACT.Copy))
            yield

        relu = proj(0).rearrange("p (t w) -> p t w", t=NT)
        hid = proj(1).rearrange("p (t w) -> p t w", t=NT)

        def up(after=(), between=iter(()), acts=()):
            for n, m in enumerate(project((4, 5), KD, after=after, acts=acts)):
                if n % 2:
                    next(between, None)
            return m

        def down(nk, ready, last, between=iter(())):
            accs = [[PS[:, 2 * t, :], PS[:, 2 * t + 1, :]] for t in range(NT)]
            for k in range(nk):
                slot, ok = take_half()
                m = product(accs, h_hi, h_lo, k, slot, [(0, W), (W, D)], False, last and k == nk - 1,
                            tuple(ok) + tuple(ready), True)
                next(between, None)
            return m

        def clear_sums(after, pad=False):
            for b in range(4):
                if pad:
                    _, ok = take_half()
                    used_half(lambda e, b=b: e.matmul(PS[:, b, :], zcol[0:1, :], zrow[0:1, :], start=True, stop=False,
                                                      skip_group_check=True), ok + tuple(after))
                    continue
                mm(PS[:, b, :], zcol[0:1, :], zrow[0:1, :], start=True, stop=False, signal=(b == 3),
                   after=after)

        def ff_hidden(m, read=None):
            for t in range(NT):
                m1 = act(relu[:, t, :], PS[:, 4 + t, :], ACT.Relu, after=(m, read))
                m2 = tt(hid[:, t, :], relu[:, t, :], relu[:, t, :], ALU.mult, after=(m1,))
            return (m2,)

        def before_turn(width):
            return mark("act", -(width // T)), mark("dve", -(width // T))

        def hid_turn(width, after=()):
            v = PR[:, NT * W:NT * W + NT * width].rearrange("p (t w) -> p t w", t=NT)
            return turn_split(lambda t, k: v[:, t, k * P:(k + 1) * P], width // P, h_hi, h_lo, [6, 7],
                              after=after or (mark("dve"), mark("act")))

        def add_to_x(m, gate_rows=None):
            x_done = []
            for t in range(NT):
                for n in range(2):
                    cols = slice(n * W, (n + 1) * W)
                    if gate_rows is None:
                        last = tt(X[:, t, cols], PS[:, 2 * t + n, :], X[:, t, cols], ALU.add, after=(m,))
                    else:
                        tmp = MS[:, 0:W]
                        tt(tmp, PS[:, 2 * t + n, :], gate_rows[:, n, :], ALU.mult, after=(m,))
                        last = tt(X[:, t, cols], tmp, X[:, t, cols], ALU.add)
                x_done.append(last)
            return x_done

        def mixed_out(mix, mixed, free, gate_rows=None):
            mT = turn_split(lambda t, k: mix[:, t, k * P:(k + 1) * P], KD, a_hi, a_lo, [2, 3, 6, 7],
                            after=(mark("act"),), ready=[(mixed[b // 2],) for b in range(KD // 2)])
            x_done = []
            for nh in range(D // W):
                banks = PAIRS[nh % 2]
                m = finish(project(banks, KD, after=free[banks], acts=mT))
                for t in range(NT):
                    cols = slice(nh * W, (nh + 1) * W)
                    if gate_rows is None:
                        m1 = tt(X[:, t, cols], PS[:, banks[t], :], X[:, t, cols], ALU.add, after=(m,))
                    else:
                        tt(MS[:, 0:W], PS[:, banks[t], :], gate_rows[:, nh, :], ALU.mult, after=(m,))
                        m1 = tt(X[:, t, cols], MS[:, 0:W], X[:, t, cols], ALU.add)
                    x_done.append(m1)
            return x_done[-NT:]

        def until(stream, progress, chunks):
            while progress[0] < chunks:
                next(stream)

        def layer(lp):
            small_ready, h_read = mark("ld_small"), mark("pe")
            bias = step("act", lambda e: e.dma_start(
                G[:, 0, :], gate_b[bass.ds(index(lp, "act"), 1), :].broadcast_to([P, 3 * D])), sem="ld_gate", by=16)
            xT = norm_turn(lay("g1"), after=(small_ready, loaded_x, loaded_const, mark("dve")))
            free = {PAIRS[0]: (), PAIRS[1]: xT[-1]}
            progress, lanes, evac = [0], list(PAIRS), {}

            def projections():
                for cix in range(10):
                    banks = lanes[cix % len(lanes)]
                    for n, m in enumerate(project(banks, KD, after=free[banks], acts=xT)):
                        if n + 1 < KD:
                            yield
                    free[banks] = evac[cix] = evacuate(cix, banks, m)
                    progress[0] = cix + 1
                    yield
                yield from gates_stream(6, free, (bias,), G, lanes)

            stream = projections()
            gate_weights = narrow_weights(lay("wsm").rearrange("p (k n) -> p k n", k=KD),
                                          ((0, 16, 0), (16, MH, 32), (20, MH, 64)), 64 + MH, (small_ready, h_read))
            until(stream, progress, 1)
            m = narrow(gate_weights)
            copy(fix[0:MH, 288:288 + T], PS[64:64 + MH, 6, 0:T], after=(m,))
            copy(li_row, PS[32:32 + MH, 6, 0:T])
            ga = copy(fix[0:16, 0:T], PS[0:16, 6, 0:T])
            done = {}
            interleave((gla(ga, progress, evac, done), moba_prepare(progress, evac, done)), stream, GLA_PACE)
            until(stream, progress, 8)
            lanes[:] = PAIRS[0:1]

            def moba_then_banks():
                yield from moba(done)
                free[SPARE] = (mark("act"), mark("dve"))
                lanes[:] = [PAIRS[0], SPARE]

            interleave((moba_then_banks(), mlstm(progress, evac, free[PAIRS[1]], done)), stream)
            free[PAIRS[1]] = (mark("act"), mark("dve"))
            lanes[:] = PAIRS
            mix = PR[:, 0:NT * D].rearrange("p (t d) -> p t d", t=NT)
            operands = [(3, h_hi, h_lo), (4, a_hi[:, 0:4, :], a_lo[:, 0:4, :]), (9, a_hi[:, 4:8, :], a_lo[:, 4:8, :])]
            written = (mark("act"), mark("dve"))
            for _ in range(4):
                next(stream, None)
            turns = [branch_turn(*operands[0], (2, 3), written)]
            for _ in stream:
                pass
            turns.append(branch_turn(*operands[1], (2, 3), written + turns[0][-1]))
            turns.append(branch_turn(*operands[2], SPARE, written + tuple(free.get(SPARE, ()))))
            for n, (c, hi, lo) in enumerate(operands):
                mixed = branch(n, turns[n], hi, lo, free, n == 0, mix, G)
            x_done = mixed_out(mix, mixed, free)
            xT = norm_turn(lay("g2"), x_done=x_done)
            step("act", lambda e: e.dma_start(
                lsm[:, :], small[bass.ds(index(lp, "act", 1, 1), 1), :, :].rearrange("o p n -> p (o n)")),
                (mark("pe"), mark("dve"), mark("pool")), sem="ld_small", by=16)

            load_ada(lp, 0, 0, (mark("dve"), mark("pe")))
            m = up(acts=xT)
            squared = ff_hidden(m)
            clear_sums(xT[-1], pad=True)
            hid_turn(W, squared)

            def ff_step(cl):
                read, ready = before_turn(W), (mark("act"), mark("dve"))
                ada = ada_step(lp, cl)
                squared = ff_hidden(up(read, ada), read[1])
                down(W // P, ready, False, ada)
                hid_turn(W, squared + (mark("act"),))

            stream_loop(FF_CHUNKS - 1, ff_step)
            ready = (mark("act"), mark("dve"))
            ada = ada_step(lp, FF_CHUNKS - 1, more=False)
            for _ in range(2):
                next(ada)
            m = down(W // P, ready, True, ada)
            for _ in ada:
                pass
            add_to_x(m)

        stream_loop(DEPTH, layer)

        def fourier(ld, u_ready):
            ft = S[:, 2048:4096].rearrange("p (g n) -> p g n", g=4)
            u, read = chunk(5), {}
            C = dftc[:, 0:1024].rearrange("p (k n) -> p k n", k=NT)
            for g in range(4):
                for k in range(NT):
                    mt = mm(PS[:, 2 + g % 2, :], u[:, k, g * P:(g + 1) * P], C[:, k, :], start=(k == 0), stop=(k == 1),
                            after=(ld, read.get(g - 2)) + u_ready, signal=(k == 1))
                m = read[g] = act(ft[:, g, :], PS[:, 2 + g % 2, :], after=(mt,))
                yield
            fT = proj(5).rearrange("p (g t) -> p g t", g=4)
            for b in range(2):
                for j in range(2):
                    g = 2 * b + j
                    for s in range(2):
                        mt = mm(PS[:, 6 + b, j * T:(j + 1) * T], dftc[:, 1024 + s * P:1024 + (s + 1) * P],
                                ft[:, g, s * T:(s + 1) * T], start=(s == 0), stop=(s == 1), after=(m, mark("dve")),
                                signal=(s == 1))
                mf = act(fT[:, 2 * b:2 * b + 2, :], PS[:, 6 + b, :].rearrange("p (j t) -> p j t", j=2), after=(mt,))
                yield

        def angles(ld):
            pf, ang, n, r = (Gf[:, 5120 + 64 * i:5120 + 64 * (i + 1)] for i in range(4))
            twopi = 2 * np.pi
            c1 = float(np.float32(6.28125))
            c2 = float(np.float32(np.float32((twopi - c1) * 2 ** 24) // 2 ** 12 * 2 ** 12 / 2 ** 24))
            c3 = float(twopi - c1 - c2)
            magic = 1.5 * 2 ** 23
            lim = 3.1415925
            copy(pf[:, 0:NT], posi, after=(ld,))
            for t in range(NT):
                ts(ang[:, t * 16:(t + 1) * 16], const("invf"), pf[:, t:t + 1], None, ALU.mult)
            out_ = []
            for i, (quarter, shift) in enumerate(((0.25, np.pi / 2), (0.0, 0.0))):
                a, nn, rr = ang[:, 0:32], n[:, 0:32], r[:, 32 * i:32 * i + 32]
                ts(nn, a, 1 / twopi, quarter, ALU.mult, ALU.add)
                ts(nn, nn, magic, None, ALU.add)
                ts(nn, nn, -magic, None, ALU.add)
                stt(rr, nn, -c1, a, ALU.mult, ALU.add)
                stt(rr, nn, -c2, rr, ALU.mult, ALU.add)
                stt(rr, nn, -c3, rr, ALU.mult, ALU.add)
                ts(rr, rr, float(shift), lim, ALU.add, ALU.min)
                m = ts(rr, rr, -lim, None, ALU.max)
                m = act(rope2[:, i, :], rr, ACT.Sin, after=(m,))
            return m

        def rotate(x, n, cs, after=()):
            cos, sin = (a.unsqueeze(1).broadcast_to([P, n, 16]) for a in cs)
            w4 = [Gf[:, 5376 + 128 * i:5376 + 128 * i + 16 * n].rearrange("p (n d) -> p n d", n=n) for i in range(4)]
            x1, x2 = x[:, :, 0:16], x[:, :, 16:32]
            tt(w4[0], x1, cos, ALU.mult, after=after)
            tt(w4[1], x2, sin, ALU.mult)
            tt(w4[2], x2, cos, ALU.mult)
            tt(w4[3], x1, sin, ALU.mult)
            tt(x1, w4[0], w4[1], ALU.subtract)
            return tt(x2, w4[2], w4[3], ALU.add)

        posi = fix[:, 464:466].bitcast(I32)
        rope2 = fix[:, 544:608].rearrange("p (s n) -> p s n", s=2)
        cond = fix[:, 608:640]
        dftc = S[:, 4096:4096 + 1280]

        h_read = mark("pe")
        xs, scaled = norm_rows((mark("dve"),))
        tt(cond[:, 0:32], ada_cols[:, 0, :], b2("bcols"), ALU.add, after=(mark("ld_small"), mark("act")))
        for at_, gain in ((8, "gmix"), (24, "gffn")):
            ts(cond[:, at_:at_ + 8], cond[:, at_:at_ + 8], 1.0, None, ALU.add)
            tt(cond[:, at_:at_ + 8], cond[:, at_:at_ + 8], b2(gain), ALU.mult)
        uT = turn_split(lambda t, k: xs[:, t, k * P:(k + 1) * P], KD, a_hi, a_lo, [0, 1, 2, 3],
                        after=scaled + (mark("dve"),), scale=cond[:, 8:16], bias=cond[:, 0:8])
        ld_pos = step("act", lambda e: e.dma_start(posi, pos), (mark("pe"), mark("dve")), sem="ld_pos", by=16)
        gates2 = PR[:, 0:NT * 2 * D].rearrange("p (t n) -> p t n", t=NT)
        bias2 = step("act", lambda e: e.dma_start(gates2[:, 0, :], rows2[0:1, 5 * D:7 * D].broadcast_to([P, 2 * D])),
                     sem="ld_gate", by=16)
        ld_rows = step("act", lambda e: e.dma_start(PR[:, 6144:6144 + 4 * D], rows2[0:1, 0:4 * D].broadcast_to([P, 4 * D])),
                       sem="ld_rows", by=16)
        ld_dft = step("act", lambda e: e.dma_start(dftc, dft), sem="ld_dft", by=16)
        kr = fix[:, 0:64].rearrange("p (t n) -> p t n", t=NT)
        free = {PAIRS[0]: (), PAIRS[1]: uT[-1]}
        rope_weights = block2_weights("wkr", ROPE2, (h_read,))
        for cix in (4, 5):
            m = finish(project(PAIRS[cix % 2], KD, after=free[PAIRS[cix % 2]], acts=uT))
            free[PAIRS[cix % 2]] = evacuate(cix, PAIRS[cix % 2], m)
        rows_flat = ada_rows.rearrange("p c w -> p (c w)")
        tt(rows_flat, rows_flat, PR[:, 6144:6144 + 4 * D], ALU.add, after=(ld_rows, mark("act")))
        m, narrow_out = narrow_tokens(rope_weights)
        copy(kr, narrow_out, after=(m,))
        gated = [0]
        stream = gates_stream(4, free, (bias2,), gates2, done=gated)

        def latents():
            for t in range(NT):
                v = chunk(4)[:, t, :].rearrange("p (n d) -> p n d", n=2)
                tmp = S[:, 0:W].rearrange("p (n d) -> p n d", n=2)
                tt(tmp, v, v, ALU.mult, after=(mark("act"),))
                reduce(st[:, 16:18], tmp, ALU.add)
                m = rsqrt_mean(st[:, 32:34], st[:, 16:18], 256, 2)
                tt(v, v, st[:, 32:34].unsqueeze(2).broadcast_to([P, 2, 256]), ALU.mult, after=(m,))
                yield
            angles(ld_pos)
            yield
            turn_split(lambda t, k: chunk(4)[:, t, k * P:(k + 1) * P], 4, h_hi, h_lo, [6, 7],
                       after=(mark("dve"), mark("act")), scale=lsm[:, B2_AT["gq"][0]:B2_AT["gkv"][1]])
            yield

        interleave((latents(), fourier(ld_dft, (mark("act"), mark("dve")))), stream)
        until(stream, gated, 2)
        Q = PR[:, 6144:6144 + NT * 768].rearrange("p (t n) -> p t n", t=NT)
        K = PR[:, 7680:7680 + NT * 768].rearrange("p (t n) -> p t n", t=NT)
        V = chunk(9)
        latent_ready = (mark("act"), mark("dve"))
        for half in range(4):
            banks = (PAIRS[0], PAIRS[1], (2, 3), (6, 7))[half]
            width, k0 = (4 * QK2, 0) if half < 2 else (W, 2)
            slot, ok = take_half()
            for k in range(2):
                m = product([[PS[:, banks[t], 0:width]] for t in range(NT)], h_hi, h_lo, k0 + k, slot,
                            [(k * width, (k + 1) * width)], k == 0, k == 1, tuple(ok) + latent_ready, k == 1)
            for t in range(NT):
                src = PS[:, banks[t], 0:width]
                if half < 2:
                    dst = Q[:, t, half * width:(half + 1) * width]
                elif half == 2:
                    dst = K[:, t, :].rearrange("p (h d) -> p h d", h=H8)[:, :, 0:HD]
                    src = src.rearrange("p (h d) -> p h d", h=H8)
                else:
                    dst = V[:, t, :]
                if t:
                    e2 = act(dst, src, after=(m,))
                else:
                    e1 = copy(dst, src, after=(m,))
            if half < 2:
                free[banks] = (e1, e2)
        latents_used = m

        def mla():
            qkv = (mark("act"), mark("dve"))
            for t in range(NT):
                cs = (rope2[:, 0, t * 16:(t + 1) * 16], rope2[:, 1, t * 16:(t + 1) * 16])
                rotate(Q[:, t, :].rearrange("p (h d) -> p h d", h=H8)[:, :, HD:QK2], H8, cs, after=qkv)
                rotate(kr[:, t:t + 1, :], 1, cs)
                m = copy(K[:, t, :].rearrange("p (h d) -> p h d", h=H8)[:, :, HD:QK2],
                         kr[:, t:t + 1, :].broadcast_to([P, H8, 32]))
                yield
            QT = S[0:QK2, 0:2048].rearrange("p (h t) -> p h t", h=H8)
            KT = S[0:QK2, 2048:4096].rearrange("p (h t) -> p h t", h=H8)
            rotated, read = m, {}
            for i, (src, dst) in enumerate(((Q, QT), (K, KT))):
                for g in range(4):
                    bank = (2, 3, 6, 7)[g]
                    for j in range(2):
                        for t in range(NT):
                            h = 2 * g + j
                            mt = turn(PS[0:QK2, bank, (2 * j + t) * P:(2 * j + t + 1) * P],
                                      src[:, t, h * QK2:(h + 1) * QK2], (rotated, read.get(bank)) + qkv,
                                      signal=(j == 1 and t == 1))
                    to, ps = dst[:, 2 * g:2 * g + 2, :], PS[0:QK2, bank, :].rearrange("p (h t) -> p h t", h=2)
                    ma = read[bank] = act(to, ps, after=(mt,)) if g % 2 else copy(to, ps, after=(mt,))
                yield
            ma = mark("act")
            yield from softmax_heads(
                H8, lambda h, t: QT[:, h, t * P:(t + 1) * P], lambda h, n: KT[:, h, 0:n],
                lambda h, t: V[:, t, h * HD:(h + 1) * HD],
                lambda t: chunk(4)[:, t, :].rearrange("p (h d) -> p h d", h=H8), float(QK2) ** -0.5, False,
                (2, 3, 6, 7), after=(ma, mark("dve")), pt_at=Gf[:, 4096:5120])

        fT = proj(5).rearrange("p (g t) -> p g t", g=4)
        fourier_split = []
        for g in range(2):
            pair = slice(2 * g, 2 * g + 2)
            rounded = act(h_hi[:, pair, :], fT[:, pair, :], after=(latents_used,))
            fourier_split.append((rounded, tt(h_lo[:, pair, :], fT[:, pair, :], r32(h_hi[:, pair, :]),
                                              ALU.subtract, after=(rounded, latents_used))))
        interleave((mla(),), stream)
        for _ in stream:
            pass
        mix2 = PR[:, 6144:6144 + NT * D].rearrange("p (t d) -> p t d", t=NT)
        t0 = branch_turn(4, a_hi[:, 0:4, :], a_lo[:, 0:4, :], (2, 3))
        branch(1, fourier_split, h_hi, h_lo, free, True, mix2, gates2)
        mixed = branch(0, t0, a_hi, a_lo, free, False, mix2, gates2)
        x_done = mixed_out(mix2, mixed, free, ada_rows[:, 0:2, :])
        h_read = mark("pe")
        vT = norm_turn(cond[:, 24:32], cond[:, 16:24], x_done=x_done)
        router_weights = block2_weights("wr", 36, (h_read,))
        first = project((4, 5), KD, acts=vT)
        for _ in range(KD // 2):
            next(first)

        m, narrow_out = narrow_tokens(router_weights)
        first_up = finish(first)
        lg = fix[:, 0:72].rearrange("p (t n) -> p t n", t=NT)
        tt(lg, narrow_out,
           b2("br").unsqueeze(1).broadcast_to([P, NT, 36]), ALU.add, after=(m,))
        gl, el = lg[:, :, 0:4], lg[:, :, 4:36].rearrange("p t (g e) -> p t g e", g=N_GROUPS)

        def spot(a, b, n):
            return fix[:, a:a + NT * n].rearrange("p (t n) -> p t n", t=NT)

        def first_max(x, n, best, onehot):
            reduce(best, x, ALU.max)
            tt(onehot, x, best.broadcast_to([P, NT, n]), ALU.is_equal)
            tt(onehot, onehot, const("desc")[:, 0:n].unsqueeze(1).broadcast_to([P, NT, n]), ALU.mult)
            reduce(spot(200, 0, 1), onehot, ALU.max)
            return tt(onehot, onehot, spot(200, 0, 1).broadcast_to([P, NT, n]), ALU.is_equal)

        gbest, gsum, ohg, eg = spot(204, 0, 1), spot(208, 0, 1), spot(212, 0, 4), spot(220, 0, 4)
        sel, oh1, oh2, m1_, m2_ = spot(228, 0, 8), spot(244, 0, 8), spot(260, 0, 8), spot(276, 0, 1), spot(278, 0, 1)
        first_max(gl, 4, gbest, ohg)
        m = tt(eg, gl, gbest.broadcast_to([P, NT, 4]), ALU.subtract)
        m = act(eg, eg, ACT.Exp, after=(m,))
        reduce(gsum, eg, ALU.add, after=(m,))
        recip(gsum, gsum)
        picked = fix[:, 300:364].rearrange("p (t g e) -> p t g e", t=NT, g=N_GROUPS)
        for t in range(NT):
            tt(picked[:, t], el[:, t], ohg[:, t, :].unsqueeze(2).broadcast_to([P, N_GROUPS, PER_GROUP]), ALU.mult)
            reduce(sel[:, t, :], picked[:, t].rearrange("p g e -> p e g"), ALU.add)
        first_max(sel, 8, m1_, oh1)
        for t in range(NT):
            stt(sel[:, t, :], oh1[:, t, :], NEG, sel[:, t, :], ALU.mult, ALU.add)
        first_max(sel, 8, m2_, oh2)
        m = tt(m2_, m2_, m1_, ALU.subtract)
        m = act(m2_, m2_, ACT.Exp, after=(m,))
        ts(m1_, m2_, 1.0, None, ALU.add, after=(m,))
        recip(m1_, m1_)
        tt(m1_, m1_, gsum, ALU.mult)
        tt(m2_, m2_, m1_, ALU.mult)
        tt(oh1, oh1, m1_.broadcast_to([P, NT, 8]), ALU.mult)
        tt(oh2, oh2, m2_.broadcast_to([P, NT, 8]), ALU.mult)
        tt(oh1, oh1, oh2, ALU.add)
        cw = fix[:, 400:400 + NT * EXPERTS].rearrange("p (t g e) -> p t g e", t=NT, g=N_GROUPS)
        for t in range(NT):
            tt(cw[:, t], ohg[:, t, :].unsqueeze(2).broadcast_to([P, N_GROUPS, PER_GROUP]),
               oh1[:, t, :].unsqueeze(1).broadcast_to([P, N_GROUPS, PER_GROUP]), ALU.mult)
        ld_final = step("act", lambda e: e.dma_start(PR[:, 6144:6144 + D], rows2[0:1, 4 * D:5 * D].broadcast_to([P, D])),
                        (mark("dve"), mark("pe")), sem="ld_rows", by=16)

        F = 256
        sg = PR[:, 0:NT * F].rearrange("p (t f) -> p t f", t=NT)
        eh = PR[:, NT * W:NT * W + NT * F].rearrange("p (t f) -> p t f", t=NT)

        def expert_hidden(m, loop, offset):
            for t in range(NT):
                m1 = act(sg[:, t, :], PS[:, 4 + t, 0:F], ACT.Silu, after=(m, mark("dve")))
                col = lambda e, t=t: fix[:, bass.ds(index(loop, "dve", 4, 400 + t * EXPERTS + offset), 1)]
                m2 = step("dve", lambda e, t=t, col=col: e.scalar_tensor_tensor(
                    out=eh[:, t, :], in0=sg[:, t, :], scalar=col(e), in1=PS[:, 4 + t, F:2 * F],
                    op0=ALU.mult, op1=ALU.mult), (m1,))
            return (m2,)

        def expert_step(loop, offset):
            read, ready = before_turn(F), (mark("act"), mark("dve"))
            gated = expert_hidden(up(read), loop, offset)
            down(F // P, ready, False)
            hid_turn(F, gated)

        gated = expert_hidden(first_up, 0, 0)
        clear_sums(vT[-1])
        hid_turn(F, gated)
        expert_step(0, 1)

        def four_experts(loop):
            for j in range(4):
                expert_step(loop, 2 + j)

        stream_loop(7, four_experts)
        expert_step(0, EXPERTS - 2)
        expert_step(0, EXPERTS - 1)
        m = down(F // P, (mark("act"), mark("dve")), True)
        add_to_x(m, ada_rows[:, 2:4, :])

        xs, scaled = norm_rows((mark("dve"),))
        gain = PR[:, 6144:6144 + D]
        scf, shf = ada_rows[:, 6:8, :].rearrange("p c w -> p (c w)"), ada_rows[:, 4:6, :].rearrange("p c w -> p (c w)")
        ts(scf, scf, 1.0, None, ALU.add)
        tt(gain, gain, scf, ALU.mult, after=(ld_final,) + scaled)
        for t in range(NT):
            tt(xs[:, t, :], xs[:, t, :], gain, ALU.mult)
            m = tt(xs[:, t, :], xs[:, t, :], shf, ALU.add)
            step("act", lambda e, t=t: e.dma_start(out[t * P:(t + 1) * P, :], xs[:, t, :]), (m,), sem="st_out", by=16)

        block = ctx.enter_context(nc.Block())

        @block.sync
        def _(e):
            feed(e)
            e.wait_ge(sems["st_out"], rec.at["st_out"])

        @block.scalar
        def _(e):
            rec.emit("act", e, sems)

        @block.vector
        def _(e):
            rec.emit("dve", e, sems)

        @block.gpsimd
        def _(e):
            rec.emit("pool", e, sems)

        @block.tensor
        def _(e):
            rec.emit("pe", e, sems)


def _chunk(w):
    nk = w.shape[0] // P
    a = w.reshape(nk, P, w.shape[1]).transpose(1, 0, 2).reshape(P, -1, UNIT)
    return a.transpose(1, 0, 2)


def _cols(v):
    return v.reshape(-1, P).T


def _rows(v):
    return np.broadcast_to(v.reshape(1, -1), (P, v.size))


def _narrow(w):
    return w.reshape(KD, P, -1).transpose(1, 0, 2).reshape(P, -1)


def _lead(a):
    z = np.zeros((P, a.shape[1]), np.float32)
    z[:a.shape[0]] = a
    return z


def _constants():
    f = np.float32
    j, i = np.arange(P)[:, None], np.arange(P)[None, :]
    tri = np.where(i <= j, 0.0, NEG)
    lmask = np.where((j <= i) & (j // L == i // L), 0.0, NEG)
    start = (np.arange(T) % L == 0)[None, :]
    inv = (f(1.0) / np.power(f(10000.0), np.arange(0, HD, 2, dtype=f) / f(HD))).astype(f)
    ang = (np.arange(T, dtype=f)[:, None] * inv[None, :]).astype(f)
    tok = lambda a: a.reshape(NT, P, -1).transpose(1, 0, 2).reshape(P, -1)
    invf = np.power(f(10000.0), -np.arange(0, ROPE2, 2, dtype=f) / f(ROPE2)).astype(f)
    parts = dict(ident=np.eye(P), cmask=np.concatenate([np.zeros((P, P)), tri], 1), lmask=lmask,
                 reset=np.broadcast_to(np.where(start, 0.0, 1.0), (P, T)),
                 resetneg=np.broadcast_to(np.where(start, NEG, 0.0), (P, T)),
                 cos=tok(np.cos(ang)), sin=tok(np.sin(ang)),
                 desc=np.broadcast_to(8.0 - np.arange(8), (P, 8)), invf=np.broadcast_to(invf, (P, 16)))
    consts = np.concatenate([parts[n] for n in CONST_COLS], 1).astype(f)
    n = np.arange(T)
    a = 2 * np.pi * ((n[:, None] * n[None, :]) % T) / T
    d = np.arange(64)
    b = 2 * np.pi * ((d[:, None] * d[None, :]) % 64) / 64
    two = lambda m: np.kron(np.eye(2), m)
    scale = (T * 64) ** -0.5
    tokens = np.concatenate([np.cos(a), np.sin(a)], 1).reshape(NT, P, 2 * T).transpose(1, 0, 2).reshape(P, -1)
    dft = np.concatenate([tokens, two(np.cos(b)) * scale, two(-np.sin(b)) * scale], 1).astype(f)
    return consts, dft


def _layout(i):
    w_in, ff1, ff2 = i["w_in"], i["w_ff1"], i["w_ff2"]
    starts = [0, 512, 1024, 1536, 2064, 2576, 3088, 3600, 4112, 4624] + [5144 + W * k for k in range(6)]
    units = []
    for l in range(DEPTH):
        units += [_chunk(w_in[l][:, s:s + W]) for s in starts]
        for name in ("w_br_gla", "w_br_moba", "w_br_mlstm"):
            units += [_chunk(i[name][l][:, n:n + W]) for n in (0, W)]
        units += [_chunk(i["w_out"][l][:, n:n + W]) for n in (0, W)]
        units.append(_chunk(ff1[l][:, 0:W]))
        units.append(np.zeros((PAD_UNITS, P, UNIT), np.float32))
        for c in range(FF_CHUNKS):
            if c + 1 < FF_CHUNKS:
                units.append(_chunk(ff1[l][:, (c + 1) * W:(c + 2) * W]))
            units.append(_chunk(ff2[l][c * W:(c + 1) * W]))
    z = i["w_in_2"][0]
    gate_at = 256 + 256 + 32 + 512
    uq = i["w_uq_2"][0].reshape(2, P, 2, 4 * QK2).transpose(1, 2, 0, 3).reshape(P, 2, 8 * QK2)
    uq = np.concatenate([uq, np.zeros((P, 2, HALF - 8 * QK2), np.float32)], 2).reshape(1, P, UNIT)
    kv = [i[n][0].reshape(2, P, W).transpose(1, 0, 2).reshape(P, HALF) for n in ("w_uk_2", "w_uv_2")]
    units += [_chunk(z[:, 0:512]), _chunk(z[:, 544:1056])]
    units += [_chunk(z[:, gate_at + W * k:gate_at + W * (k + 1)]) for k in (0, 1)]
    units += [uq, np.concatenate(kv, 1)[None]]
    units += [_chunk(z[:, gate_at + W * k:gate_at + W * (k + 1)]) for k in (2, 3)]
    for name in ("w_branch_fourier_2", "w_branch_attn_2"):
        units += [_chunk(i[name][0][:, n:n + W]) for n in (0, W)]
    units += [_chunk(i["w_out_2"][0][:, n:n + W]) for n in (0, W)]
    gu = np.concatenate([i["w_expert_gate_2"][0], i["w_expert_up_2"][0]], 2)
    dn = i["w_expert_down_2"][0]
    units.append(_chunk(gu[0]))
    for e in range(EXPERTS):
        if e + 1 < EXPERTS:
            units.append(_chunk(gu[e + 1]))
        units.append(_chunk(dn[e]))
    wall = np.concatenate(units, 0)
    assert wall.shape == (UNITS, P, UNIT), (wall.shape, UNITS)

    layers = []
    for l in range(DEPTH):
        win = w_in[l]
        parts = dict(
            g1=_cols(i["norm1_g"][l]), g2=_cols(i["norm2_g"][l]), ab=_cols(i["gla_a_b"][l]),
            conv=i["mlstm_conv_w"][l].reshape(4, 4, P).transpose(2, 1, 0).reshape(P, 16),
            gn=_rows(i["gla_norm_g"][l]), qn=_rows(i["moba_qn_g"][l]), kn=_rows(i["moba_kn_g"][l]),
            mn=_rows(i["mlstm_norm_g"][l]),
            ifb=_lead(np.stack([i["mlstm_i_b"][l], i["mlstm_f_b"][l]], 1)), aup=_lead(i["gla_a_up"][l]),
            wsm=_narrow(np.concatenate([win[:, 2048:2064], win[:, 5136:5144]], 1)))
        layers.append(np.concatenate([parts[n] for n in LAYER_COLS], 1))
    b_ada, bf = i["b_ada_2"][0], i["b_ada_final_2"]
    six = [b_ada[k * D:(k + 1) * D] for k in range(6)]
    parts = dict(gmix=_cols(i["g_norm_mix_2"][0]), gffn=_cols(i["g_norm_ffn_2"][0]), gq=_cols(i["g_q_lat_2"][0]),
                 gkv=_cols(i["g_kv_lat_2"][0]),
                 bcols=np.concatenate([_cols(six[k]) for k in (0, 1, 3, 4)], 1),
                 wkr=_narrow(z[:, 512:544]),
                 wr=_narrow(np.concatenate([i["w_router_group_2"][0], i["w_router_expert_2"][0].reshape(D, 32)], 1)),
                 br=_rows(np.concatenate([i["b_router_group_2"][0], i["b_router_expert_2"][0].reshape(-1)])))
    block2 = np.concatenate([parts[n] for n in B2_COLS], 1)
    assert LAYER_N >= B2_N
    layers.append(np.pad(block2, ((0, 0), (0, LAYER_N - B2_N))))
    rows2 = np.concatenate([six[2], six[5], bf[:D], bf[D:], i["g_norm_final_2"], i["b_gates_2"][0]])[None]
    wa, wf = i["w_ada_2"][0], i["w_ada_final_2"]
    order = [wa[:, k * D:(k + 1) * D] for k in (0, 1, 3, 4, 2, 5)] + [wf[:, :D], wf[:, D:]]
    wada = np.concatenate([_chunk(w[:, n:n + W]) for w in order for n in (0, W)], 0)
    consts, dft = _constants()
    return dict(wall=wall, wada=wada, small=np.stack(layers), gate_b=i["gate_b"],
                rows2=rows2, consts=consts, dft=dft,
                pos=i["positions_2"].reshape(NT, P).T, c=_cols(i["c_2"].reshape(-1)), x_in=i["x"][0])


def kernel(**inputs):
    import concourse.bacc as bacc
    from concourse.bass_utils import run_bass_kernel_spmd

    arrays = _layout({k: np.asarray(v) for k, v in inputs.items()})
    arrays = {k: np.ascontiguousarray(v) for k, v in arrays.items()}
    nc = bacc.Bacc("TRN2", target_bir_lowering=False, num_devices=1)
    args = {n: nc.dram_tensor(n, a.shape, mybir.dt.from_np(a.dtype), kind="ExternalInput").ap()
            for n, a in arrays.items()}
    out = nc.dram_tensor("out", (T, D), F32, kind="ExternalOutput").ap()
    build_program(nc, out=out, **args)
    result = run_bass_kernel_spmd(nc, [arrays], core_ids=[0])
    return result.results[0]["out"].reshape(1, T, D)
```
